# Optimizing a Trainium2 kernel written in Bass

```python
import math
import jax, jax.numpy as jnp
from jax import lax
import numpy as np
import jax
import jax.numpy as jnp

D_MODEL = 1024
BATCH = 1
SEQ = 256
DEPTH = 1

D_MIX = D_MODEL
C_CONV = D_MIX // 4
C_POOL = D_MIX // 4
C_ATTN = D_MIX - C_CONV - C_POOL
DIFF_HEADS = 4
DIFF_HEAD_DIM = C_ATTN // (2 * DIFF_HEADS)
CONV_WIDTH = 31
POOL_WINDOWS = (2, 4, 8, 16)
POOL_GROUP = C_POOL // len(POOL_WINDOWS)
N_IN = 2 * C_CONV + C_POOL + 3 * C_ATTN
N_EXPERT_GROUPS = 4
EXPERTS_PER_GROUP = 4
N_EXPERTS = N_EXPERT_GROUPS * EXPERTS_PER_GROUP
D_EXPERT = D_MODEL // 4
MOE_TOP_K = 2
ATTN_BLOCK = 128
NORM_EPS = 1e-6


def rms_norm(x, g):
    xf = x.astype(jnp.float32)
    y = xf * lax.rsqrt(jnp.mean(xf * xf, axis=-1, keepdims=True) + NORM_EPS)
    return (y * g.astype(jnp.float32)).astype(x.dtype)

def layer_norm(x, g, b):
    xf = x.astype(jnp.float32)
    mu = jnp.mean(xf, axis=-1, keepdims=True)
    xc = xf - mu
    y = xc * lax.rsqrt(jnp.mean(xc * xc, axis=-1, keepdims=True) + NORM_EPS)
    return (y * g.astype(jnp.float32) + b.astype(jnp.float32)).astype(x.dtype)

def alibi_slopes(n_heads):
    start = 2.0 ** (-8.0 / n_heads)
    return jnp.asarray(np.array([start ** (i + 1) for i in range(n_heads)], dtype=np.float32))

def conv_mixer(a_val, a_gate, w_dw, b_dw, ln_g, ln_b, w_pw, b_pw):
    u = a_val * jax.nn.sigmoid(a_gate)
    y = lax.conv_general_dilated(
        u, w_dw[:, None, :].astype(u.dtype), window_strides=(1,),
        padding=[(CONV_WIDTH - 1, 0)],
        dimension_numbers=("NWC", "WIO", "NWC"),
        feature_group_count=C_CONV) + b_dw
    y = jax.nn.silu(layer_norm(y, ln_g, ln_b))
    return y @ w_pw + b_pw

def pool_mixer(u, w_pool, scale):
    s_len = u.shape[1]
    uf = u.astype(jnp.float32)
    c0 = jnp.pad(lax.cumsum(uf, axis=1), ((0, 0), (1, 0), (0, 0)))
    t = jnp.arange(s_len)
    outs = []
    for gi, win in enumerate(POOL_WINDOWS):
        sl = slice(gi * POOL_GROUP, (gi + 1) * POOL_GROUP)
        lo = jnp.maximum(t + 1 - win, 0)
        window_sum = c0[:, 1:, sl] - c0[:, lo, sl]
        count = jnp.minimum(t + 1, win).astype(jnp.float32)[None, :, None]
        d = (window_sum / count - uf[:, :, sl]).astype(u.dtype)
        outs.append(jnp.einsum("bsc,cd->bsd", d, w_pool[gi]))
    return jnp.concatenate(outs, axis=-1) * scale

def diff_attention(q, k, v, lam, slopes):
    s_len = q.shape[1]
    q = q.transpose(0, 2, 3, 1, 4)
    k = k.transpose(0, 2, 3, 1, 4)
    v = v.transpose(0, 2, 1, 3)
    scale = DIFF_HEAD_DIM ** -0.5
    outs = []
    for blk in range(s_len // ATTN_BLOCK):
        q0 = blk * ATTN_BLOCK
        end = q0 + ATTN_BLOCK
        qb = q[:, :, :, q0:end]
        kb = k[:, :, :, :end]
        vb = v[:, :, :end]
        s = jnp.einsum("bhmqd,bhmkd->bhmqk", qb, kb,
                       preferred_element_type=jnp.float32) * scale
        tq = jnp.arange(q0, end)[:, None]
        tk = jnp.arange(end)[None, :]
        dist = (tq - tk).astype(jnp.float32)
        s = s - slopes[None, :, None, None, None] * dist
        s = jnp.where(tk <= tq, s, -jnp.inf)
        p = jax.nn.softmax(s, axis=-1)
        a = p[:, :, 0] - lam * p[:, :, 1]
        outs.append(jnp.einsum("bhqk,bhkd->bhqd", a.astype(vb.dtype), vb))
    o = jnp.concatenate(outs, axis=2)
    return o.transpose(0, 2, 1, 3)

def hier_moe(h, wg, bg, we, be, w_gate, w_up, w_down):
    b_, s_, d_ = h.shape
    t = h.reshape(-1, d_)
    pg = jax.nn.softmax((t @ wg).astype(jnp.float32) + bg.astype(jnp.float32), axis=-1)
    g_idx = jnp.argmax(pg, axis=-1)
    g_p = jnp.take_along_axis(pg, g_idx[:, None], axis=1)[:, 0]
    le = ((t @ we).astype(jnp.float32) + be.astype(jnp.float32)).reshape(-1, N_EXPERT_GROUPS, EXPERTS_PER_GROUP)
    le = jnp.take_along_axis(le, g_idx[:, None, None], axis=1)[:, 0]
    pe = jax.nn.softmax(le, axis=-1)
    top_p, top_i = lax.top_k(pe, MOE_TOP_K)
    top_p = top_p / jnp.sum(top_p, axis=-1, keepdims=True)
    weights = g_p[:, None] * top_p
    eid = g_idx[:, None] * EXPERTS_PER_GROUP + top_i
    gates = jnp.sum(jax.nn.one_hot(eid, N_EXPERTS, dtype=jnp.float32) * weights[..., None], axis=1)
    gates = gates.astype(t.dtype)
    y = jnp.zeros_like(t)
    for e in range(N_EXPERTS):
        act = jax.nn.silu(t @ w_gate[e]) * (t @ w_up[e]) * gates[:, e:e + 1]
        y = y + act @ w_down[e]
    return y.reshape(b_, s_, d_)

def first_inputs(seed: int = 0) -> dict:
    key = jax.random.key(seed)
    ks = iter(jax.random.split(key, 40))
    L = DEPTH

    def nrm(shape, scale):
        return jax.random.normal(next(ks), shape, jnp.float32) * scale

    def gain(shape):
        return 1.0 + nrm(shape, 0.02)

    return {
        "x": nrm((BATCH, SEQ, D_MODEL), 1.0),
        "attn_norm_g": gain((L, D_MODEL)),
        "w_in": nrm((L, D_MODEL, N_IN), D_MODEL ** -0.5),
        "conv_w": nrm((L, CONV_WIDTH, C_CONV), CONV_WIDTH ** -0.5),
        "conv_b": nrm((L, C_CONV), 0.02),
        "conv_ln_g": gain((L, C_CONV)),
        "conv_ln_b": nrm((L, C_CONV), 0.02),
        "conv_pw_w": nrm((L, C_CONV, C_CONV), C_CONV ** -0.5),
        "conv_pw_b": nrm((L, C_CONV), 0.02),
        "pool_w": nrm((L, len(POOL_WINDOWS), POOL_GROUP, POOL_GROUP), POOL_GROUP ** -0.5),
        "pool_scale": gain((L, C_POOL)),
        "q_norm_g": gain((L, DIFF_HEAD_DIM)),
        "k_norm_g": gain((L, DIFF_HEAD_DIM)),
        "lambda_q1": nrm((L, DIFF_HEAD_DIM), 0.1),
        "lambda_k1": nrm((L, DIFF_HEAD_DIM), 0.1),
        "lambda_q2": nrm((L, DIFF_HEAD_DIM), 0.1),
        "lambda_k2": nrm((L, DIFF_HEAD_DIM), 0.1),
        "attn_sub_norm_g": gain((L, 2 * DIFF_HEAD_DIM)),
        "w_out": nrm((L, D_MIX, D_MODEL), D_MIX ** -0.5),
        "ffn_norm_g": gain((L, D_MODEL)),
        "router_g_w": nrm((L, D_MODEL, N_EXPERT_GROUPS), D_MODEL ** -0.5),
        "router_g_b": nrm((L, N_EXPERT_GROUPS), 0.01),
        "router_e_w": nrm((L, D_MODEL, N_EXPERTS), D_MODEL ** -0.5),
        "router_e_b": nrm((L, N_EXPERTS), 0.01),
        "w_gate": nrm((L, N_EXPERTS, D_MODEL, D_EXPERT), D_MODEL ** -0.5),
        "w_up": nrm((L, N_EXPERTS, D_MODEL, D_EXPERT), D_MODEL ** -0.5),
        "w_down": nrm((L, N_EXPERTS, D_EXPERT, D_MODEL), D_EXPERT ** -0.5),
    }

def first_block(x, attn_norm_g, w_in, conv_w, conv_b, conv_ln_g, conv_ln_b, conv_pw_w, conv_pw_b,
              pool_w, pool_scale, q_norm_g, k_norm_g, lambda_q1, lambda_k1, lambda_q2, lambda_k2,
              attn_sub_norm_g, w_out, ffn_norm_g, router_g_w, router_g_b, router_e_w, router_e_b,
              w_gate, w_up, w_down):
    b_, s_, _ = x.shape
    slopes = alibi_slopes(DIFF_HEADS)
    splits = [C_CONV, 2 * C_CONV, 2 * C_CONV + C_POOL,
              2 * C_CONV + C_POOL + C_ATTN, 2 * C_CONV + C_POOL + 2 * C_ATTN]
    for l in range(DEPTH):
        h = rms_norm(x, attn_norm_g[l])
        z = h @ w_in[l]
        a_val, a_gate, p_in, q, k, v = jnp.split(z, splits, axis=-1)

        y_conv = conv_mixer(a_val, a_gate, conv_w[l], conv_b[l], conv_ln_g[l], conv_ln_b[l],
                            conv_pw_w[l], conv_pw_b[l])
        y_pool = pool_mixer(p_in, pool_w[l], pool_scale[l])

        q = rms_norm(q.reshape(b_, s_, DIFF_HEADS, 2, DIFF_HEAD_DIM), q_norm_g[l])
        k = rms_norm(k.reshape(b_, s_, DIFF_HEADS, 2, DIFF_HEAD_DIM), k_norm_g[l])
        v = v.reshape(b_, s_, DIFF_HEADS, 2 * DIFF_HEAD_DIM)
        lam_init = 0.8 - 0.6 * math.exp(-0.3 * l)
        lam = (jnp.exp(jnp.sum(lambda_q1[l].astype(jnp.float32) * lambda_k1[l].astype(jnp.float32)))
               - jnp.exp(jnp.sum(lambda_q2[l].astype(jnp.float32) * lambda_k2[l].astype(jnp.float32)))
               + lam_init)
        o = diff_attention(q, k, v, lam, slopes)
        o = rms_norm(o, attn_sub_norm_g[l]) * (1.0 - lam_init)
        y_attn = o.reshape(b_, s_, C_ATTN)

        mix = jnp.concatenate([y_conv, y_pool, y_attn], axis=-1)
        x = x + mix @ w_out[l]

        hf = rms_norm(x, ffn_norm_g[l])
        x = x + hier_moe(hf, router_g_w[l], router_g_b[l], router_e_w[l], router_e_b[l],
                         w_gate[l], w_up[l], w_down[l])
    return x


CTX_LEN = 256
GRID_W = 64
CHUNK = 64
EPS = 1e-6
HG_DK = 128
HG_HEADS = D_MODEL // HG_DK
HG_DV = D_MODEL // HG_HEADS
HG_FDIM = HG_HEADS * HG_DK
HG_VDIM = HG_HEADS * HG_DV
ML_HEADS = 4
ML_DV = D_MODEL // ML_HEADS
ML_DK = ML_DV // 2
ML_QKDIM = ML_HEADS * ML_DK
ML_VDIM = ML_HEADS * ML_DV
CONV_W = 5
N_GROUPS = 4
EXPERTS_PER_GROUP_2 = 8
N_EXPERTS_2 = N_GROUPS * EXPERTS_PER_GROUP_2
TOP_K = 2
D_EXPERT_2 = 512
SEG_SIZES = (HG_FDIM, HG_FDIM, HG_FDIM, HG_VDIM, HG_VDIM,
             ML_QKDIM, ML_QKDIM, ML_VDIM, 2 * ML_HEADS, 2 * ML_HEADS, ML_VDIM,
             D_MODEL, D_MODEL)
SEG_OFFSETS = tuple(int(o) for o in np.cumsum(SEG_SIZES))
D_IN = SEG_OFFSETS[-1]
ML_F_OFFSET = SEG_OFFSETS[8]


def rms_norm_2(x, g):
    xf = x.astype(jnp.float32)
    y = xf * lax.rsqrt(jnp.mean(xf * xf, axis=-1, keepdims=True) + EPS)
    return (y * g.astype(jnp.float32)).astype(x.dtype)

def head_rms_norm(y, g, n_heads):
    b, t, ch = y.shape
    yf = y.astype(jnp.float32).reshape(b, t, n_heads, ch // n_heads)
    yf = yf * lax.rsqrt(jnp.mean(yf * yf, axis=-1, keepdims=True) + EPS)
    return (yf.reshape(b, t, ch) * g.astype(jnp.float32)).astype(y.dtype)

def modulation(cvec, w_ada, b_ada):
    m = jax.nn.silu(cvec) @ w_ada + b_ada
    return jnp.split(m, 6, axis=-1)

def to_heads(a, n_heads):
    b, t, ch = a.shape
    return a.reshape(b, t, n_heads, ch // n_heads).transpose(0, 2, 1, 3)

def from_heads(a):
    b, h, t, d = a.shape
    return a.transpose(0, 2, 1, 3).reshape(b, t, h * d)

def to_colmajor(a):
    b, t, ch = a.shape
    rows = t // GRID_W
    return a.reshape(b, rows, GRID_W, ch).transpose(0, 2, 1, 3).reshape(b, t, ch)

def from_colmajor(a):
    b, t, ch = a.shape
    rows = t // GRID_W
    return a.reshape(b, GRID_W, rows, ch).transpose(0, 2, 1, 3).reshape(b, t, ch)

def flip_t(a):
    return jnp.flip(a, axis=2)

def chunked(a):
    nc = a.shape[2] // CHUNK
    a = a.reshape(a.shape[:2] + (nc, CHUNK) + a.shape[3:])
    return jnp.moveaxis(a, 2, 0)

def unchunk(a):
    a = jnp.moveaxis(a, 0, 2)
    return a.reshape(a.shape[:2] + (a.shape[2] * a.shape[3],) + a.shape[4:])

def short_conv(a, w, b):
    ch = a.shape[-1]
    pad = CONV_W // 2
    y = lax.conv_general_dilated(a, w[:, None, :].astype(a.dtype), window_strides=(1,),
                                 padding=[(pad, pad)], dimension_numbers=('NWC', 'WIO', 'NWC'),
                                 feature_group_count=ch)
    return y + b

def gla_scan(q, k, v, logf, s0):
    mask = jnp.tril(jnp.ones((CHUNK, CHUNK), dtype=bool))

    def step(s, inp):
        qc, kc, vc, lc = inp
        b = jnp.cumsum(lc, axis=2)
        diff = b[:, :, :, None, :] - b[:, :, None, :, :]
        w = jnp.exp(jnp.where(mask[:, :, None], diff, -jnp.inf))
        a = jnp.einsum('bhtk,bhtsk,bhsk->bhts', qc, w, kc)
        o = a @ vc + jnp.einsum('bhtk,bhkv->bhtv', qc * jnp.exp(b), s)
        bl = b[:, :, -1]
        s = jnp.exp(bl)[..., None] * s + jnp.einsum('bhsk,bhsv->bhkv', kc * jnp.exp(bl[:, :, None] - b), vc)
        return s, o

    s, o = lax.scan(step, s0, (chunked(q), chunked(k), chunked(v), chunked(logf)))
    return unchunk(o), s

def mlstm_scan(q, k, v, li, lf, state):
    mask = jnp.tril(jnp.ones((CHUNK, CHUNK), dtype=bool))

    def step(carry, inp):
        c_st, n_st, m_st = carry
        qc, kc, vc, ic, fc = inp
        b = jnp.cumsum(fc, axis=-1)
        d = jnp.where(mask, b[..., :, None] - b[..., None, :] + ic[..., None, :], -jnp.inf)
        g = b + m_st[..., None]
        m_t = jnp.maximum(jnp.max(d, axis=-1), g)
        p = jnp.exp(d - m_t[..., None]) * jnp.einsum('bhtk,bhsk->bhts', qc, kc)
        inter = jnp.exp(g - m_t)
        num = p @ vc + inter[..., None] * jnp.einsum('bhtk,bhkv->bhtv', qc, c_st)
        den = jnp.sum(p, axis=-1) + inter * jnp.einsum('bhtk,bhk->bht', qc, n_st)
        h = num / jnp.maximum(jnp.abs(den), jnp.exp(-m_t))[..., None]
        bl = b[..., -1]
        lw = bl[..., None] - b + ic
        m_new = jnp.maximum(bl + m_st, jnp.max(lw, axis=-1))
        decay = jnp.exp(bl + m_st - m_new)
        wk = jnp.exp(lw - m_new[..., None])[..., None] * kc
        c_st = decay[..., None, None] * c_st + jnp.einsum('bhsk,bhsv->bhkv', wk, vc)
        n_st = decay[..., None] * n_st + jnp.sum(wk, axis=2)
        return (c_st, n_st, m_new), h

    state, h = lax.scan(step, state, (chunked(q), chunked(k), chunked(v), chunked(li), chunked(lf)))
    return unchunk(h), state

def hgrn_core(hq, hff, hfb, hi, lb, s_f, s_b):
    f32 = jnp.float32
    q = to_heads(jax.nn.silu(hq.astype(f32)), HG_HEADS)
    v = to_heads(hi.astype(f32), HG_HEADS)

    def gates(hf, lbd):
        z = hf.astype(f32)
        f = lbd + (1.0 - lbd) * jax.nn.sigmoid(z)
        k = (1.0 - lbd) * jax.nn.sigmoid(-z)
        return to_heads(k, HG_HEADS), to_heads(jnp.log(f), HG_HEADS)

    kf, lff = gates(hff, lb[0])
    kb, lfb = gates(hfb, lb[1])
    o_f, s_f = gla_scan(q, kf, v, lff, s_f)
    o_b, s_b = gla_scan(flip_t(q), flip_t(kb), flip_t(v), flip_t(lfb), s_b)
    o = from_heads(o_f + flip_t(o_b))
    return o.astype(hq.dtype), s_f, s_b

def mlstm_core(hq, hk, hv, hi, hf, conv_w, conv_b, st_f, st_b, grid):
    f32 = jnp.float32
    if grid:
        hq, hk, hv, hi, hf = [to_colmajor(a) for a in (hq, hk, hv, hi, hf)]
    qk = jax.nn.silu(short_conv(jnp.concatenate([hq, hk], axis=-1), conv_w, conv_b))
    q = to_heads(qk[..., :ML_QKDIM].astype(f32), ML_HEADS) * (ML_DK ** -0.5)
    k = to_heads(qk[..., ML_QKDIM:].astype(f32), ML_HEADS)
    v = to_heads(hv.astype(f32), ML_HEADS)
    li = hi.astype(f32).transpose(0, 2, 1)
    lf = jax.nn.log_sigmoid(hf.astype(f32)).transpose(0, 2, 1)
    h_f, st_f = mlstm_scan(q, k, v, li[:, :ML_HEADS], lf[:, :ML_HEADS], st_f)
    h_b, st_b = mlstm_scan(flip_t(q), flip_t(k), flip_t(v), flip_t(li[:, ML_HEADS:]),
                           flip_t(lf[:, ML_HEADS:]), st_b)
    h = from_heads(h_f + flip_t(h_b))
    if grid:
        h = from_colmajor(h)
    return h.astype(hq.dtype), st_f, st_b

def token_mixer(h_lat, h_ctx, w_in, b_in, lb, conv_w, conv_b, hg_norm_g, ml_norm_g,
                w_pa, w_pb, w_out, need_ctx):
    f32 = jnp.float32
    p_lat = jnp.split(h_lat @ w_in + b_in, SEG_OFFSETS[:-1], axis=-1)
    p_ctx = jnp.split(h_ctx @ w_in + b_in, SEG_OFFSETS[:-1], axis=-1)
    bsz = h_lat.shape[0]
    s0 = jnp.zeros((bsz, HG_HEADS, HG_DK, HG_DV), f32)
    m0 = (jnp.zeros((bsz, ML_HEADS, ML_DK, ML_DV), f32),
          jnp.zeros((bsz, ML_HEADS, ML_DK), f32),
          jnp.zeros((bsz, ML_HEADS), f32))
    o_ctx, hs_f, hs_b = hgrn_core(p_ctx[0], p_ctx[1], p_ctx[2], p_ctx[3], lb, s0, s0)
    o_lat, _, _ = hgrn_core(p_lat[0], p_lat[1], p_lat[2], p_lat[3], lb, hs_f, hs_b)
    r_ctx, ms_f, ms_b = mlstm_core(p_ctx[5], p_ctx[6], p_ctx[7], p_ctx[8], p_ctx[9],
                                   conv_w, conv_b, m0, m0, False)
    r_lat, _, _ = mlstm_core(p_lat[5], p_lat[6], p_lat[7], p_lat[8], p_lat[9],
                             conv_w, conv_b, ms_f, ms_b, True)

    def merge(parts, o, r):
        y_a = head_rms_norm(o, hg_norm_g, HG_HEADS) * jax.nn.silu(parts[4])
        y_b = head_rms_norm(r, ml_norm_g, ML_HEADS) * jax.nn.sigmoid(parts[10])
        y = jax.nn.sigmoid(parts[11]) * (y_a @ w_pa) + jax.nn.sigmoid(parts[12]) * (y_b @ w_pb)
        return y @ w_out

    out_lat = merge(p_lat, o_lat, r_lat)
    out_ctx = merge(p_ctx, o_ctx, r_ctx) if need_ctx else None
    return out_lat, out_ctx

def hier_moe_2(h, w_group, b_group, w_router, b_router, w_gate, w_up, w_down):
    bsz, t, d = h.shape
    tok = h.reshape(bsz * t, d)
    n_tok = tok.shape[0]
    g_logits = (tok @ w_group + b_group).astype(jnp.float32)
    g_idx = jnp.argmax(g_logits, axis=-1)
    g_w = jnp.max(jax.nn.softmax(g_logits, axis=-1), axis=-1, keepdims=True)
    e_logits = (tok @ w_router + b_router).astype(jnp.float32).reshape(n_tok, N_GROUPS, EXPERTS_PER_GROUP_2)
    e_logits = e_logits[jnp.arange(n_tok), g_idx]
    top_v, top_i = lax.top_k(e_logits, TOP_K)
    top_w = jax.nn.softmax(top_v, axis=-1) * g_w
    expert_id = g_idx[:, None] * EXPERTS_PER_GROUP_2 + top_i
    combine = jnp.sum(jax.nn.one_hot(expert_id, N_EXPERTS_2, dtype=jnp.float32) * top_w[..., None],
                      axis=1).astype(h.dtype)
    out = jnp.zeros_like(tok)
    for e in range(N_EXPERTS_2):
        a = jax.nn.silu(tok @ w_gate[e]) * (tok @ w_up[e])
        out = out + combine[:, e:e + 1] * (a @ w_down[e])
    return out.reshape(bsz, t, d)

def second_inputs(seed: int = 0) -> dict:
    key = jax.random.key(seed)
    ks = jax.random.split(key, 32)
    nrm = jax.random.normal
    f32 = jnp.float32
    b_in = 0.02 * nrm(ks[9], (DEPTH, D_IN), f32)
    forget_bias = jnp.tile(jnp.linspace(3.0, 6.0, ML_HEADS), 2)
    b_in = b_in.at[:, ML_F_OFFSET:ML_F_OFFSET + 2 * ML_HEADS].add(forget_bias)
    return {
        'x': nrm(ks[0], (BATCH, SEQ, D_MODEL), f32),
        'c': nrm(ks[1], (BATCH, D_MODEL), f32),
        'ctx': nrm(ks[2], (BATCH, CTX_LEN, D_MODEL), f32),
        'c_ctx': nrm(ks[3], (D_MODEL,), f32),
        'w_ada': 0.5 * D_MODEL ** -0.5 * nrm(ks[4], (DEPTH, D_MODEL, 6 * D_MODEL), f32),
        'b_ada': 0.02 * nrm(ks[5], (DEPTH, 6 * D_MODEL), f32),
        'norm1_g': 1.0 + 0.02 * nrm(ks[6], (DEPTH, D_MODEL), f32),
        'norm2_g': 1.0 + 0.02 * nrm(ks[7], (DEPTH, D_MODEL), f32),
        'w_in': D_MODEL ** -0.5 * nrm(ks[8], (DEPTH, D_MODEL, D_IN), f32),
        'b_in': b_in,
        'hg_lb_logits': 0.5 * nrm(ks[10], (2, DEPTH + 1, HG_FDIM), f32),
        'hg_norm_g': 1.0 + 0.02 * nrm(ks[11], (DEPTH, HG_VDIM), f32),
        'ml_conv_w': CONV_W ** -0.5 * nrm(ks[12], (DEPTH, CONV_W, 2 * ML_QKDIM), f32),
        'ml_conv_b': 0.02 * nrm(ks[13], (DEPTH, 2 * ML_QKDIM), f32),
        'ml_norm_g': 1.0 + 0.02 * nrm(ks[14], (DEPTH, ML_VDIM), f32),
        'w_branch_a': HG_VDIM ** -0.5 * nrm(ks[15], (DEPTH, HG_VDIM, D_MODEL), f32),
        'w_branch_b': ML_VDIM ** -0.5 * nrm(ks[16], (DEPTH, ML_VDIM, D_MODEL), f32),
        'w_out': D_MODEL ** -0.5 * nrm(ks[17], (DEPTH, D_MODEL, D_MODEL), f32),
        'w_group': D_MODEL ** -0.5 * nrm(ks[18], (DEPTH, D_MODEL, N_GROUPS), f32),
        'b_group': 0.01 * nrm(ks[19], (DEPTH, N_GROUPS), f32),
        'w_router': D_MODEL ** -0.5 * nrm(ks[20], (DEPTH, D_MODEL, N_EXPERTS_2), f32),
        'b_router': 0.01 * nrm(ks[21], (DEPTH, N_EXPERTS_2), f32),
        'w_gate': D_MODEL ** -0.5 * nrm(ks[22], (DEPTH, N_EXPERTS_2, D_MODEL, D_EXPERT_2), f32),
        'w_up': D_MODEL ** -0.5 * nrm(ks[23], (DEPTH, N_EXPERTS_2, D_MODEL, D_EXPERT_2), f32),
        'w_down': D_EXPERT_2 ** -0.5 * nrm(ks[24], (DEPTH, N_EXPERTS_2, D_EXPERT_2, D_MODEL), f32),
        'final_norm_g': 1.0 + 0.02 * nrm(ks[25], (D_MODEL,), f32),
    }

def second_block(x, c, ctx, c_ctx, w_ada, b_ada, norm1_g, norm2_g, w_in, b_in, hg_lb_logits,
              hg_norm_g, ml_conv_w, ml_conv_b, ml_norm_g, w_branch_a, w_branch_b, w_out,
              w_group, b_group, w_router, b_router, w_gate, w_up, w_down, final_norm_g):
    lb_all = jnp.cumsum(jax.nn.softmax(hg_lb_logits.astype(jnp.float32), axis=1), axis=1)
    for l in range(DEPTH):
        need_ctx = l < DEPTH - 1
        sh1, sc1, g1, sh2, sc2, g2 = [m[:, None, :] for m in modulation(c, w_ada[l], b_ada[l])]
        csh1, csc1, cg1, csh2, csc2, cg2 = modulation(c_ctx, w_ada[l], b_ada[l])
        h_lat = rms_norm_2(x, norm1_g[l]) * (1.0 + sc1) + sh1
        h_ctx = rms_norm_2(ctx, norm1_g[l]) * (1.0 + csc1) + csh1
        mix_lat, mix_ctx = token_mixer(h_lat, h_ctx, w_in[l], b_in[l], lb_all[:, l], ml_conv_w[l],
                                       ml_conv_b[l], hg_norm_g[l], ml_norm_g[l], w_branch_a[l],
                                       w_branch_b[l], w_out[l], need_ctx)
        x = x + g1 * mix_lat
        h2 = rms_norm_2(x, norm2_g[l]) * (1.0 + sc2) + sh2
        x = x + g2 * hier_moe_2(h2, w_group[l], b_group[l], w_router[l], b_router[l],
                              w_gate[l], w_up[l], w_down[l])
        if need_ctx:
            ctx = ctx + cg1 * mix_ctx
            hc2 = rms_norm_2(ctx, norm2_g[l]) * (1.0 + csc2) + csh2
            ctx = ctx + cg2 * hier_moe_2(hc2, w_group[l], b_group[l], w_router[l], b_router[l],
                                       w_gate[l], w_up[l], w_down[l])
    return rms_norm_2(x, final_norm_g)


def setup_inputs(seed=0):
    out = dict(first_inputs(seed))
    for name, value in second_inputs(seed + 1).items():
        if name != "x":
            out[name + "_2"] = value
    return out


def reference(
    x, attn_norm_g, w_in, conv_w, conv_b, conv_ln_g, conv_ln_b, conv_pw_w, conv_pw_b, pool_w,
    pool_scale, q_norm_g, k_norm_g, lambda_q1, lambda_k1, lambda_q2, lambda_k2, attn_sub_norm_g,
    w_out, ffn_norm_g, router_g_w, router_g_b, router_e_w, router_e_b, w_gate, w_up, w_down,
    c_2, ctx_2, c_ctx_2, w_ada_2, b_ada_2, norm1_g_2, norm2_g_2, w_in_2, b_in_2, hg_lb_logits_2,
    hg_norm_g_2, ml_conv_w_2, ml_conv_b_2, ml_norm_g_2, w_branch_a_2, w_branch_b_2, w_out_2,
    w_group_2, b_group_2, w_router_2, b_router_2, w_gate_2, w_up_2, w_down_2, final_norm_g_2,
):
    x = first_block(
        x, attn_norm_g, w_in, conv_w, conv_b, conv_ln_g, conv_ln_b, conv_pw_w, conv_pw_b,
        pool_w, pool_scale, q_norm_g, k_norm_g, lambda_q1, lambda_k1, lambda_q2, lambda_k2,
        attn_sub_norm_g, w_out, ffn_norm_g, router_g_w, router_g_b, router_e_w, router_e_b,
        w_gate, w_up, w_down,
    )
    return second_block(
        x, c_2, ctx_2, c_ctx_2, w_ada_2, b_ada_2, norm1_g_2, norm2_g_2, w_in_2, b_in_2,
        hg_lb_logits_2, hg_norm_g_2, ml_conv_w_2, ml_conv_b_2, ml_norm_g_2, w_branch_a_2,
        w_branch_b_2, w_out_2, w_group_2, b_group_2, w_router_2, b_router_2, w_gate_2, w_up_2,
        w_down_2, final_norm_g_2,
    )


_drawn_inputs = setup_inputs


def setup_inputs(seed=0):
    import zlib

    import numpy as np

    out = dict(_drawn_inputs(seed))
    spreads = {}
    factors = {'conv_b': 4.044,
     'conv_ln_g': 4.606,
     'conv_ln_b': 6.299,
     'conv_pw_b': 3.904,
     'pool_scale': 3.928,
     'q_norm_g': 4.39,
     'k_norm_g': 4.476,
     'router_g_b': 23.919,
     'router_e_b': 8.0,
     'ctx_2': 3.545,
     'b_ada_2': 3.578,
     'norm1_g_2': 8.0,
     'norm2_g_2': 5.136,
     'hg_lb_logits_2': 8.0,
     'hg_norm_g_2': 8.0,
     'ml_conv_b_2': 200.0,
     'ml_norm_g_2': 64.0,
     'b_group_2': 8.0,
     'b_router_2': 27.067,
     'final_norm_g_2': 22.105,
     'ml_conv_w_2': 3.903}
    for name, (base, spread) in spreads.items():
        noise = np.random.default_rng([zlib.crc32(name.encode()), seed]).standard_normal(out[name].shape)
        drawn = base * np.exp(spread * noise) if base else spread * noise
        out[name] = jnp.asarray(drawn.astype(out[name].dtype))
    for name, factor in factors.items():
        out[name] = (out[name] * factor).astype(out[name].dtype)
    return out
```

```python
import math
from contextlib import ExitStack

import numpy as np

import concourse.bass as bass
from concourse import mybir
from concourse.alu_op_type import AluOpType as ALU

F32 = mybir.dt.float32
I32 = mybir.dt.int32
U8 = mybir.dt.uint8
ACT = mybir.ActivationFunctionType
AX = mybir.AxisListType.X

P = 128
D = 1024
KD = D // P
T = 256
NT = T // P
EPS = 1e-6
C_CONV, CONV_W = 256, 31
WINDOWS = (2, 4, 8, 16)
PADP = max(WINDOWS)
HA, DH = 4, 64
LAM_INIT = 0.8 - 0.6 * math.exp(0.0)
GRID_W = 64
GRID_R = T // GRID_W
HG = 8
HB = 4
MLH, MLV = 4, 256
MLC = 5
LEVELS = [1 << n for n in range(7)]
FWD, BWD = 0, 1
LAT, CTX = 0, 1
NG = 4
E1, F1 = 4, 256
E2, F2 = 8, 512
BIG = 1e6
NEG = -1e30

LEAD = 256

RING = 4
SLOT = KD * 512

O_Q, O_FF, O_FB, O_HI, O_HG = 0, 1024, 2048, 3072, 4096
O_MQ, O_MK, O_MV, O_IF = 5120, 5632, 6144, 7168
O_MG, O_GA, O_GB = 7184, 8208, 9232


class Layout:

    def __init__(self):
        self.at, self.n = {}, 0

    def add(self, name, width):
        self.at[name] = (self.n, width)
        self.n += width


def cols_layout():
    lay = Layout()
    for name, width in [
        ("ident", P), ("ones", P), ("ones64", P), ("before", P), ("iota", P), ("iota8", 8),
        ("alibi", HA * T), ("inv_count", 2 * T), ("mask_f", P), ("mask_b", P),
        ("attn_norm_g", 8), ("ffn_norm_g", 8), ("norm1_g", 8), ("norm2_g", 8),
        ("conv_w", 2 * CONV_W), ("conv_b", 2), ("conv_ln_g", 2), ("conv_ln_b", 2), ("conv_pw_b", 2),
        ("pool_scale", 2), ("q_norm_g", 1), ("k_norm_g", 1), ("attn_sub_norm_g", 1),
        ("lb", 32), ("hg_norm_g", 8), ("ml_norm_g", 8), ("ml_conv_w", 8 * MLC), ("ml_conv_b", 8),
        ("b_in", 80), ("b_if", 1), ("b_ada", 48), ("c", 8), ("c_ctx", 8),
    ]:
        lay.add(name, width)
    return lay


def rows_layout():
    lay = Layout()
    for name, width in [("r1_b", NG + NG * E1), ("r2_b", NG + NG * E2), ("lambdas", 4 * DH), ("final_g", D)]:
        lay.add(name, width)
    return lay


COLS, ROWS = cols_layout(), rows_layout()


class Counter:

    def __init__(self, sem):
        self.sem, self.total, self.rel, self.loop = sem, 0, 0, None

    def bump(self, n):
        if self.loop is None:
            self.total += n
            return Mark(self, None, self.total)
        self.rel += n
        return Mark(self, self.loop, self.rel)


class Loop:

    def __init__(self, turns):
        self.turns, self.base, self.per = turns, {}, {}


class Mark:

    def __init__(self, counter, loop, k, back=0):
        self.counter, self.loop, self.k, self.back = counter, loop, k, back

    def last_turn(self):
        return Mark(self.counter, self.loop, self.k, 1)

    def value(self, loop, i):
        if self.loop is None:
            return self.k
        base, per = self.loop.base[self.counter], self.loop.per[self.counter]
        if self.loop is not loop:
            return base + (self.loop.turns - 1) * per + self.k
        least = base + self.k - self.back * per
        assert least > 0
        return i * per + least


class Later:

    def set(self, mark):
        self.mark, self.counter = mark, mark.counter
        return mark

    def value(self, loop, i):
        return self.mark.last_turn().value(loop, i)


class Later2:

    def set(self, mark):
        self.mark, self.counter = mark, mark.counter
        return mark

    def value(self, loop, i):
        return self.mark.value(loop, i)


class Queue:

    def __init__(self, prog, sem):
        self.prog, self.counter, self.items = prog, Counter(sem), []
        self.tail, self.ahead_part = [], False

    def do(self, fn, counter=None, n=1):
        c = counter or self.counter
        mark = c.bump(n)
        if self.ahead_part:
            self.prog.skipped[c] = self.prog.skipped.get(c, 0) + n
        self.put(lambda e, lp, i: (fn(e, i) if lp else fn(e)).then_inc(c.sem, n))
        return mark

    def put(self, item):
        self.items.append(item)
        if not self.ahead_part:
            self.tail.append(item)

    def step(self, fn):
        m = self.do(fn)
        self.wait(m)
        return m

    def wait(self, *marks):
        for m in marks:
            if m is None:
                continue
            if isinstance(m, (list, tuple)):
                self.wait(*m)
                continue
            self.put(lambda e, lp, i, m=m: e.wait_ge(m.counter.sem, m.value(lp, i)))

    def run(self, e, items=None):
        for item in self.items if items is None else items:
            if isinstance(item, tuple):
                loop, body, tail = item
                with e.Fori(0, loop.turns - (tail is not None)) as i:
                    for f in body:
                        f(e, loop, i)
                for f in tail or ():
                    f(e, loop, loop.turns - 1)
            elif isinstance(item, Branch):
                n = e.value_load(item.number, min_val=0, max_val=item.most)
                with e.If(n > item.above):
                    self.run(e, item.items[self])
            else:
                item(e, None, None)


class Branch:

    def __init__(self, number, most, above):
        self.number, self.most, self.above, self.items = number, most, above, {}


class Program:
    def __init__(self, nc, ctx):
        self.nc, self.ctx = nc, ctx
        self.pe, self.v, self.a, self.g, self.s = (
            Queue(self, self.sem(n)) for n in ("pe_done", "vector_done", "scalar_done", "gpsimd_done", "sync_done"))
        self.queues = [self.pe, self.v, self.a, self.g, self.s]
        self.counters = [q.counter for q in self.queues]

    def sem(self, name):
        return self.ctx.enter_context(self.nc.semaphore(name))

    def new_counter(self, name):
        c = Counter(self.sem(name))
        self.counters.append(c)
        return c

    def loop(self, turns, body):
        lp = Loop(turns)
        self.skipped = {}
        saved = [q.items for q in self.queues]
        for q in self.queues:
            q.items, q.tail = [], []
        for c in self.counters:
            lp.base[c], c.loop, c.rel = c.total, lp, 0
        body()
        for c in self.counters:
            lp.per[c] = c.rel
            c.total += turns * c.rel - self.skipped.get(c, 0)
            c.loop = None
        for q, before in zip(self.queues, saved):
            q.ahead_part = False
            if q.items:
                before.append((lp, q.items, q.tail if q is self.s else None))
            q.items, q.tail = before, []


    def branch(self, number, most, above, name, body):
        br = Branch(number, most, above)
        saved = [(q.items, q.counter) for q in self.queues]
        before = [Mark(q.counter, None, q.counter.total) for q in self.queues if q.counter.total]
        for q in self.queues:
            q.items, q.counter = [], self.new_counter(f"{name}_{q.counter.sem.name}")
            q.wait([m for m in before if m.counter is not dict(zip(self.queues, saved))[q][1]])
            q.put(lambda e, lp, i, c=q.counter: e.sem_inc(c.sem, LEAD))
            q.counter.total = LEAD
        body()
        after = [Mark(q.counter, None, q.counter.total) for q in self.queues]
        for q, (items, counter) in zip(self.queues, saved):
            q.wait([m for m in after if m.counter is not q.counter])
            br.items[q] = q.items
            q.items, q.counter = items + [br], counter


def build(nc, d, y_out):
    ctx = ExitStack()
    with ctx:
        prog = Program(nc, ctx)
        pe, v, a, g, s = prog.pe, prog.v, prog.a, prog.g, prog.s

        def sb(name, width, dt=F32):
            return ctx.enter_context(nc.sbuf_tensor(name, [P, width], dt))[:, :]

        banks = [ctx.enter_context(nc.psum_tensor(f"bank{i}", [P, 512], F32))[:, :] for i in range(8)]

        cols = sb("cols", COLS.n)
        rows = sb("rows", ROWS.n)
        level_mask = sb("level_mask", 15 * P, U8)
        pick_row = sb("pick_row", 8 * P)
        x = sb("x", NT * D)
        small = sb("small", 512)
        group_most = sb("group_most", 4)
        w_route = [sb("w_route1", KD * (NG + NG * E1)), sb("w_route2", KD * (NG + NG * E2))]
        zone = sb("zone", 53000 - RING * SLOT - COLS.n - ROWS.n - 480 - 8 * P - NT * D - 512 - KD * (2 * NG + NG * (E1 + E2)) - 64)
        ring = [sb(f"ring{i}", SLOT) for i in range(RING)]
        slot_in = [prog.new_counter(f"slot_in{i}") for i in range(RING)]
        params_in = prog.new_counter("params_in")
        mask_in = prog.new_counter("mask_in")
        x_in = prog.new_counter("x_in")
        out_done = prog.new_counter("out_done")

        def C(name, i=0, n=1):
            o, _ = COLS.at[name]
            return cols[:, o + i:o + i + n]

        def Call(name):
            o, w = COLS.at[name]
            return cols[:, o:o + w]

        def R(name):
            o, w = ROWS.at[name]
            return rows[:, o:o + w]

        ident, ones = Call("ident"), Call("ones")

        class Zone:

            def __init__(self):
                self.n = 0

            def take(self, width):
                o = self.n
                self.n += width
                assert self.n <= zone.shape[1], (self.n, zone.shape)
                return zone[:, o:o + width]

        def join():
            marks = [Mark(q.counter, None, q.counter.total) for q in (pe, v, a, g) if q.counter.total]
            for q in (pe, v, a, g, s):
                q.wait([m for m in marks if m.counter is not q.counter])

        class Stream:
            def __init__(self):
                self.n = 0
                self.released = [None] * RING
                self.slot_in = slot_in

            def load(self, *parts):
                k = self.n % RING
                self.n += 1
                s.wait(self.released[k])
                for dst, src in parts:
                    m = s.do(lambda e, dst=dst, src=src: e.dma_start(dst(ring[k]), src), self.slot_in[k], 16)
                return k, m

            def release(self, k, mark):
                self.released[k] = mark

        stream = Stream()

        def as_k(n, k=KD):
            return lambda slot: slot[:, 0:k * n].rearrange("p (k n) -> p k n", k=k)

        def column_chunk(w, c0, n=512):
            k, m = stream.load((as_k(n), w[:, c0:c0 + n].rearrange("(k p) n -> p k n", p=P)))
            return k, m, as_k(n)(ring[k])

        s.do(lambda e: e.dma_start(x.rearrange("p (t n) -> p t n", t=NT), d["x"][0].rearrange("(t p) n -> p t n", p=P)), x_in, 16)
        m_x = s.do(lambda e: e.dma_start(cols, d["cols"]), x_in, 16)
        z = Zone()
        xn = z.take(NT * D)
        hT = z.take(KD * T)
        wp1 = z.take(2 * C_CONV).rearrange("p (k n) -> p k n", k=2)
        wpool = z.take(2 * P).rearrange("p (t n) -> p t n", t=2)
        chunk0 = [column_chunk(d["w_in"][0], 0), column_chunk(d["w_in"][0], 512)]
        m_zero = [g.do(lambda e: e.memset(wpool, 0.0))]
        s.do(lambda e: e.dma_start(rows, d["rows"].broadcast_to([P, ROWS.n])), params_in, 16)
        mask_f32 = zone[:, zone.shape[1] - 15 * P:]
        m_mask = s.do(lambda e: e.dma_start(mask_f32, d["masks"]), mask_in, 16)
        s.do(lambda e: e.dma_start(pick_row[0:36, :], d["pick"]), params_in, 16)
        s.do(lambda e: e.dma_start(wp1, d["conv_pw_w"][0].rearrange("(k p) n -> p k n", p=P)), params_in, 16)
        for w_r, names, ne in ((w_route[0], ("router_g_w", "router_e_w"), E1), (w_route[1], ("w_group_2", "w_router_2"), E2)):
            wv = w_r.rearrange("p (k n) -> p k n", k=KD)
            for nm, lo, hi in ((names[0], 0, NG), (names[1], NG, NG + NG * ne)):
                s.do(lambda e, nm=nm, wv=wv, lo=lo, hi=hi: e.dma_start(wv[:, :, lo:hi], d[nm][0].rearrange("(k p) n -> p k n", p=P)), params_in, 16)
        s.wait(m_zero)
        for gi in range(4):
            o = 64 * (gi % 2)
            m_params = s.do(lambda e, gi=gi, o=o: e.dma_start(wpool[o:o + 64, gi // 2, o:o + 64], d["pool_w"][0, gi]), params_in, 16)
        chunk0 += [column_chunk(d["w_in"][0], 1024), column_chunk(d["w_in"][0], 1536, 256)]

        for q in (v, a, pe, g):
            q.wait(m_x)
        g.wait(m_mask)
        m_mask8 = g.do(lambda e: e.tensor_copy(level_mask, mask_f32))

        def rstd_of(src, dst, scale, after=()):
            v.wait(after)
            m = v.do(lambda e: e.tensor_scalar(dst, src, scale, EPS, ALU.mult, ALU.add))
            a.wait(m)
            m = a.do(lambda e: e.activation(dst, dst, ACT.Sqrt))
            v.wait(m)
            return v.step(lambda e: e.reciprocal(dst, dst))

        def norm_tokens(src, dst, stat, after=()):
            a.wait(after)
            for t in range(NT):
                m = a.do(lambda e, t=t: e.activation(dst[:, t * D:(t + 1) * D], src[:, t * D:(t + 1) * D], ACT.Square, accum_out=stat[:, t:t + 1]))
            rstd_of(stat[:, 0:NT], stat[:, 0:NT], 1.0 / D, m)
            out = []
            for t in range(NT):
                out.append(v.do(lambda e, t=t: e.tensor_scalar(dst[:, t * D:(t + 1) * D], src[:, t * D:(t + 1) * D], stat[:, t:t + 1], None, ALU.mult)))
            return out

        def to_channels(src, dst, scale, shift, after, free):
            pe.wait(after)
            out = []
            free = list(free)
            for k in range(KD):
                b = banks[6 + k % 2]
                pe.wait(free[k % 2])
                for t in range(NT):
                    fn = lambda e, k=k, t=t, b=b: e.transpose(b[:, t * P:(t + 1) * P], src[:, t * D + k * P:t * D + (k + 1) * P], ident)
                    m = pe.do(fn)
                q = v if k % 2 == 0 else a
                q.wait(m)
                if q is v:
                    sh = None if shift is None else shift(k)
                    m = v.do(lambda e, k=k, b=b, sh=sh: e.tensor_scalar(dst(k), b[:, 0:T], scale(k), sh, ALU.mult, *([] if sh is None else [ALU.add])))
                else:
                    sh = 0.0 if shift is None else shift(k)
                    m = a.do(lambda e, k=k, b=b, sh=sh: e.activation(dst(k), b[:, 0:T], ACT.Identity, bias=sh, scale=scale(k)))
                free[k % 2] = m
                out.append(m)
            return out

        bank_free = [None] * 8

        turn = [0]

        def next_bank():
            turn[0] += 1
            return turn[0] % 2

        def project(chunk, j, rhs, n, b):
            pe.wait(bank_free[b])
            w = chunk[2]

            def fn(e):
                for k in range(KD):
                    m = e.matmul(banks[b][:, 0:n], w[:, k, j * P:(j + 1) * P], rhs(k), start=(k == 0), stop=(k == KD - 1))
                return m
            return pe.do(fn)

        def project_tokens(chunk, lhsT, n, b, bias=None, c0=0):
            pe.wait(bank_free[b])
            w = chunk[2]

            def fn(e):
                for k in range(KD):
                    m = e.matmul(banks[b][:, 0:n], lhsT(k), w[:, k, c0:c0 + n], start=(k == 0), stop=(k == KD - 1 and bias is None))
                if bias is not None:
                    m = e.matmul(banks[b][:, 0:n], ones[0:1, :], bias, start=False, stop=True)
                return m
            return pe.do(fn)

        def first_block():
            stat = small[:, 0:8]
            m_xn = norm_tokens(x, xn, stat)
            hTk = hT.rearrange("p (k t) -> p k t", k=KD)
            m_h = to_channels(xn, lambda k: hTk[:, k, :], lambda k: C("attn_norm_g", k), None, m_xn, [None, None])
            bank_free[6], bank_free[7] = m_h[-2], m_h[-1]
            h_rhs = lambda k: hTk[:, k, :]

            gate = z.take(2 * T).rearrange("p (j t) -> p j t", j=2)
            U = T + CONV_W - 1
            u = z.take(2 * U).rearrange("p (j t) -> p j t", j=2)
            pin = z.take(2 * (T + PADP)).rearrange("p (j t) -> p j t", j=2)
            qk = z.take(8 * T).rearrange("p (j t) -> p j t", j=8)
            vv = z.take(NT * 512).rearrange("p (t n) -> p t n", t=NT)
            m_pad = g.do(lambda e: e.memset(u[:, :, 0:CONV_W - 1], 0.0))
            m_pad = g.do(lambda e: e.memset(pin[:, :, 0:PADP], 0.0))
            pe.wait(m_h)

            c = chunk0[0]
            pe.wait(c[1])
            m_gate = []
            for j in (2, 3):
                b = next_bank()
                m = project(c, j, h_rhs, T, b)
                a.wait(m)
                bank_free[b] = a.do(lambda e, j=j, b=b: e.activation(gate[:, j - 2, :], banks[b][:, 0:T], ACT.Sigmoid))
                m_gate.append(bank_free[b])
            for j in (0, 1):
                b = next_bank()
                m = project(c, j, h_rhs, T, b)
                v.wait(m, m_gate[j])
                bank_free[b] = v.do(lambda e, j=j, b=b: e.tensor_tensor(u[:, j, CONV_W - 1:U], banks[b][:, 0:T], gate[:, j, :], ALU.mult))
            m_u = bank_free[b]
            stream.release(c[0], m)
            c = chunk0[1]
            pe.wait(c[1])
            m_qk = []
            for j in range(4):
                b = next_bank()
                m = project(c, j, h_rhs, T, b)
                dst = pin[:, j, PADP:] if j < 2 else qk[:, j - 2, :]
                a.wait(m)
                bank_free[b] = a.do(lambda e, dst=dst, b=b: e.activation(dst, banks[b][:, 0:T], ACT.Copy))
                if j == 1:
                    m_pin = bank_free[b]
            stream.release(c[0], m)
            jq = 2
            c_v = column_chunk(d["w_in"][0], 1792)
            for c, nj in ((chunk0[2], 4), (chunk0[3], 2)):
                pe.wait(c[1])
                for j in range(nj):
                    b = next_bank()
                    m = project(c, j, h_rhs, T, b)
                    a.wait(m)
                    bank_free[b] = a.do(lambda e, jq=jq, b=b: e.activation(qk[:, jq, :], banks[b][:, 0:T], ACT.Copy))
                    jq += 1
                stream.release(c[0], m)
            m_qk = bank_free[b]
            pe.wait(c_v[1])
            for t in range(NT):
                b = next_bank()
                m = project_tokens(c_v, lambda k, t=t: hTk[:, k, t * P:(t + 1) * P], 512, b)
                a.wait(m)
                bank_free[b] = a.do(lambda e, t=t, b=b: e.activation(vv[:, t, :], banks[b], ACT.Copy))
            m_vv = bank_free[b]
            stream.release(c_v[0], m)

            ada = z.take(6 * D)
            cc = small[:, 8:24].rearrange("p (k c) -> p k c", k=KD)
            m = a.do(lambda e: e.activation(cc[:, :, 0], Call("c"), ACT.Silu))
            m = a.do(lambda e: e.activation(cc[:, :, 1], Call("c_ctx"), ACT.Silu))
            pe.wait(m)
            n_ada = 6 * D // 512
            w_ada = d["w_ada_2"][0].rearrange("(k p) n -> p k n", p=P)
            pe.wait(bank_free[0], bank_free[1])
            first = [stream.load((as_k(512), w_ada[:, :, k * 512:(k + 1) * 512])) for k in range(RING)]
            m_ev = {}
            base = stream.n % RING
            at_slot = [(base + k) % RING for k in range(RING)]

            def ada_turn():
                loaded, m_pe = [Later() for _ in range(RING)], []
                read = [Later(), Later()]
                for k in range(RING):
                    pe.wait(loaded[k], m_ev[k - 2] if k >= 2 else read[k])

                    def mm(e, i, k=k):
                        for kk in range(KD):
                            r = e.matmul(banks[k % 2][0:2, :], cc[:, kk, :], as_k(512)(ring[at_slot[k]])[:, kk, :], start=(kk == 0), stop=(kk == KD - 1))
                        return r
                    m_pe.append(pe.do(mm))
                    a.wait(m_pe[k])
                    m_ev[k] = a.do(lambda e, i, k=k: e.activation(ada[0:2, bass.ds(i * (RING * 512) + k * 512, 512)], banks[k % 2][0:2, :], ACT.Copy))
                read[0].set(m_ev[RING - 2]), read[1].set(m_ev[RING - 1])
                s.ahead_part = True
                for k in range(RING):
                    s.wait(m_pe[k])
                    loaded[k].set(s.do(lambda e, i, k=k: e.dma_start(as_k(512)(ring[at_slot[k]]), w_ada[:, :, bass.ds(i * (RING * 512) + (RING + k) * 512, 512)]), slot_in[at_slot[k]], 16))
                    stream.released[at_slot[k]] = m_pe[k]
            prog.loop(n_ada // RING, ada_turn)
            bank_free[0], bank_free[1] = m_ev[RING - 2], m_ev[RING - 1]
            m_ada = m_ev[RING - 1]

            yc = z.take(2 * T).rearrange("p (j t) -> p j t", j=2)
            v.wait(m_pad, m_u)
            m_y = [v.do(lambda e, j=j: e.tensor_scalar(yc[:, j, :], u[:, j, 0:T], C("conv_w", j * CONV_W), C("conv_b", j), ALU.mult, ALU.add)) for j in range(2)]
            for w in range(1, CONV_W):
                for j in range(2):
                    v.wait(m_y[j])
                    m_y[j] = v.do(lambda e, j=j, w=w: e.scalar_tensor_tensor(yc[:, j, :], u[:, j, w:w + T], C("conv_w", j * CONV_W + w), yc[:, j, :], ALU.mult, ALU.add))

            sums = [z.take(2 * (T + PADP)).rearrange("p (j t) -> p j t", j=2) for _ in range(2)]
            dd = z.take(2 * T).rearrange("p (j t) -> p j t", j=2)
            inv = Call("inv_count").rearrange("p (j t) -> p j t", j=2)
            v.wait(m_pin)
            end = T + PADP
            src = pin
            for n, win in enumerate(WINDOWS):
                dst = sums[n % 2]
                h_ = win // 2
                v.step(lambda e, src=src, dst=dst, win=win, h_=h_: e.tensor_tensor(dst[:, :, win:end], src[:, :, win:end], src[:, :, win - h_:end - h_], ALU.add))
                o, j = 64 * (n % 2), n // 2
                v.do(lambda e, dst=dst, o=o, j=j: e.tensor_tensor(dd[o:o + 64, j, :], dst[o:o + 64, j, PADP:end], inv[o:o + 64, j, :], ALU.mult))
                src = dst
            v.wait(Mark(v.counter, None, v.counter.total))
            m_dd = v.do(lambda e: e.tensor_tensor(dd, dd, pin[:, :, PADP:end], ALU.subtract))

            sq = z.take(8 * T).rearrange("p (j t) -> p j t", j=8)
            sqf = sq.rearrange("p j t -> p (j t)")
            qkf = qk.rearrange("p j t -> p (j t)")
            qg = small[:, 24:25]
            v.do(lambda e: e.tensor_scalar(qg, C("q_norm_g"), DH ** -0.5, None, ALU.mult))
            a.wait(m_qk)
            m_sq = a.do(lambda e: e.activation(sq, qk, ACT.Square))
            pe.wait(m_sq)
            m_ms = []
            for n in range(4):
                pe.wait(bank_free[2 + n])
                m_ms.append(pe.do(lambda e, n=n: e.matmul(banks[2 + n], Call("ones64"), sqf[:, n * 512:(n + 1) * 512], start=True, stop=True)))
            for n in range(4):
                v.wait(m_ms[n])
                m = v.do(lambda e, n=n: e.tensor_scalar(sqf[:, n * 512:(n + 1) * 512], banks[2 + n], 1.0 / DH, EPS, ALU.mult, ALU.add))
                bank_free[2 + n] = m
            a.wait(m)
            m = a.do(lambda e: e.activation(sq, sq, ACT.Sqrt))
            v.wait(m)
            v.step(lambda e: e.reciprocal(sqf, sqf))
            v.do(lambda e: e.scalar_tensor_tensor(qkf[:, 0:4 * T], qkf[:, 0:4 * T], qg, sqf[:, 0:4 * T], ALU.mult, ALU.mult))
            m_qkn = v.do(lambda e: e.scalar_tensor_tensor(qkf[:, 4 * T:], qkf[:, 4 * T:], C("k_norm_g"), sqf[:, 4 * T:], ALU.mult, ALU.mult))

            v.wait(m_params)
            lmb = R("lambdas").rearrange("p (n d) -> p n d", n=4)
            lm = small[:, 32:160].rearrange("p (n d) -> p n d", n=2)
            ls, nlam, sg = small[:, 26:28], small[:, 28:29], small[:, 29:30]
            v.step(lambda e: e.tensor_tensor(lm, lmb[:, 0:4:2, :], lmb[:, 1:4:2, :], ALU.mult))
            m = v.step(lambda e: e.tensor_reduce(ls, lm, AX, ALU.add))
            a.wait(m)
            m = a.do(lambda e: e.activation(ls, ls, ACT.Exp))
            v.wait(m)
            v.step(lambda e: e.tensor_tensor(nlam, ls[:, 1:2], ls[:, 0:1], ALU.subtract))
            v.step(lambda e: e.tensor_scalar(nlam, nlam, -LAM_INIT, None, ALU.add))
            v.do(lambda e: e.tensor_scalar(sg, C("attn_sub_norm_g"), 1.0 - LAM_INIT, None, ALU.mult))

            mixT = z.take(KD * T).rearrange("p (k t) -> p k t", k=KD)
            sc = [z.take(2 * T).rearrange("p (m k) -> p m k", m=2) for _ in range(2)]
            aT = [z.take(T) for _ in range(2)]
            st = small[:, 160:256].rearrange("p (u n) -> p u n", u=8)
            ali = Call("alibi").rearrange("p (h k) -> p h k", h=HA)
            pe.wait(m_qkn, m_vv)
            sc_free, aT_free = [None, None], [None, None]
            o_marks = {}
            units = [(h, blk) for h in range(HA) for blk in range(NT)]
            for n, (h, blk) in enumerate(units):
                nk = (blk + 1) * P
                b = 2 * (n % 2)
                pe.wait(bank_free[b], bank_free[b + 1])

                def mm(e, h=h, blk=blk, nk=nk, b=b):
                    for mp in range(2):
                        o = 64 * mp
                        r = e.matmul(banks[b + mp][:, 0:nk], qk[o:o + 64, h, blk * P:(blk + 1) * P], qk[o:o + 64, 4 + h, 0:nk], start=True, stop=True)
                    return r
                m = pe.do(mm)
                s2 = sc[n % 2]
                sv = s2[:, :, 0:nk]
                v.wait(m, aT_free[n % 2])
                for mp in range(2):
                    m = v.do(lambda e, s2=s2, b=b, mp=mp, h=h, nk=nk: e.tensor_tensor(s2[:, mp, 0:nk], banks[b + mp][:, 0:nk], ali[:, h, T - nk:T], ALU.add))
                    bank_free[b + mp] = m
                v.wait(m)
                m = v.do(lambda e, sv=sv, n=n: e.tensor_reduce(st[:, n, 0:2], sv, AX, ALU.max, negate=True))
                a.wait(m)
                for mp in range(2):
                    m = a.do(lambda e, s2=s2, mp=mp, nk=nk, n=n: e.activation(s2[:, mp, 0:nk], s2[:, mp, 0:nk], ACT.Exp, bias=st[:, n, mp:mp + 1], accum_out=st[:, n, 2 + mp:3 + mp]))
                v.wait(m)
                v.step(lambda e, n=n: e.reciprocal(st[:, n, 4:6], st[:, n, 2:4]))
                v.step(lambda e, n=n: e.tensor_tensor(st[:, n, 5:6], st[:, n, 5:6], nlam, ALU.mult))
                v.step(lambda e, n=n, s2=s2, nk=nk: e.tensor_scalar(s2[:, 0, 0:nk], s2[:, 0, 0:nk], st[:, n, 4:5], None, ALU.mult))
                m = v.do(lambda e, n=n, s2=s2, nk=nk: e.scalar_tensor_tensor(s2[:, 0, 0:nk], s2[:, 1, 0:nk], st[:, n, 5:6], s2[:, 0, 0:nk], ALU.mult, ALU.add))
                pe.wait(m)
                bt = 4 + n % 2
                pe.wait(bank_free[bt])
                for kt in range(blk + 1):
                    m = pe.do(lambda e, s2=s2, kt=kt, bt=bt: e.transpose(banks[bt][:, kt * P:(kt + 1) * P], s2[:, 0, kt * P:(kt + 1) * P], ident))
                aT_free[n % 2] = m
                a.wait(m)
                at = aT[n % 2]
                m = a.do(lambda e, at=at, bt=bt, nk=nk: e.activation(at[:, 0:nk], banks[bt][:, 0:nk], ACT.Copy))
                bank_free[bt] = m
                ob = 6 + h // 2
                pe.wait(m, bank_free[ob])

                def mm(e, h=h, blk=blk, ob=ob, at=at):
                    o = (h % 2) * T + blk * P
                    for kt in range(blk + 1):
                        r = e.matmul(banks[ob][:, o:o + P], vv[:, kt, h * P:(h + 1) * P], at[:, kt * P:(kt + 1) * P], start=(kt == 0), stop=(kt == blk))
                    return r
                m_o = pe.do(mm)
                o_marks[n] = m_o
                if n >= 1:
                    a.wait(o_marks[n - 1])
            osq = sqf[:, 0:2 * T]
            for hp in range(2):
                ob = 6 + hp
                dst = sqf[:, hp * 512:(hp + 1) * 512]
                a.wait(m_o)
                m = a.do(lambda e, ob=ob, dst=dst: e.activation(dst, banks[ob], ACT.Square))
                pe.wait(m, bank_free[2 + hp])
                m = pe.do(lambda e, dst=dst, hp=hp: e.matmul(banks[2 + hp], ones, dst, start=True, stop=True))
                m = rstd_of(banks[2 + hp], dst, 1.0 / P, m)
                bank_free[2 + hp] = m
                md = mixT[:, 4 + 2 * hp:6 + 2 * hp, :].rearrange("p k t -> p (k t)")
                m_att = v.do(lambda e, ob=ob, dst=dst, md=md: e.scalar_tensor_tensor(md, banks[ob], sg, dst, ALU.mult, ALU.mult))
                bank_free[ob] = m_att

            pe.wait(m_dd, m_params)
            for j in range(2):
                pe.wait(bank_free[4 + j])
                m = pe.do(lambda e, j=j: e.matmul(banks[4 + j][:, 0:T], wpool[:, j, :], dd[:, j, :], start=True, stop=True))
                a.wait(m)
                bank_free[4 + j] = a.do(lambda e, j=j: e.activation(mixT[:, 2 + j, :], banks[4 + j][:, 0:T], ACT.Copy, scale=C("pool_scale", j)))
            m_pool = bank_free[5]

            ycf = yc.rearrange("p j t -> p (j t)")
            pe.wait(m_y, bank_free[2])
            lnb = sqf[:, 1024:1024 + 2 * T]
            r_ = sqf[:, 1536:1536 + T]

            def sum_channels(src, b):
                def mm(e):
                    for j in range(2):
                        r = e.matmul(banks[b][:, 0:T], ones, src[:, j, :], start=(j == 0), stop=(j == 1))
                    return r
                return pe.do(mm)
            m = sum_channels(yc, 2)
            v.wait(m)
            for j in range(2):
                m = v.do(lambda e, j=j: e.scalar_tensor_tensor(yc[:, j, :], banks[2][:, 0:T], -1.0 / C_CONV, yc[:, j, :], ALU.mult, ALU.add))
            bank_free[2] = m
            a.wait(m)
            m = a.do(lambda e: e.activation(lnb, ycf, ACT.Square))
            pe.wait(m, bank_free[3])
            m = sum_channels(lnb.rearrange("p (j t) -> p j t", j=2), 3)
            m = rstd_of(banks[3][:, 0:T], r_, 1.0 / C_CONV, m)
            bank_free[3] = m
            for j in range(2):
                m = v.do(lambda e, j=j: e.tensor_tensor(yc[:, j, :], yc[:, j, :], r_, ALU.mult))
            a.wait(m)
            for j in range(2):
                m = a.do(lambda e, j=j: e.activation(yc[:, j, :], yc[:, j, :], ACT.Silu, bias=C("conv_ln_b", j), scale=C("conv_ln_g", j)))
            pe.wait(m)
            for j in range(2):
                b = 4 + j
                pe.wait(bank_free[b])

                def mm(e, j=j, b=b):
                    for k in range(2):
                        r = e.matmul(banks[b][:, 0:T], wp1[:, k, j * P:(j + 1) * P], yc[:, k, :], start=(k == 0), stop=(k == 1))
                    return r
                m = pe.do(mm)
                a.wait(m)
                bank_free[b] = a.do(lambda e, j=j, b=b: e.activation(mixT[:, j, :], banks[b][:, 0:T], ACT.Identity, bias=C("conv_pw_b", j)))
            m_conv = bank_free[b]

            mcol = small[:, 256:352].rearrange("p (n c) -> p n c", c=2)
            pe.wait(m_ada, bank_free[0])

            def mm(e):
                for n in range(48):
                    r = e.matmul(banks[0][:, 2 * n:2 * n + 2], ada[0:2, n * P:(n + 1) * P], ident[0:2, 0:2], start=True, stop=True)
                return r
            m = pe.do(mm)
            v.wait(m)
            bada = Call("b_ada").rearrange("p (n o) -> p n o", o=1).to_broadcast([P, 48, 2])
            v.step(lambda e: e.tensor_tensor(mcol, banks[0][:, 0:96].rearrange("p (n c) -> p n c", c=2), bada, ALU.add))
            bank_free[0] = Mark(v.counter, None, v.counter.total)
            scl1, scl2 = small[:, 352:368].rearrange("p (k c) -> p k c", c=2), small[:, 368:376]
            n1 = Call("norm1_g").rearrange("p (k o) -> p k o", o=1).to_broadcast([P, 8, 2])
            v.do(lambda e: e.scalar_tensor_tensor(scl1, mcol[:, 8:16, :], 1.0, n1, ALU.add, ALU.mult))
            m_mod = v.do(lambda e: e.scalar_tensor_tensor(scl2, mcol[:, 32:40, 0], 1.0, Call("norm2_g"), ALU.add, ALU.mult))

            pe.wait(m_att, m_pool, m_conv)
            m_x1 = []
            for nb in range(2):
                c = column_chunk(d["w_out"][0], nb * 512)
                pe.wait(c[1])
                for t in range(NT):
                    b = 2 * (nb % 2) + t
                    m = project_tokens(c, lambda k, t=t: mixT[:, k, t * P:(t + 1) * P], 512, b)
                    v.wait(m)
                    xs = x[:, t * D + nb * 512:t * D + (nb + 1) * 512]
                    bank_free[b] = v.do(lambda e, xs=xs, b=b: e.tensor_tensor(xs, xs, banks[b], ALU.add))
                    m_x1.append(bank_free[b])
                stream.release(c[0], m)
            join()
            assert z.n <= zone.shape[1] - 15 * P
            return mcol, scl1, scl2

        mcol, scl1, scl2 = first_block()
        def moe(name, ne, nf, wr, bias, wg, wu, wd, scale, shift, acc, after):
            ft = nf // P
            nr = NG + NG * ne
            z = Zone()
            hx = z.take(NT * D)
            hg = z.take(NG * KD * P)
            gates_bc = z.take(NG * ne * P)
            selT = z.take(NG * T)
            hcur, gcur, scur = z.take(KD * P), z.take(ne * P), z.take(T)
            act = [z.take(ft * P) for _ in range(2)]
            sil = [z.take(ft * P) for _ in range(2)]
            ysb = z.take(D)
            slotid = z.take(NT * NG).rearrange("p (t g) -> p t g", t=NT)
            gates = z.take(NT * NG * ne).rearrange("p (t g e) -> p t g e", t=NT, g=NG)
            over = group_most[:, 2 * (ne == E2):2 * (ne == E2) + 2]
            keep = z.n
            hr = z.take(KD * T).rearrange("p (k t) -> p k t", k=KD)
            lg = z.take(NT * nr).rearrange("p (t n) -> p t n", t=NT)
            oh = z.take(NT * NG).rearrange("p (t g) -> p t g", t=NT)
            tmp = z.take(NT * NG * ne)
            le = z.take(NT * ne).rearrange("p (t e) -> p t e", t=NT)
            l2 = z.take(NT * ne).rearrange("p (t e) -> p t e", t=NT)
            oh1 = z.take(NT * ne).rearrange("p (t e) -> p t e", t=NT)
            oh2 = z.take(NT * ne).rearrange("p (t e) -> p t e", t=NT)
            one = z.take(16 * NT).rearrange("p (n t) -> p n t", t=NT)
            z.n = keep
            sel = z.take(NT * NG * P).rearrange("p (t g s) -> p t g s", t=NT, g=NG)
            wsel = z.take(NT * ne * P).rearrange("p (t n) -> p t n", t=NT)
            stat = small[:, 0:8]

            m_n = norm_tokens(x, hx, stat, after)
            m_h = to_channels(hx, lambda k: hr[:, k, :], scale, shift, m_n, [None, None])

            pe.wait(m_h)
            wv = wr.rearrange("p (k n) -> p k n", k=KD)
            for t in range(NT):
                def mm(e, t=t):
                    for k in range(KD):
                        r = e.matmul(banks[0][:, t * nr:(t + 1) * nr], hr[:, k, t * P:(t + 1) * P], wv[:, k, :], start=(k == 0), stop=(k == KD - 1))
                    return r
                m = pe.do(mm)
            v.wait(m)
            bb = bias.unsqueeze(1).to_broadcast([P, NT, nr])
            v.step(lambda e: e.tensor_tensor(lg, banks[0][:, 0:NT * nr].rearrange("p (t n) -> p t n", t=NT), bb, ALU.add))

            def bc(col, n):
                return one[:, col, :].unsqueeze(2).to_broadcast([P, NT, n])

            def first_of_max(src, n, out, cm, ci):
                io = Call("iota")[:, 0:n].unsqueeze(1).to_broadcast([P, NT, n])
                v.step(lambda e: e.tensor_reduce(one[:, cm, :], src, AX, ALU.max))
                v.step(lambda e: e.tensor_tensor(out, src, bc(cm, n), ALU.is_lt))
                v.step(lambda e: e.scalar_tensor_tensor(out, out, BIG, io, ALU.mult, ALU.add))
                v.step(lambda e: e.tensor_reduce(one[:, ci, :], out, AX, ALU.min))
                v.step(lambda e: e.tensor_tensor(out, io, bc(ci, n), ALU.is_equal))

            lgg = lg[:, :, 0:NG]
            first_of_max(lgg, NG, oh, 0, 1)
            v.step(lambda e: e.tensor_tensor(tmp[:, 0:NT * NG].rearrange("p (t g) -> p t g", t=NT), lgg, bc(0, NG), ALU.subtract))
            m_d = Mark(v.counter, None, v.counter.total)
            a.wait(m_d)
            m = a.do(lambda e: e.activation(tmp[:, 0:NT * NG], tmp[:, 0:NT * NG], ACT.Exp))
            v.wait(m)
            v.step(lambda e: e.tensor_reduce(one[:, 2, :], tmp[:, 0:NT * NG].rearrange("p (t g) -> p t g", t=NT), AX, ALU.add))
            for t in range(NT):
                src = lg[:, t, NG:].rearrange("p (g e) -> p g e", g=NG)
                tv = tmp[:, t * NG * ne:(t + 1) * NG * ne]
                v.step(lambda e, t=t, src=src, tv=tv: e.tensor_tensor(tv.rearrange("p (g e) -> p g e", g=NG), src, oh[:, t, :].unsqueeze(2).to_broadcast([P, NG, ne]), ALU.mult))
                v.step(lambda e, t=t, tv=tv: e.tensor_reduce(le[:, t, :], tv.rearrange("p (g e) -> p e g", g=NG), AX, ALU.add))
            first_of_max(le, ne, oh1, 3, 4)
            v.step(lambda e: e.scalar_tensor_tensor(l2, oh1, NEG, le, ALU.mult, ALU.add))
            first_of_max(l2, ne, oh2, 5, 6)
            v.step(lambda e: e.tensor_tensor(one[:, 7, :], one[:, 5, :], one[:, 3, :], ALU.subtract))
            m_d = Mark(v.counter, None, v.counter.total)
            a.wait(m_d)
            m = a.do(lambda e: e.activation(one[:, 7, :], one[:, 7, :], ACT.Exp))
            v.wait(m)
            v.step(lambda e: e.tensor_scalar(one[:, 8, :], one[:, 7, :], 1.0, None, ALU.add))
            v.step(lambda e: e.tensor_tensor(one[:, 8, :], one[:, 8, :], one[:, 2, :], ALU.mult))
            v.step(lambda e: e.reciprocal(one[:, 8, :], one[:, 8, :]))
            v.step(lambda e: e.tensor_tensor(one[:, 7, :], one[:, 7, :], one[:, 8, :], ALU.mult))
            v.step(lambda e: e.tensor_tensor(oh1, oh1, bc(8, ne), ALU.mult))
            v.step(lambda e: e.tensor_tensor(oh2, oh2, bc(7, ne), ALU.mult))
            v.step(lambda e: e.tensor_tensor(oh1, oh1, oh2, ALU.add))
            for t in range(NT):
                v.step(lambda e, t=t: e.tensor_tensor(gates[:, t], oh[:, t, :].unsqueeze(2).to_broadcast([P, NG, ne]), oh1[:, t, :].unsqueeze(1).to_broadcast([P, NG, ne]), ALU.mult))

            m_oh = Mark(v.counter, None, v.counter.total)
            pe.wait(m_oh)

            def mm(e):
                e.matmul(banks[1][:, 0:NG], Call("before"), oh[:, 0, :], start=True, stop=True)
                e.matmul(banks[1][:, NG:2 * NG], Call("before"), oh[:, 1, :], start=True, stop=False)
                e.matmul(banks[1][:, NG:2 * NG], ones, oh[:, 0, :], start=False, stop=True)
                e.matmul(banks[1][:, 2 * NG:3 * NG], ones, oh[:, 0, :], start=True, stop=False)
                return e.matmul(banks[1][:, 2 * NG:3 * NG], ones, oh[:, 1, :], start=False, stop=True)
            m = pe.do(mm)
            v.wait(m)
            v.step(lambda e: e.tensor_scalar(tmp[:, 0:NT * NG].rearrange("p (t g) -> p t g", t=NT), oh, -1.0, BIG, ALU.add, ALU.mult))
            v.step(lambda e: e.tensor_tensor(slotid, banks[1][:, 0:NT * NG].rearrange("p (t g) -> p t g", t=NT), oh, ALU.mult))
            v.step(lambda e: e.tensor_tensor(slotid, slotid, tmp[:, 0:NT * NG].rearrange("p (t g) -> p t g", t=NT), ALU.add))
            v.step(lambda e: e.tensor_reduce(over[:, 1:2], banks[1][:, 2 * NG:3 * NG], AX, ALU.max))
            m_over = v.step(lambda e: e.tensor_copy(over[:, 0:1].bitcast(I32), over[:, 1:2]))

            def prepare(start):
                if start:
                    v.step(lambda e: e.tensor_scalar(slotid, slotid, -float(start), None, ALU.add))
                for t in range(NT):
                    for gi in range(NG):
                        m = v.do(lambda e, t=t, gi=gi: e.tensor_scalar(sel[:, t, gi, :], Call("iota"), slotid[:, t, gi:gi + 1], None, ALU.is_equal))
                v.wait(m)
                pe.wait(m)
                f = [None] * 4
                m_out = []
                for gi in range(NG):
                    for half in range(2):
                        b = half

                        def mm(e, gi=gi, half=half, b=b):
                            for kk in range(4):
                                k = half * 4 + kk
                                for t in range(NT):
                                    r = e.matmul(banks[b][:, kk * P:(kk + 1) * P], hx[:, t * D + k * P:t * D + (k + 1) * P], sel[:, t, gi, :], start=(t == 0), stop=(t == NT - 1))
                            return r
                        pe.wait(f[b])
                        m = pe.do(mm)
                        q = a if half else v
                        q.wait(m)
                        for kk in range(4):
                            k = half * 4 + kk
                            dst = hg[:, gi * D + k * P:gi * D + (k + 1) * P]
                            src = banks[b][:, kk * P:(kk + 1) * P]
                            sc_, sh_ = scale(k), None if shift is None else shift(k)
                            if q is v:
                                m = v.do(lambda e, dst=dst, src=src, sc_=sc_, sh_=sh_: e.tensor_scalar(dst, src, sc_, sh_, ALU.mult, *([] if sh_ is None else [ALU.add])))
                            else:
                                m = a.do(lambda e, dst=dst, src=src, sc_=sc_, sh_=sh_: e.activation(dst, src, ACT.Identity, bias=0.0 if sh_ is None else sh_, scale=sc_))
                        f[b] = m
                        m_out.append(m)
                    for t in range(NT):
                        if gi or t:
                            v.wait(m_w)
                        m = v.do(lambda e, t=t, gi=gi: e.tensor_tensor(wsel[:, t, :].rearrange("p (e s) -> p e s", e=ne), sel[:, t, gi, :].unsqueeze(1).to_broadcast([P, ne, P]), gates[:, t, gi, :].unsqueeze(2).to_broadcast([P, ne, P]), ALU.mult))
                        m_w = m if t == 0 and gi == 0 else m_w
                    pe.wait(m)
                    for nb in range(ne * P // 512):
                        b = 2 + nb

                        def mm(e, nb=nb, b=b):
                            for t in range(NT):
                                r = e.matmul(banks[b], ones, wsel[:, t, nb * 512:(nb + 1) * 512], start=(t == 0), stop=(t == NT - 1))
                            return r
                        pe.wait(f[b])
                        m_w = pe.do(mm)
                        a.wait(m_w)
                        o = gi * ne * P + nb * 512
                        f[b] = a.do(lambda e, o=o, b=b: e.activation(gates_bc[:, o:o + 512], banks[b], ACT.Copy))
                    m_out.append(f[b])
                for gp in range(NG // 2):
                    b = 4 + gp
                    for gi in range(2):
                        for t in range(NT):
                            m = pe.do(lambda e, gi=gi, t=t, gp=gp, b=b: e.transpose(banks[b][:, gi * T + t * P:gi * T + (t + 1) * P], sel[:, t, 2 * gp + gi, :], ident))
                    a.wait(m)
                    m_out.append(a.do(lambda e, gp=gp, b=b: e.activation(selT[:, gp * 2 * T:(gp + 1) * 2 * T], banks[b], ACT.Copy)))
                return m_out

            pack = 2 if nf == F1 else 1

            def sources(ex):
                return (wg[bass.ds(ex, 1)].rearrange("o (k p) f -> p (o k) f", p=P), wu[bass.ds(ex, 1)].rearrange("o (k p) f -> p (o k) f", p=P),
                        wd[bass.ds(ex, 1)].rearrange("o (k p) n -> p (o k) n", p=P))

            half_a = lambda slot: slot[:, 0:KD * nf].rearrange("p (k n) -> p k n", k=KD)
            half_b = lambda slot: slot[:, KD * nf:2 * KD * nf].rearrange("p (k n) -> p k n", k=KD)
            down_a = lambda slot: slot[:, 0:ft * D].rearrange("p (k n) -> p k n", k=ft)
            down_b = lambda slot: slot[:, ft * D:2 * ft * D].rearrange("p (k n) -> p k n", k=ft)

            groups_per_turn = 2 if pack == 2 else 1
            turns = NG // groups_per_turn
            nx = ne * groups_per_turn
            plan = []
            if pack == 2:
                for e2 in range(0, nx, 2):
                    plan.append([("gu", e2, [(half_a, 0, e2), (half_b, 1, e2)])])
                    plan.append([("gu", e2 + 1, [(half_a, 0, e2 + 1), (half_b, 1, e2 + 1)])])
                    plan.append([("d", e2, [(down_a, 2, e2), (down_b, 2, e2 + 1)])])
                plan = [p_[0] for p_ in plan]
            else:
                for ex in range(nx + 1):
                    if ex < nx:
                        plan.append(("g", ex, [(half_a, 0, ex)]))
                        plan.append(("u", ex, [(half_a, 1, ex)]))
                    if ex > 0:
                        plan.append(("d", ex - 1, [(down_a, 2, ex - 1)]))
            assert len(plan) % RING == 0

            base = stream.n

            def load_chunk(j, turn_of):
                k = (base + j) % RING
                for view, which, ex in plan[j][2]:
                    def go(e, i=None, view=view, which=which, ex=ex, k=k):
                        t0 = turn_of(i)
                        return e.dma_start(view(ring[k]), sources(t0 * nx + ex)[which])
                    m = s.do(go, stream.slot_in[k], 16)
                return m

            def groups(m_ready):
                for k in range(RING):
                    s.wait(stream.released[(base + k) % RING])
                    load_chunk(k, lambda i: 0)
                for q in (pe, v, a):
                    q.wait(m_ready)

                def turn():
                    ahead = [Later() for _ in range(RING)]
                    loaded = ahead + [None] * (len(plan) - RING)
                    released = [None] * len(plan)
                    rel = [Later2() for _ in plan]
                    for j in range(RING, len(plan)):
                        s.wait(rel[j - RING])
                        loaded[j] = load_chunk(j, lambda i: i)
                    s.ahead_part = True
                    for j in range(RING):
                        s.wait(rel[len(plan) - RING + j])
                        ahead[j].set(load_chunk(j, lambda i: i + 1))
                    at = {}
                    for j, (what, ex, _) in enumerate(plan):
                        at[what, ex] = j

                    prev_gu, prev_sel, prev_add = Later(), Later(), [Later(), Later()]
                    prev_bank = [Later(), Later()]
                    prev_y = [Later(), Later()]
                    prev_down = [Later(), Later()]
                    act_m, gu_free, down_m = {}, {}, {}
                    state = {}

                    def gate_up(ex):
                        p2 = ex % 2
                        gl, el = ex // ne, ex % ne
                        if el == 0:
                            if gl:
                                v.wait(state["gu"]), a.wait(state["gu"])
                                v.wait(state["scatter"])
                            else:
                                v.wait(prev_gu, prev_sel), a.wait(prev_gu)
                            m1 = v.do(lambda e, i: e.tensor_copy(hcur, hg[:, bass.ds((i * groups_per_turn + gl) * D, D)]))
                            m2 = a.do(lambda e, i: e.activation(gcur, gates_bc[:, bass.ds((i * groups_per_turn + gl) * (ne * P), ne * P)], ACT.Copy))
                            m3 = v.do(lambda e, i: e.tensor_copy(scur, selT[:, bass.ds((i * groups_per_turn + gl) * T, T)]))
                            v.wait(m2)
                            pe.wait(m1)
                            state["scur"] = m3
                        pe.wait(gu_free[ex - 2] if ex >= 2 else prev_bank[ex])
                        gb, ub = banks[2 * p2], banks[2 * p2 + 1]
                        ms = []
                        for n, (bk, key) in enumerate(((gb, "g"), (ub, "u"))):
                            if pack == 2:
                                j = at["gu", ex]
                                view = half_b if n else half_a
                            else:
                                j = at[key, ex]
                                view = half_a
                            if n == 0 or pack == 1:
                                pe.wait(loaded[j])
                            w = view(ring[(base + j) % RING])

                            def mm(e, i, bk=bk, w=w):
                                for f_ in range(ft):
                                    for k in range(KD):
                                        r = e.matmul(bk[:, f_ * P:(f_ + 1) * P], w[:, k, f_ * P:(f_ + 1) * P], hcur[:, k * P:(k + 1) * P], start=(k == 0), stop=(k == KD - 1))
                                return r
                            ms.append(pe.do(mm))
                            rel[j].set(ms[-1])
                        state["gu"] = ms[1]
                        if ex == nx - 1:
                            prev_gu.set(ms[1])
                        a.wait(ms[0])
                        if ex >= 2:
                            a.wait(act_m[ex - 2])
                        else:
                            a.wait(prev_bank[ex])
                        m = a.do(lambda e, i: e.activation(sil[p2], gb[:, 0:ft * P], ACT.Silu))
                        v.wait(m, ms[1])
                        m = v.do(lambda e, i: e.tensor_tensor(sil[p2], sil[p2], ub[:, 0:ft * P], ALU.mult))
                        gu_free[ex] = m
                        v.wait(m)
                        v.wait(down_m[ex - 2] if ex >= 2 else prev_down[ex])
                        gc = gcur[:, el * P:(el + 1) * P].unsqueeze(1).to_broadcast([P, ft, P])
                        act_m[ex] = v.do(lambda e, i: e.tensor_tensor(act[p2].rearrange("p (f s) -> p f s", f=ft), sil[p2].rearrange("p (f s) -> p f s", f=ft), gc, ALU.mult))
                        if ex >= nx - 2:
                            prev_bank[ex - nx + 2].set(act_m[ex])

                    def down(ex):
                        p2 = ex % 2
                        gl, el = ex // ne, ex % ne
                        j = at["d", ex - ex % 2] if pack == 2 else at["d", ex]
                        w = (down_b if pack == 2 and ex % 2 else down_a)(ring[(base + j) % RING])
                        pe.wait(loaded[j], act_m[ex])
                        if el == 0:
                            pe.wait(state["y"] if gl else prev_y)

                        def mm(e, i):
                            for f_ in range(ft):
                                for nb in range(2):
                                    r = e.matmul(banks[4 + nb], act[p2][:, f_ * P:(f_ + 1) * P], w[:, f_, nb * 512:(nb + 1) * 512],
                                                 start=(el == 0 and f_ == 0), stop=(el == ne - 1 and f_ == ft - 1))
                            return r
                        down_m[ex] = pe.do(mm)
                        if pack == 1 or ex % 2:
                            rel[j].set(down_m[ex])
                        if ex >= nx - 2:
                            prev_down[ex - nx + 2].set(down_m[ex])
                        if el == ne - 1:
                            scatter(gl)

                    def scatter(gl):
                        v.wait(down_m[gl * ne + ne - 1], state["scatter"] if gl else prev_sel)
                        a.wait(down_m[gl * ne + ne - 1], state["scatter"] if gl else prev_sel)
                        y0 = v.do(lambda e, i: e.tensor_copy(ysb[:, 0:512], banks[4]))
                        y1 = a.do(lambda e, i: e.activation(ysb[:, 512:1024], banks[5], ACT.Copy))
                        state["y"] = [y0, y1]
                        if gl == groups_per_turn - 1:
                            prev_y[0].set(y0), prev_y[1].set(y1)
                        pe.wait(y0, y1, state["scur"])
                        for n, (t, nb) in enumerate([(t, nb) for t in range(NT) for nb in range(2)]):
                            b = 6 + n % 2
                            pe.wait(state["add", n - 2] if n >= 2 else (state["add", n + 2] if gl else prev_add[n]))
                            m = pe.do(lambda e, i, t=t, nb=nb, b=b: e.matmul(banks[b], scur[:, t * P:(t + 1) * P], ysb[:, nb * 512:(nb + 1) * 512], start=True, stop=True))
                            state["scatter"] = m
                            v.wait(m)
                            av = acc[:, t * D + nb * 512:t * D + (nb + 1) * 512]
                            v.wait(state.get(("acc", t, nb)) or prev_acc[t * 2 + nb])
                            m = v.do(lambda e, i, av=av, b=b: e.tensor_tensor(av, av, banks[b], ALU.add))
                            state["add", n] = m
                            state["acc", t, nb] = m
                            if gl == groups_per_turn - 1:
                                prev_acc[t * 2 + nb].set(m)
                                if n >= 2:
                                    prev_add[n - 2].set(m)
                        if gl == groups_per_turn - 1:
                            prev_sel.set(state["scatter"])

                    prev_acc = [Later() for _ in range(4)]
                    for what, ex, _ in plan:
                        if what in ("u", "gu"):
                            gate_up(ex)
                        if what == "d":
                            down(ex)
                            if pack == 2:
                                down(ex + 1)
                    for k in range(RING):
                        stream.released[(base + k) % RING] = rel[len(plan) - RING + k].mark
                prog.loop(turns, turn)

            m_ready = prepare(0)
            groups(m_ready)

            def second_pass():
                released, stream.released = stream.released, [None] * RING
                stream.slot_in = [prog.new_counter(f"{name}_slot_in{k}") for k in range(RING)]
                groups(prepare(P))
                stream.released, stream.slot_in = released, slot_in
            for q in prog.queues:
                q.wait(m_over)
            s.wait(stream.released)
            prog.branch(over[0:1, 0:1].bitcast(I32), T, P, name, second_pass)

        moe("moe1", E1, F1, w_route[0], R("r1_b"), d["w_gate"][0], d["w_up"][0], d["w_down"][0],
            lambda k: C("ffn_norm_g", k), None, x, [])
        join()
        w2 = d["w_in_2"][0]
        for i_ in range(8):
            bank_free[i_] = None
        z = Zone()
        hT = z.take(KD * 2 * T).rearrange("p (k t) -> p k t", k=KD)
        yaT = z.take(KD * T).rearrange("p (k t) -> p k t", k=KD)
        brow = z.take(2048)
        w_if = z.take(KD * P).rearrange("p (k n) -> p k n", k=KD)
        keep_gla = z.n
        cx, xn, cn = z.take(NT * D), z.take(NT * D), z.take(NT * D)
        w16 = z.take(KD * 16).rearrange("p (k n) -> p k n", k=KD)

        s.do(lambda e: e.dma_start(cx.rearrange("p (t n) -> p t n", t=NT), d["ctx_2"][0].rearrange("(t p) n -> p t n", p=P)), params_in, 16)
        s.do(lambda e: e.dma_start(brow[0:1, 0:1024], d["b_in_2"][0:1, O_HI:O_HI + 1024]), params_in, 16)
        s.do(lambda e: e.dma_start(brow[0:1, 1024:2048], d["b_in_2"][0:1, O_MV:O_MV + 1024]), params_in, 16)
        m_small = s.do(lambda e: e.dma_start(w16, w2[:, O_IF:O_IF + 16].rearrange("(k p) n -> p k n", p=P)), params_in, 16)
        m = g.do(lambda e: e.memset(w_if, 0.0))
        g.wait(m, m_small)
        for n in range(4):
            m_wif = g.do(lambda e, n=n: e.tensor_copy(w_if[:, :, 32 * n:32 * n + 4], w16[:, :, 4 * n:4 * n + 4]))

        lbv = Call("lb").rearrange("p (d l j) -> p d l j", d=2, l=2)
        lbs = small[:, 376:408].rearrange("p (o d j) -> p o d j", o=2, d=2)
        nbf = small[:, 408:424]
        v.do(lambda e: e.tensor_tensor(lbs[:, 0], lbv[:, :, 0, :], lbv[:, :, 1, :], ALU.subtract))
        v.do(lambda e: e.tensor_scalar(nbf, C("b_in", O_FF // P, 16), -1.0, None, ALU.mult))
        m = v.do(lambda e: e.tensor_tensor(lbs[:, 1], lbv[:, :, 1, :], lbv[:, :, 0, :], ALU.subtract))
        a.wait(m)
        m_lb = a.do(lambda e: e.activation(lbs, lbs, ACT.Sigmoid))

        m_n = norm_tokens(x, xn, small[:, 0:2])
        m_n2 = norm_tokens(cx, cn, small[:, 2:4], m_small)
        m_h = to_channels(xn, lambda k: hT[:, k, 0:T], lambda k: scl1[:, k, 0:1], lambda k: mcol[:, k, 0:1], m_n, [None, None])
        m_h2 = to_channels(cn, lambda k: hT[:, k, T:2 * T], lambda k: scl1[:, k, 1:2], lambda k: mcol[:, k, 1:2], m_n2, m_h[-2:])
        bank_free[6], bank_free[7] = m_h2[-2:]
        pe.wait(m_h, m_h2)
        h_all = lambda k: hT[:, k, :]
        h_lat = lambda k: hT[:, k, 0:T]

        def gated_linear_attention():
            z.n = keep_gla
            kk_ = z.take(2 * 2 * HB * T).rearrange("p (d n) -> p d n", d=2)
            ff_ = z.take(2 * 2 * HB * T).rearrange("p (d n) -> p d n", d=2)
            q_ = z.take(HB * T)
            qd = z.take(2 * HB * T).rearrange("p (d n) -> p d n", d=2)
            v_ = z.take(4 * 512).rearrange("p (s n) -> p s n", s=4)
            AT = z.take(HB * 4 * T).rearrange("p (h s t) -> p h s t", h=HB, s=4)
            SL = HB * T
            masks = level_mask.rearrange("p (n t) -> p n t", n=15)
            v.wait(m_params, m_mask8), a.wait(m_params)
            m_ya = None
            m_all = [m_h, m_h2]
            for q in (v, a, g):
                q.wait(m_all, m_wif, m_lb)

            prev_av = None
            for hb in range(HG // HB):
                heads = range(hb * HB, hb * HB + HB)
                for q in (v, a, g):
                    q.wait(prev_av)
                m_k = [[], []]
                m_f = [[], []]
                for dr, off in ((FWD, O_FF), (BWD, O_FB)):
                    c = column_chunk(w2, off + hb * 512)
                    pe.wait(c[1])
                    for j in range(HB):
                        b = next_bank()
                        m = project(c, j, h_all, 2 * T, b)
                        tile = 8 * dr + hb * HB + j
                        fv = ff_[:, dr, :].rearrange("p (s h t) -> p s h t", s=2, h=HB)[:, :, j, :]
                        kv = kk_[:, dr, :].rearrange("p (s h t) -> p s h t", s=2, h=HB)[:, :, j, :]
                        src = banks[b].rearrange("p (s t) -> p s t", s=2)
                        a.wait(m)
                        m1 = a.do(lambda e, fv=fv, src=src, tile=tile: e.activation(fv, src, ACT.Sigmoid, bias=C("b_in", O_FF // P + tile)))
                        m2 = a.do(lambda e, kv=kv, src=src, tile=tile: e.activation(kv, src, ACT.Sigmoid, bias=nbf[:, tile:tile + 1], scale=-1.0))
                        bank_free[b] = m2
                        lo, om = lbs[:, 0, dr, hb * HB + j:hb * HB + j + 1], lbs[:, 1, dr, hb * HB + j:hb * HB + j + 1]
                        v.wait(m1)
                        m_f[dr].append(v.do(lambda e, fv=fv, lo=lo, om=om: e.tensor_scalar(fv, fv, om, lo, ALU.mult, ALU.add)))
                        g.wait(m2)
                        m_k[dr].append(g.do(lambda e, kv=kv, om=om: e.tensor_scalar(kv, kv, om, None, ALU.mult)))
                    stream.release(c[0], m)
                c = column_chunk(w2, O_Q + hb * 512)
                pe.wait(c[1])
                for j in range(HB):
                    b = next_bank()
                    m = project(c, j, h_lat, T, b)
                    a.wait(m)
                    m_q = a.do(lambda e, j=j, b=b, hb=hb: e.activation(q_[:, j * T:(j + 1) * T], banks[b][:, 0:T], ACT.Silu, bias=C("b_in", O_Q // P + hb * HB + j)))
                    bank_free[b] = m_q
                stream.release(c[0], m)
                c = column_chunk(w2, O_HI + hb * 512)
                pe.wait(c[1])
                for st in range(4):
                    b = next_bank()
                    m = project_tokens(c, lambda k, st=st: hT[:, k, st * P:(st + 1) * P], 512, b, brow[0:1, hb * 512:(hb + 1) * 512])
                    a.wait(m)
                    m_v = a.do(lambda e, st=st, b=b: e.activation(v_[:, st, :], banks[b], ACT.Copy))
                    bank_free[b] = m_v
                stream.release(c[0], m)

                pe.wait(m_q, m_k)
                pair = [[2, 3], [4, 5]]
                for t in range(NT):
                    b = pair[0][t]
                    pe.wait(bank_free[b])

                    def mm(e, t=t, b=b):
                        for h in range(HB):
                            for dr in range(2):
                                r = e.matmul(banks[b][:, h * P:(h + 1) * P], kk_[:, dr, h * T + t * P:h * T + (t + 1) * P], q_[:, h * T + t * P:h * T + (t + 1) * P], start=(dr == 0), stop=(dr == 1))
                        return r
                    m = pe.do(mm)
                    v.wait(m)
                    av = AT[:, :, t, t * P:(t + 1) * P]
                    m_ev0 = v.do(lambda e, av=av, b=b: e.tensor_copy(av, banks[b].rearrange("p (h t) -> p h t", h=HB)))
                    bank_free[b] = m_ev0
                v.wait(m_q, m_f[0])
                g.wait(m_q, m_f[1])
                eng = [v, g]
                m_qd = [eng[dr].do(lambda e, dr=dr: e.tensor_tensor(qd[:, dr, :], q_, ff_[:, dr, 0:SL], ALU.mult)) for dr in range(2)]
                m_kd = [m_k[0][-1], m_k[1][-1]]
                m_at = [m_ev0, m_ev0]
                for li, m_ in enumerate(LEVELS + [P]):
                    for dr in range(2):
                        pe.wait(m_qd[dr], m_kd[dr])
                        m_mm = None
                        if m_ < P:
                            for t in range(NT):
                                b = pair[dr][t]
                                pe.wait(bank_free[b])

                                def mm(e, t=t, b=b, dr=dr):
                                    for h in range(HB):
                                        o = h * T + t * P
                                        r = e.matmul(banks[b][:, h * P:(h + 1) * P], kk_[:, dr, o:o + P], qd[:, dr, o:o + P], start=True, stop=True)
                                    return r
                                m_mm = pe.do(mm)
                                v.wait(m_mm, m_at[t])
                                av = AT[:, :, t, t * P:(t + 1) * P]
                                mk = masks[:, 1 + 7 * dr + li:2 + 7 * dr + li, :].to_broadcast([P, HB, P])
                                m_at[t] = v.do(lambda e, av=av, mk=mk, b=b: e.copy_predicated(av, mk, banks[b].rearrange("p (h t) -> p h t", h=HB)))
                                bank_free[b] = m_at[t]
                        else:
                            kt, qt = (0, 1) if dr == FWD else (1, 0)
                            b = pair[dr][0]
                            pe.wait(bank_free[b])

                            def mm(e, kt=kt, qt=qt, b=b, dr=dr):
                                for h in range(HB):
                                    r = e.matmul(banks[b][:, h * P:(h + 1) * P], kk_[:, dr, h * T + kt * P:h * T + (kt + 1) * P], qd[:, dr, h * T + qt * P:h * T + (qt + 1) * P], start=True, stop=True)
                                return r
                            m_mm = pe.do(mm)
                            a.wait(m_mm)
                            bank_free[b] = a.do(lambda e, kt=kt, qt=qt, b=b: e.activation(AT[:, :, kt, qt * P:(qt + 1) * P], banks[b].rearrange("p (h t) -> p h t", h=HB), ACT.Copy))
                        q = eng[dr]
                        q.wait(m_mm)
                        late, early = (1, 0) if dr == FWD else (0, 1)
                        nblk = 2 * SL // (2 * m_)
                        kb = kk_[:, dr, :].rearrange("p (n o m) -> p n o m", o=2, m=m_)
                        qb = qd[:, dr, :].rearrange("p (n o m) -> p n o m", o=2, m=m_)
                        fb = ff_[:, dr, :].rearrange("p (n o m) -> p n o m", o=2, m=m_)
                        nl = SL // (2 * m_)
                        m_qd[dr] = q.do(lambda e, qb=qb, fb=fb, nl=nl, late=late, early=early, m_=m_: e.tensor_tensor(qb[:, :, late, :], qb[:, :, late, :], fb[:, 0:nl, early, 0:1].to_broadcast([P, nl, m_]), ALU.mult))
                        m_kd[dr] = q.do(lambda e, kb=kb, fb=fb, nblk=nblk, late=late, early=early, m_=m_: e.tensor_tensor(kb[:, :, early, :], kb[:, :, early, :], fb[:, :, late, 0:1].to_broadcast([P, nblk, m_]), ALU.mult))
                        q.wait(m_kd[dr])
                        if m_ < P:
                            m_t = q.do(lambda e, fb=fb: e.tensor_tensor(fb[:, :, 0, 0], fb[:, :, 0, 0], fb[:, :, 1, 0], ALU.mult))
                            q.wait(m_t)
                for n in range(HB * 2):
                    h, cti = n // 2, n % 2
                    b = 2 + (n // 2) % 4
                    if cti == 0:
                        pe.wait(bank_free[b], m_qd, m_kd)

                    def mm(e, h=h, cti=cti, b=b):
                        for dr in range(2):
                            o = SL + h * T + cti * P
                            r = e.matmul(banks[b][:, cti * T:(cti + 1) * T], kk_[:, dr, o:o + P], qd[:, dr, h * T:(h + 1) * T], start=(dr == 0), stop=(dr == 1))
                        return r
                    m = pe.do(mm)
                    if cti == 1:
                        a.wait(m)
                        m_at2 = a.do(lambda e, h=h, b=b: e.activation(AT[:, h, 2:4, :].rearrange("p s t -> p (s t)"), banks[b], ACT.Copy))
                        bank_free[b] = m_at2
                pe.wait(m_at, m_at2, m_v)
                for hp in range(HB // 2):
                    b = 6 + hp
                    pe.wait(bank_free[b])

                    def mm(e, hp=hp, b=b):
                        for o in range(2):
                            h = 2 * hp + o
                            for st in range(4):
                                r = e.matmul(banks[b][:, o * T:(o + 1) * T], v_[:, st, h * P:(h + 1) * P], AT[:, h, st, :], start=(st == 0), stop=(st == 3))
                        return r
                    m = pe.do(mm)
                    prev_av = m
                    sqd = qd[:, hp, 0:512]
                    a.wait(m)
                    m = a.do(lambda e, b=b, sqd=sqd: e.activation(sqd, banks[b], ACT.Square))
                    pe.wait(m, bank_free[2 + hp])
                    m = pe.do(lambda e, hp=hp, sqd=sqd: e.matmul(banks[2 + hp], ones, sqd, start=True, stop=True))
                    m = rstd_of(banks[2 + hp], sqd, 1.0 / P, m)
                    bank_free[2 + hp] = m
                    for o in range(2):
                        h = hb * HB + 2 * hp + o
                        m_ya = v.do(lambda e, h=h, o=o, b=b, sqd=sqd: e.scalar_tensor_tensor(yaT[:, h, :], banks[b][:, o * T:(o + 1) * T], C("hg_norm_g", h), sqd[:, o * T:(o + 1) * T], ALU.mult, ALU.mult))
                    bank_free[b] = m_ya
                prev_av = [prev_av, m_ya]
            gt = [z_ for z_ in (q_[:, 0:T], q_[:, T:2 * T])]
            m_g = [None, None]
            a.wait(prev_av)
            for nb in range(2):
                c = column_chunk(w2, O_HG + nb * 512)
                pe.wait(c[1])
                for j in range(4):
                    b = next_bank()
                    m = project(c, j, h_lat, T, b)
                    k = nb * 4 + j
                    a.wait(m, m_g[k % 2])
                    bank_free[b] = a.do(lambda e, k=k, b=b: e.activation(gt[k % 2], banks[b][:, 0:T], ACT.Silu, bias=C("b_in", O_HG // P + k)))
                    v.wait(bank_free[b])
                    m_g[k % 2] = v.do(lambda e, k=k: e.tensor_tensor(yaT[:, k, :], yaT[:, k, :], gt[k % 2], ALU.mult))
                stream.release(c[0], m)
            m_yaT = m_g


        gated_linear_attention()
        def mlstm():
            join()
            z.n = keep_gla
            qT = z.take(MLH * T).rearrange("p (h t) -> p h t", h=MLH)
            kT = z.take(MLH * 2 * T).rearrange("p (h s t) -> p h s t", h=MLH, s=2)
            shared = z.take(9 * 2 * T)
            va = shared[:, 0:4 * MLH * (MLV + 1)].rearrange("p (s h n) -> p s h n", s=4, h=MLH)
            Rb = z.take(8 * T).rearrange("p (d h t) -> p d h t", d=2, h=MLH)
            Rd = z.take(8 * T).rearrange("p (d h t) -> p d h t", d=2, h=MLH)
            cc_ = z.take(8 * 36).rearrange("p (q s n) -> p q s n", q=2, s=4)
            nm = z.take(2 * 36).rearrange("p (q n) -> p q n", q=2)
            share = z.n
            PADM = MLC // 2
            W = T + 2 * PADM
            raw = z.take(12 * W).rearrange("p (n t) -> p n t", n=12)
            names = "fr LI LF B M CS0 CS1 CO0 CO1".split()
            rw = {n: shared[:, i_ * 2 * T:(i_ + 1) * 2 * T] for i_, n in enumerate(names)}
            Rr, NMr = z.take(T), z.take(T)
            hp = z.take(KD * T).rearrange("p (k t) -> p k t", k=KD)

            def permuted(ap):
                return ap.rearrange("p (r c) -> p c r", r=GRID_R)

            for k in range(KD):
                m_hp = g.do(lambda e, k=k: e.tensor_copy(hp[:, k, :].rearrange("p (c r) -> p c r", r=GRID_R), permuted(hT[:, k, 0:T])))
            m_pad = g.do(lambda e: e.memset(raw[:, :, 0:PADM], 0.0))
            m_pad = g.do(lambda e: e.memset(raw[:, :, W - PADM:W], 0.0))
            m_z1 = g.do(lambda e: e.memset(rw["LI"], 0.0))
            m_z2 = g.do(lambda e: e.memset(rw["LF"], 0.0))
            m_z3 = g.do(lambda e: e.memset(rw["CO0"], 0.0))
            m_z3 = g.do(lambda e: e.memset(rw["CO1"], 0.0))
            m_z3 = g.do(lambda e: e.memset(Rr, 0.0))
            m_z3 = g.do(lambda e: e.memset(NMr, 0.0))

            pe.wait(bank_free[2])

            def mm(e):
                for k in range(KD):
                    r = e.matmul(banks[2], w_if[:, k, :], hT[:, k, :], start=(k == 0), stop=(k == KD - 1))
                return r
            m = pe.do(mm)
            a.wait(m)
            a.do(lambda e: e.activation(rw["fr"][:, 0:T], banks[2][:, T:2 * T], ACT.Identity, bias=C("b_if")))
            m = a.do(lambda e: e.activation(rw["fr"][:, T:2 * T].rearrange("p (c r) -> p c r", r=GRID_R), permuted(banks[2][:, 0:T]), ACT.Identity, bias=C("b_if")))
            bank_free[2] = m
            v.wait(m, m_z3)

            def turned(dst, src, o, o2):
                v.do(lambda e: e.tensor_copy(dst[0:4, :], src[o:o + 4, :]))
                v.do(lambda e: e.tensor_copy(dst[32:36, 0:T], src[o2:o2 + 4, T - 1::-1]))
                return v.do(lambda e: e.tensor_copy(dst[32:36, T:2 * T], src[o2:o2 + 4, 2 * T - 1:T - 1:-1]))
            turned(rw["LI"], rw["fr"], 0, 32)
            v.wait(turned(rw["LF"], rw["fr"], 64, 96))
            H = slice(0, 36)
            LI, LF, B_, M_ = (rw[n][H, :] for n in ("LI", "LF", "B", "M"))
            m_lf = Mark(v.counter, None, v.counter.total)
            a.wait(m_lf)
            a.step(lambda e: e.activation(B_, LF, ACT.Abs))
            m = a.step(lambda e: e.activation(B_, B_, ACT.Exp, scale=-1.0))
            m = a.do(lambda e: e.activation(B_, B_, ACT.Ln, bias=1.0))
            v.wait(m)
            v.step(lambda e: e.scalar_tensor_tensor(LF, LF, 0.0, B_, ALU.min, ALU.subtract))
            v.do(lambda e: e.tensor_tensor_scan(M_, LF, LI, 0.0, ALU.add, ALU.max))
            for j in range(4):
                v.do(lambda e, j=j: e.tensor_tensor_scan(B_[:, j * P:(j + 1) * P], ones[0:36, :], LF[:, j * P:(j + 1) * P], 0.0, ALU.mult, ALU.add))
            v.wait(Mark(v.counter, None, v.counter.total))
            CS = [rw["CS0"][H, :], rw["CS1"][H, :]]
            for qs in (0, 1):
                v.step(lambda e, qs=qs: e.tensor_tensor(CS[qs], LI, B_, ALU.subtract))
            v.step(lambda e: e.tensor_tensor(LI[:, 0:T], B_[:, T:2 * T], M_[:, T:2 * T], ALU.subtract))
            v.step(lambda e: e.tensor_copy(LI[:, T:2 * T], M_[:, T:2 * T]))
            for qs in (0, 1):
                for j in range(2 + qs):
                    for kt in range(j + 1):
                        v.step(lambda e, qs=qs, j=j, kt=kt: e.tensor_scalar(CS[qs][:, kt * P:(kt + 1) * P], CS[qs][:, kt * P:(kt + 1) * P], B_[:, j * P + P - 1:(j + 1) * P], None, ALU.add))
            CO = [rw["CO0"], rw["CO1"]]
            for qo in (0, 1):
                v.do(lambda e, qo=qo: e.tensor_copy(CO[qo][0:4, :], CS[qo][0:4, :]))
                v.do(lambda e, qo=qo: e.tensor_copy(CO[qo][32:36, 0:T], CS[1 - qo][32:36, T - 1::-1]))
                v.do(lambda e, qo=qo: e.tensor_copy(CO[qo][32:36, T:2 * T], CS[1 - qo][32:36, 2 * T - 1:T - 1:-1]))
            v.do(lambda e: e.tensor_copy(Rr[0:4, :], LI[0:4, 0:T]))
            v.do(lambda e: e.tensor_copy(Rr[32:36, :], LI[32:36, T - 1::-1]))
            v.do(lambda e: e.tensor_copy(NMr[0:4, :], LI[0:4, T:2 * T]))
            m_rows = v.do(lambda e: e.tensor_copy(NMr[32:36, :], LI[32:36, 2 * T - 1:T - 1:-1]))
            pe.wait(m_rows, bank_free[2], bank_free[3], bank_free[4], bank_free[5], bank_free[6])

            def mm(e):
                for qo in range(2):
                    for st in range(4):
                        o = (qo * 4 + st) * 36
                        r = e.transpose(banks[2][:, o:o + 36], CO[qo][0:36, st * P:(st + 1) * P], ident[0:36, 0:36])
                for t in range(2):
                    o = (8 + t) * 36
                    r = e.transpose(banks[2][:, o:o + 36], NMr[0:36, t * P:(t + 1) * P], ident[0:36, 0:36])
                return r
            m = pe.do(mm)
            v.wait(m)
            m_cc = v.do(lambda e: e.tensor_copy(cc_.rearrange("p q s n -> p (q s n)"), banks[2][:, 0:288]))
            a.wait(m, m_cc)
            m_nm = a.do(lambda e: e.activation(nm.rearrange("p q n -> p (q n)"), banks[2][:, 288:360], ACT.Exp, scale=-1.0))
            bank_free[2] = m_nm
            for n in range(4):
                b = 3 + n

                def mm(e, n=n, b=b):
                    for o in range(2):
                        r = e.matmul(banks[b][:, o * T:(o + 1) * T], pick_row[0:36, (2 * n + o) * P:(2 * n + o + 1) * P], Rr[0:36, :], start=True, stop=True)
                    return r
                m = pe.do(mm)
                a.wait(m)
                m = a.do(lambda e, n=n, b=b: e.activation(Rb.rearrange("p d h t -> p (d h t)")[:, n * 512:(n + 1) * 512], banks[b], ACT.Copy))
                bank_free[b] = m
            m_Rb = m
            v.wait(m)
            for dr in range(2):
                for t in range(NT):
                    mk = (Call("mask_f") if dr == FWD else Call("mask_b")).unsqueeze(1).to_broadcast([P, MLH, P])
                    m_Rd = v.do(lambda e, dr=dr, t=t, mk=mk: e.tensor_tensor(Rd[:, dr, :, t * P:(t + 1) * P], Rb[:, dr, :, t * P:(t + 1) * P], mk, ALU.add))

            a.wait(m_pad), v.wait(m_pad)
            m_c = []
            for what, off in ((0, O_MQ), (1, O_MK)):
                c = column_chunk(w2, off)
                pe.wait(c[1])
                for h in range(MLH):
                    b = next_bank()
                    m = project(c, h, h_all if what else h_lat, 2 * T if what else T, b)
                    row = 4 + 2 * h + 1 if what else h
                    bias = C("b_in", off // P + h)
                    a.wait(m)
                    m = a.do(lambda e, row=row, b=b, bias=bias: e.activation(raw[:, row, PADM:PADM + T].rearrange("p (c r) -> p c r", r=GRID_R), permuted(banks[b][:, 0:T]), ACT.Identity, bias=bias))
                    if what:
                        m = a.do(lambda e, row=row, b=b, bias=bias: e.activation(raw[:, row - 1, PADM:PADM + T], banks[b][:, T:2 * T], ACT.Identity, bias=bias))
                    bank_free[b] = m
                    v.wait(m)
                    src = raw[:, 4 + 2 * h:6 + 2 * h, :] if what else raw[:, h:h + 1, :]
                    dst = kT[:, h] if what else qT[:, h:h + 1, :]
                    cw = lambda w_, h=h, what=what: C("ml_conv_w", (4 * what + h) * MLC + w_)
                    v.step(lambda e, dst=dst, src=src, cw=cw: e.tensor_scalar(dst, src[:, :, 0:T], cw(0), None, ALU.mult))
                    for w_ in range(1, MLC):
                        m = v.step(lambda e, dst=dst, src=src, cw=cw, w_=w_: e.scalar_tensor_tensor(dst, src[:, :, w_:w_ + T], cw(w_), dst, ALU.mult, ALU.add))
                    a.wait(m)
                    m_c.append(a.do(lambda e, dst=dst, h=h, what=what: e.activation(dst, dst, ACT.Silu, bias=C("ml_conv_b", 4 * what + h))))
                stream.release(c[0], Mark(pe.counter, None, pe.counter.total))
                if not what:
                    g.wait(m_c)
                    m_q = g.do(lambda e: e.tensor_scalar(qT, qT, float(P) ** -0.5, None, ALU.mult))
            g.wait(m_cc, m_nm, m_Rd)
            m_one = g.do(lambda e: e.memset(va[:, :, :, MLV:MLV + 1], 1.0))
            a.wait(m_one)
            pe.wait(m_hp)
            m_vv = []
            for nb in range(2):
                c = column_chunk(w2, O_MV + nb * 512)
                pe.wait(c[1])
                for st in range(4):
                    b = next_bank()
                    if st < 2:
                        lh = lambda k, st=st: hT[:, k, T + st * P:T + (st + 1) * P]
                    else:
                        lh = lambda k, st=st: hp[:, k, (st - 2) * P:(st - 1) * P]
                    m = project_tokens(c, lh, 512, b, brow[0:1, 1024 + nb * 512:1024 + (nb + 1) * 512])
                    a.wait(m)
                    bank_free[b] = a.do(lambda e, st=st, b=b, nb=nb: e.activation(va[:, st, 2 * nb:2 * nb + 2, 0:MLV], banks[b].rearrange("p (h n) -> p h n", h=2), ACT.Copy))
                stream.release(c[0], m)
            m_va = bank_free[b]

            join()
            z.n = share
            ex = [z.take(4 * P) for _ in range(4)]
            hs = z.take(NT * D).rearrange("p (q h n) -> p q h n", q=NT, h=MLH)
            den = z.take(2 * 2 * NT * MLH).rearrange("p (n o) -> p n o", o=2)
            ybT = z.take(KD * T).rearrange("p (k t) -> p k t", k=KD)
            pe.wait(m_q, m_c, m_va, m_one)
            a.wait(m_cc, m_Rd)
            ex_read = [None] * 4
            n_u = 0
            for h in range(MLH):
                for qo in range(NT):
                    sb_ = 2 + n_u % 2
                    pe.wait(bank_free[sb_])

                    def mm(e, h=h, qo=qo, sb_=sb_):
                        for st in range(4):
                            r = e.matmul(banks[sb_][:, st * P:(st + 1) * P], kT[:, h, st // 2, (st % 2) * P:(st % 2 + 1) * P], qT[:, h, qo * P:(qo + 1) * P], start=True, stop=True)
                        return r
                    m_s = pe.do(mm)
                    for dr in range(2):
                        i4 = (2 * n_u + dr) % 4
                        eb = ex[i4]
                        lat = range(2, 3 + qo) if dr == FWD else range(2 + qo, 4)
                        row = 32 * dr + h
                        a.wait(ex_read[i4])
                        for st in [0, 1, *lat]:
                            src = (Rd if st == 2 + qo else Rb)[:, dr, h, qo * P:(qo + 1) * P]
                            m = a.do(lambda e, eb=eb, st=st, src=src, qo=qo, row=row: e.activation(eb[:, st * P:(st + 1) * P], src, ACT.Exp, bias=cc_[:, qo, st, row:row + 1]))
                        v.wait(m, m_s)
                        for lo, hi in ([(0, lat[-1] + 1)] if lat[0] == 2 else [(0, 2), (3, 4)]):
                            m = v.do(lambda e, eb=eb, lo=lo, hi=hi, sb_=sb_: e.tensor_tensor(eb[:, lo * P:hi * P], eb[:, lo * P:hi * P], banks[sb_][:, lo * P:hi * P], ALU.mult))
                        bank_free[sb_] = m
                        ob = 4 + i4
                        pe.wait(m, bank_free[ob])

                        def mm(e, eb=eb, lat=lat, h=h, ob=ob):
                            for st in [0, 1, *lat]:
                                r = e.matmul(banks[ob][:, 0:MLV + 1], eb[:, st * P:(st + 1) * P], va[:, st, h, :], start=(st == 0), stop=(st == lat[-1]))
                            return r
                        m = pe.do(mm)
                        ex_read[i4] = m
                        dn = den[:, 2 * n_u + dr, :]
                        a.wait(m)
                        m_abs = a.do(lambda e, dn=dn, ob=ob: e.activation(dn[:, 0:1], banks[ob][:, MLV:MLV + 1], ACT.Abs))
                        v.wait(m_abs, m_nm)
                        v.step(lambda e, dn=dn, qo=qo, row=row: e.tensor_scalar(dn[:, 0:1], dn[:, 0:1], nm[:, qo, row:row + 1], None, ALU.max))
                        v.step(lambda e, dn=dn: e.reciprocal(dn[:, 1:2], dn[:, 0:1]))
                        if dr == FWD:
                            m_hs = v.do(lambda e, dn=dn, ob=ob, qo=qo, h=h: e.tensor_scalar(hs[:, qo, h, :], banks[ob][:, 0:MLV], dn[:, 1:2], None, ALU.mult))
                        else:
                            v.wait(m_hs)
                            m_hs = v.do(lambda e, dn=dn, ob=ob, qo=qo, h=h: e.scalar_tensor_tensor(hs[:, qo, h, :], banks[ob][:, 0:MLV], dn[:, 1:2], hs[:, qo, h, :], ALU.mult, ALU.add))
                        bank_free[ob] = m_hs
                    n_u += 1
            hst = small[:, 424:432]
            a.wait(m_hs)
            for n in range(NT * MLH):
                junk = ex[n % 4][:, (n // 4) * T:(n // 4 + 1) * T]
                m = a.do(lambda e, n=n, junk=junk: e.activation(junk, hs[:, n // MLH, n % MLH, :], ACT.Square, accum_out=hst[:, n:n + 1]))
            rstd_of(hst, hst, 1.0 / MLV, m)
            for n in range(NT * MLH):
                m = v.do(lambda e, n=n: e.tensor_scalar(hs[:, n // MLH, n % MLH, :], hs[:, n // MLH, n % MLH, :], hst[:, n:n + 1], None, ALU.mult))
            pe.wait(m)
            hsf = hs.rearrange("p q h n -> p q (h n)")
            m_yb = [None, None]
            gts = [ex[2][:, 0:T], ex[3][:, 0:T]]
            for nb in range(2):
                c = column_chunk(w2, O_MG + nb * 512)
                pe.wait(c[1])
                for j in range(4):
                    k = nb * 4 + j
                    b = next_bank()
                    m = project(c, j, h_lat, T, b)
                    a.wait(m, m_yb[k % 2])
                    bank_free[b] = a.do(lambda e, k=k, b=b: e.activation(gts[k % 2], banks[b][:, 0:T], ACT.Sigmoid, bias=C("b_in", 56 + k)))
                    m_g = bank_free[b]
                    tb = 2 + k % 2
                    pe.wait(bank_free[tb])
                    for t in range(NT):
                        m2 = pe.do(lambda e, t=t, k=k, tb=tb: e.transpose(banks[tb][:, t * P:(t + 1) * P], hsf[:, t, k * P:(k + 1) * P], ident))
                    v.wait(m_g, m2)
                    v.step(lambda e, k=k, tb=tb: e.tensor_scalar(permuted(ybT[:, k, :]), banks[tb][:, 0:T].rearrange("p (c r) -> p c r", r=GRID_R), C("ml_norm_g", k), None, ALU.mult))
                    bank_free[tb] = Mark(v.counter, None, v.counter.total)
                    m_yb[k % 2] = v.do(lambda e, k=k: e.tensor_tensor(ybT[:, k, :], ybT[:, k, :], gts[k % 2], ALU.mult))
                stream.release(c[0], m)

            return ybT, share

        ybT, share = mlstm()

        join()
        z.n = keep_gla
        yT = z.take(KD * T).rearrange("p (k t) -> p k t", k=KD)
        sg_ = [z.take(T) for _ in range(2)]
        tg_ = [z.take(T) for _ in range(2)]
        assert z.n <= share
        m_y = {}
        n_s = [None, None]
        t_s = [None, None]
        for part, (og, wname, src_) in enumerate(((O_GA, "w_branch_a_2", yaT), (O_GB, "w_branch_b_2", ybT))):
            for nb in range(2):
                c1 = column_chunk(w2, og + nb * 512)
                c2 = column_chunk(d[wname][0], nb * 512)
                pe.wait(c1[1], c2[1])
                for j in range(4):
                    k = nb * 4 + j
                    b = next_bank()
                    m1 = project(c1, j, h_lat, T, b)
                    a.wait(m1, n_s[k % 2])
                    m = a.do(lambda e, k=k, b=b, og=og: e.activation(sg_[k % 2], banks[b][:, 0:T], ACT.Sigmoid, bias=C("b_in", 56 + (og - O_MG) // P + k)))
                    bank_free[b] = m
                    b2 = 2 + b
                    m2 = project(c2, j, lambda kk, src_=src_: src_[:, kk, :], T, b2)
                    v.wait(m, m2)
                    if part == 0:
                        m_y[k] = v.do(lambda e, k=k, b2=b2: e.tensor_tensor(yT[:, k, :], banks[b2][:, 0:T], sg_[k % 2], ALU.mult))
                        n_s[k % 2] = bank_free[b2] = m_y[k]
                    else:
                        v.wait(t_s[k % 2])
                        m3 = v.step(lambda e, k=k, b2=b2: e.tensor_tensor(tg_[k % 2], banks[b2][:, 0:T], sg_[k % 2], ALU.mult))
                        n_s[k % 2] = bank_free[b2] = m3
                        v.wait(m_y[k])
                        m_y[k] = v.do(lambda e, k=k: e.tensor_tensor(yT[:, k, :], yT[:, k, :], tg_[k % 2], ALU.add))
                        t_s[k % 2] = m_y[k]
                stream.release(c1[0], m1)
                stream.release(c2[0], m2)

        def row_of(col0, dst, pair_):
            pe.wait([bank_free[b] for b in pair_])

            def mm(e):
                for k in range(KD):
                    r = e.matmul(banks[pair_[k // 4]][:, (k % 4) * P:(k % 4 + 1) * P], mcol[:, col0 + k, 0:1].to_broadcast([P, P]), ident, start=True, stop=True)
                return r
            m = pe.do(mm)
            a.wait(m)
            for n, b in enumerate(pair_):
                bank_free[b] = a.do(lambda e, n=n, b=b: e.activation(dst[:, n * 512:(n + 1) * 512], banks[b], ACT.Copy))
            return bank_free[pair_[1]]
        g1 = z.take(D)
        mt = [z.take(512) for _ in range(2)]
        m_g1 = row_of(16, g1, (4, 5))

        pe.wait([m_y[k] for k in range(KD)])
        v.wait(m_g1)
        m_t = [None, None]
        n_ = 0
        for nb in range(2):
            c = column_chunk(d["w_out_2"][0], nb * 512)
            pe.wait(c[1])
            for t in range(NT):
                b = 2 * nb + t
                m = project_tokens(c, lambda k, t=t: yT[:, k, t * P:(t + 1) * P], 512, b)
                v.wait(m, m_t[n_ % 2])
                v.step(lambda e, n_=n_, b=b, nb=nb: e.tensor_tensor(mt[n_ % 2], banks[b], g1[:, nb * 512:(nb + 1) * 512], ALU.mult))
                xs = x[:, t * D + nb * 512:t * D + (nb + 1) * 512]
                m_t[n_ % 2] = v.do(lambda e, n_=n_, xs=xs: e.tensor_tensor(xs, xs, mt[n_ % 2], ALU.add))
                bank_free[b] = m_t[n_ % 2]
                n_ += 1
            stream.release(c[0], m)
        join()
        acc = zone[:, zone.shape[1] - NT * D:]
        m = g.do(lambda e: e.memset(acc, 0.0))
        v.wait(m)
        moe("moe2", E2, F2, w_route[1], R("r2_b"), d["w_gate_2"][0], d["w_up_2"][0], d["w_down_2"][0],
            lambda k: scl2[:, k:k + 1], lambda k: mcol[:, 24 + k, 0:1], acc, [])
        join()
        for i_ in range(8):
            bank_free[i_] = None
        z = Zone()
        g2 = z.take(D)
        on = z.take(NT * D)
        m = row_of(40, g2, (0, 1))
        v.wait(m)
        for t in range(NT):
            ts_ = slice(t * D, (t + 1) * D)
            v.step(lambda e, ts_=ts_: e.tensor_tensor(acc[:, ts_], acc[:, ts_], g2, ALU.mult))
            m = v.step(lambda e, ts_=ts_: e.tensor_tensor(x[:, ts_], x[:, ts_], acc[:, ts_], ALU.add))
        m_n = norm_tokens(x, on, small[:, 0:8], m)
        for t in range(NT):
            v.wait(m_n[t])
            m = v.do(lambda e, t=t: e.tensor_tensor(on[:, t * D:(t + 1) * D], on[:, t * D:(t + 1) * D], R("final_g"), ALU.mult))
            s.wait(m)
            m = s.do(lambda e, t=t: e.dma_start(y_out[0, t * P:(t + 1) * P, :], on[:, t * D:(t + 1) * D]), out_done, 16)
        s.wait(m)
        emit(prog, nc, ctx)


def emit(prog, nc, ctx):
    block = ctx.enter_context(nc.Block())
    block.sync(lambda e: prog.s.run(e))
    block.tensor(lambda e: prog.pe.run(e))
    block.vector(lambda e: prog.v.run(e))
    block.scalar(lambda e: prog.a.run(e))
    block.gpsimd(lambda e: prog.g.run(e))


def pack_cols(i):
    def tiles(vec):
        return np.reshape(vec, (-1, P)).T

    f = np.float32
    p = np.arange(P)
    t = np.arange(T)
    dist = (p[:, None] + P) - t[None, :]
    slopes = [(2.0 ** (-8.0 / HA)) ** (h + 1) for h in range(HA)]
    count = np.stack([np.minimum(t + 1, w) for w in WINDOWS])
    inv = np.concatenate([np.repeat(1.0 / count[2 * j:2 * j + 2], 64, axis=0) for j in range(2)], axis=1)
    b_in = i["b_in_2"][0]
    b_if = np.zeros((P, 1), f)
    for n in range(4):
        b_if[32 * n:32 * n + 4, 0] = b_in[O_IF + 4 * n:O_IF + 4 * n + 4]
    parts = {
        "ident": np.eye(P), "ones": np.ones((P, P)), "ones64": np.kron(np.eye(2), np.ones((64, 64))),
        "before": np.triu(np.ones((P, P)), 1), "iota": np.tile(p, (P, 1)), "iota8": np.tile(np.arange(8), (P, 1)),
        "alibi": np.concatenate([np.where(dist >= 0, -sl * dist, NEG) for sl in slopes], axis=1),
        "inv_count": inv, "mask_f": np.where(p[:, None] <= p[None, :], 0.0, NEG),
        "mask_b": np.where(p[:, None] >= p[None, :], 0.0, NEG),
        "attn_norm_g": tiles(i["attn_norm_g"]), "ffn_norm_g": tiles(i["ffn_norm_g"]),
        "norm1_g": tiles(i["norm1_g_2"]), "norm2_g": tiles(i["norm2_g_2"]),
        "conv_w": np.concatenate([i["conv_w"][0][:, j * P:(j + 1) * P].T for j in range(2)], axis=1),
        "conv_b": tiles(i["conv_b"]), "conv_ln_g": tiles(i["conv_ln_g"]), "conv_ln_b": tiles(i["conv_ln_b"]),
        "conv_pw_b": tiles(i["conv_pw_b"]), "pool_scale": tiles(i["pool_scale"]),
        "q_norm_g": np.tile(i["q_norm_g"][0], 2)[:, None], "k_norm_g": np.tile(i["k_norm_g"][0], 2)[:, None],
        "attn_sub_norm_g": tiles(i["attn_sub_norm_g"]),
        "lb": np.reshape(i["hg_lb_logits_2"], (32, P)).T,
        "hg_norm_g": tiles(i["hg_norm_g_2"]), "ml_norm_g": tiles(i["ml_norm_g_2"]),
        "ml_conv_w": np.concatenate([i["ml_conv_w_2"][0][:, j * P:(j + 1) * P].T for j in range(8)], axis=1),
        "ml_conv_b": tiles(i["ml_conv_b_2"]),
        "b_in": np.concatenate([tiles(b_in[0:O_IF]), tiles(b_in[O_MG:])], axis=1), "b_if": b_if,
        "b_ada": tiles(i["b_ada_2"]), "c": tiles(i["c_2"]), "c_ctx": tiles(i["c_ctx_2"]),
    }
    for name, (_, w) in COLS.at.items():
        assert parts[name].shape == (P, w), (name, parts[name].shape)
    return np.concatenate([np.asarray(parts[name], f) for name in COLS.at], axis=1)


def pack_rows(i):
    parts = [i["router_g_b"][0], i["router_e_b"][0], i["b_group_2"][0], i["b_router_2"][0],
             i["lambda_q1"][0], i["lambda_k1"][0], i["lambda_q2"][0], i["lambda_k2"][0], i["final_norm_g_2"]]
    return np.concatenate(parts)[None, :]


def level_masks():
    p = np.arange(P)
    out = [np.eye(P)]
    for m in LEVELS:
        same = (p[:, None] // (2 * m)) == (p[None, :] // (2 * m))
        out.append(same & ((p[:, None] // m) % 2 == 0) & ((p[None, :] // m) % 2 == 1))
    out += [m.T for m in out[1:]]
    return np.concatenate([m.astype(np.float32) for m in out], axis=1)


def row_picks():
    out = np.zeros((36, 8, P), np.float32)
    for n in range(8):
        out[32 * (n // 4) + n % 4, n] = 1.0
    return out.reshape(36, 8 * P)


WEIGHTS = ["x", "w_in", "conv_pw_w", "pool_w", "w_out", "router_g_w", "router_e_w", "w_gate", "w_up", "w_down",
           "ctx_2", "w_ada_2", "w_in_2", "b_in_2", "w_branch_a_2", "w_branch_b_2", "w_out_2", "w_group_2", "w_router_2",
           "w_gate_2", "w_up_2", "w_down_2"]


def program(nc, arrays):
    d = {n: nc.dram_tensor(n + "_dram", a.shape, mybir.dt.from_np(a.dtype), kind="ExternalInput").ap() for n, a in arrays.items()}
    out = nc.dram_tensor("out_dram", (1, T, D), F32, kind="ExternalOutput").ap()
    with nc.allow_non_contiguous_dma(reason="short rows of small parameters"):
        build(nc, d, out)


def arrays_of(inputs):
    i = {n: np.asarray(a) for n, a in inputs.items()}
    arrays = {n: np.ascontiguousarray(i[n]) for n in WEIGHTS}
    arrays |= {"cols": pack_cols(i), "rows": pack_rows(i), "masks": level_masks(), "pick": row_picks()}
    return arrays


def kernel(**inputs):
    import concourse.bacc as bacc
    from concourse.bass_utils import run_bass_kernel_spmd

    nc = bacc.Bacc("TRN2", target_bir_lowering=False, num_devices=1)
    arrays = arrays_of(inputs)
    program(nc, arrays)
    r = run_bass_kernel_spmd(nc, [{n + "_dram": a for n, a in arrays.items()}], core_ids=[0])
    return r.results[0]["out_dram"]
```

```python
import math
from contextlib import ExitStack

import numpy as np

import concourse.bass as bass
from concourse import mybir
from concourse.alu_op_type import AluOpType as ALU

F32 = mybir.dt.float32
I32 = mybir.dt.int32
U8 = mybir.dt.uint8
ACT = mybir.ActivationFunctionType
AX = mybir.AxisListType.X

P = 128
D = 1024
KD = D // P
T = 256
NT = T // P
EPS = 1e-6
C_CONV, CONV_W = 256, 31
WINDOWS = (2, 4, 8, 16)
PADP = max(WINDOWS)
HA, DH = 4, 64
LAM_INIT = 0.8 - 0.6 * math.exp(0.0)
GRID_W = 64
GRID_R = T // GRID_W
HG = 8
HB = 4
MLH, MLV = 4, 256
MLC = 5
LEVELS = [1 << n for n in range(7)]
FWD, BWD = 0, 1
LAT, CTX = 0, 1
NG = 4
E1, F1 = 4, 256
E2, F2 = 8, 512
BIG = 1e6
NEG = -1e30


RING = 4
RING_MOE = 8
SLOTS = 64
PAIRS = 4
SLOT = KD * 512

O_Q, O_FF, O_FB, O_HI, O_HG = 0, 1024, 2048, 3072, 4096
O_MQ, O_MK, O_MV, O_IF = 5120, 5632, 6144, 7168
O_MG, O_GA, O_GB = 7184, 8208, 9232


class Layout:

    def __init__(self):
        self.at, self.n = {}, 0

    def add(self, name, width):
        self.at[name] = (self.n, width)
        self.n += width


def cols_layout():
    lay = Layout()
    for name, width in [
        ("ident", P), ("ones", P), ("ones64", P), ("before", P), ("iota", P), ("iota8", 8),
        ("alibi", HA * T), ("inv_count", 2 * T), ("mask_f", P), ("mask_b", P),
        ("attn_norm_g", 8), ("ffn_norm_g", 8), ("norm1_g", 8), ("norm2_g", 8),
        ("conv_w", 2 * CONV_W), ("conv_b", 2), ("conv_ln_g", 2), ("conv_ln_b", 2), ("conv_pw_b", 2),
        ("pool_scale", 2), ("q_norm_g", 1), ("k_norm_g", 1), ("attn_sub_norm_g", 1),
        ("lb", 32), ("hg_norm_g", 8), ("ml_norm_g", 8), ("ml_conv_w", 8 * MLC), ("ml_conv_b", 8),
        ("b_in", 80), ("b_if", 1), ("b_ada", 48), ("c", 8), ("c_ctx", 8),
    ]:
        lay.add(name, width)
    return lay


def rows_layout():
    lay = Layout()
    for name, width in [("r1_b", NG + NG * E1), ("r2_b", NG + NG * E2), ("lambdas", 4 * DH), ("final_g", D)]:
        lay.add(name, width)
    return lay


COLS, ROWS = cols_layout(), rows_layout()


class Counter:

    def __init__(self, sem):
        self.sem, self.total, self.rel, self.loop = sem, 0, 0, None

    def bump(self, n):
        if self.loop is None:
            self.total += n
            return Mark(self, None, self.total)
        self.rel += n
        return Mark(self, self.loop, self.rel)


class Loop:

    def __init__(self, turns):
        self.turns, self.base, self.per = turns, {}, {}


class Mark:

    def __init__(self, counter, loop, k, back=0):
        self.counter, self.loop, self.k, self.back = counter, loop, k, back

    def last_turn(self):
        return Mark(self.counter, self.loop, self.k, 1)

    def value(self, loop, i):
        if self.loop is None:
            return self.k
        base, per = self.loop.base[self.counter], self.loop.per[self.counter]
        if self.loop is not loop:
            return base + (self.loop.turns - 1) * per + self.k
        least = base + self.k - self.back * per
        assert least > 0
        return i * per + least


class Later:

    def set(self, mark):
        self.mark, self.counter = mark, mark.counter
        return mark

    def value(self, loop, i):
        return self.mark.last_turn().value(loop, i)


class Later2:

    def set(self, mark):
        self.mark, self.counter = mark, mark.counter
        return mark

    def value(self, loop, i):
        return self.mark.value(loop, i)


class Queue:

    def __init__(self, prog, sem):
        self.prog, self.counter, self.items = prog, Counter(sem), []
        self.tail, self.ahead_part = [], False

    def do(self, fn, counter=None, n=1):
        c = counter or self.counter
        mark = c.bump(n)
        if self.ahead_part:
            self.prog.skipped[c] = self.prog.skipped.get(c, 0) + n
        self.put(lambda e, lp, i: (fn(e, i) if lp else fn(e)).then_inc(c.sem, n))
        return mark

    def put(self, item):
        self.items.append(item)
        if not self.ahead_part:
            self.tail.append(item)

    def step(self, fn):
        m = self.do(fn)
        self.wait(m)
        return m

    def wait(self, *marks):
        for m in marks:
            if m is None:
                continue
            if isinstance(m, (list, tuple)):
                self.wait(*m)
                continue
            self.put(lambda e, lp, i, m=m: e.wait_ge(m.counter.sem, m.value(lp, i)))

    def run(self, e, items=None):
        for item in self.items if items is None else items:
            if isinstance(item, tuple):
                loop, body, tail = item
                with e.Fori(0, loop.turns - (tail is not None)) as i:
                    for f in body:
                        f(e, loop, i)
                for f in tail or ():
                    f(e, loop, loop.turns - 1)
            elif isinstance(item, Branch):
                n = e.value_load(item.number, min_val=0, max_val=item.most)
                with e.If(n > item.above):
                    self.run(e, item.items[self])
            else:
                item(e, None, None)


class Branch:

    def __init__(self, number, most, above):
        self.number, self.most, self.above, self.items = number, most, above, {}


class Program:
    def __init__(self, nc, ctx):
        self.nc, self.ctx = nc, ctx
        self.pe, self.v, self.a, self.g, self.s = (
            Queue(self, self.sem(n)) for n in ("pe_done", "vector_done", "scalar_done", "gpsimd_done", "sync_done"))
        self.queues = [self.pe, self.v, self.a, self.g, self.s]
        self.counters = [q.counter for q in self.queues]

    def sem(self, name):
        return self.ctx.enter_context(self.nc.semaphore(name))

    def new_counter(self, name):
        c = Counter(self.sem(name))
        self.counters.append(c)
        return c

    def loop(self, turns, body):
        lp = Loop(turns)
        self.skipped = {}
        saved = [q.items for q in self.queues]
        for q in self.queues:
            q.items, q.tail = [], []
        for c in self.counters:
            lp.base[c], c.loop, c.rel = c.total, lp, 0
        body()
        for c in self.counters:
            lp.per[c] = c.rel
            c.total += turns * c.rel - self.skipped.get(c, 0)
            c.loop = None
        for q, before in zip(self.queues, saved):
            q.ahead_part = False
            if q.items:
                before.append((lp, q.items, q.tail if q is self.s else None))
            q.items, q.tail = before, []


    def branch(self, number, most, above, name, body):
        br = Branch(number, most, above)
        saved = [(q.items, q.counter) for q in self.queues]
        before = [Mark(q.counter, None, q.counter.total) for q in self.queues if q.counter.total]
        for q in self.queues:
            q.items, q.counter = [], self.new_counter(f"{name}_{q.counter.sem.name}")
            q.wait([m for m in before if m.counter is not dict(zip(self.queues, saved))[q][1]])
            q.put(lambda e, lp, i, c=q.counter: e.sem_inc(c.sem, 1))
            q.counter.total = 1
        body()
        after = [Mark(q.counter, None, q.counter.total) for q in self.queues]
        for q, (items, counter) in zip(self.queues, saved):
            q.wait([m for m in after if m.counter is not q.counter])
            br.items[q] = q.items
            q.items, q.counter = items + [br], counter


def build(nc, d, y_out):
    ctx = ExitStack()
    with ctx:
        prog = Program(nc, ctx)
        pe, v, a, g, s = prog.pe, prog.v, prog.a, prog.g, prog.s

        def sb(name, width, dt=F32):
            return ctx.enter_context(nc.sbuf_tensor(name, [P, width], dt))[:, :]

        banks = [ctx.enter_context(nc.psum_tensor(f"bank{i}", [P, 512], F32))[:, :] for i in range(8)]

        cols = sb("cols", COLS.n)
        rows = sb("rows", ROWS.n)
        level_mask = sb("level_mask", 15 * P, U8)
        pick_row = sb("pick_row", 8 * P)
        x = sb("x", NT * D)
        small = sb("small", 512)
        group_most = sb("group_most", 4)
        w_route = [sb("w_route1", KD * (NG + NG * E1)), sb("w_route2", KD * (NG + NG * E2))]
        zone = sb("zone", 53000 - RING * SLOT - COLS.n - ROWS.n - 480 - 8 * P - NT * D - 512 - KD * (2 * NG + NG * (E1 + E2)) - 64)
        ring = [sb(f"ring{i}", SLOT) for i in range(RING)]
        slot_in = [prog.new_counter(f"slot_in{i}") for i in range(RING_MOE)]
        params_in = prog.new_counter("params_in")
        mask_in = prog.new_counter("mask_in")
        x_in = prog.new_counter("x_in")
        out_done = prog.new_counter("out_done")

        def C(name, i=0, n=1):
            o, _ = COLS.at[name]
            return cols[:, o + i:o + i + n]

        def Call(name):
            o, w = COLS.at[name]
            return cols[:, o:o + w]

        def R(name):
            o, w = ROWS.at[name]
            return rows[:, o:o + w]

        ident, ones = Call("ident"), Call("ones")

        class Zone:

            def __init__(self):
                self.n = 0

            def take(self, width):
                o = self.n
                self.n += width
                assert self.n <= zone.shape[1], (self.n, zone.shape)
                return zone[:, o:o + width]

        def join():
            marks = [Mark(q.counter, None, q.counter.total) for q in (pe, v, a, g) if q.counter.total]
            for q in (pe, v, a, g):
                q.wait([m for m in marks if m.counter is not q.counter])
            return marks

        class Stream:
            def __init__(self):
                self.n = 0
                self.released = [None] * RING
                self.slot_in = slot_in

            def load(self, *parts):
                k = self.n % RING
                self.n += 1
                s.wait(self.released[k])
                for dst, src in parts:
                    m = s.do(lambda e, dst=dst, src=src: e.dma_start(dst(ring[k]), src), self.slot_in[k], 16)
                return k, m

            def release(self, k, mark):
                self.released[k] = mark

        stream = Stream()

        def as_k(n, k=KD):
            return lambda slot: slot[:, 0:k * n].rearrange("p (k n) -> p k n", k=k)

        early = {}

        def column_chunk(w, c0, n=512):
            if (id(w), c0) in early:
                return early.pop((id(w), c0))
            k, m = stream.load((as_k(n), w[:, c0:c0 + n].rearrange("(k p) n -> p k n", p=P)))
            return k, m, as_k(n)(ring[k])

        s.do(lambda e: e.dma_start(x.rearrange("p (t n) -> p t n", t=NT), d["x"][0].rearrange("(t p) n -> p t n", p=P)), x_in, 16)
        m_x = s.do(lambda e: e.dma_start(cols, d["cols"]), x_in, 16)
        z = Zone()
        xn = z.take(NT * D)
        hT = z.take(KD * T)
        wp1 = z.take(2 * C_CONV).rearrange("p (k n) -> p k n", k=2)
        wpool = z.take(2 * P).rearrange("p (t n) -> p t n", t=2)
        chunk0 = [column_chunk(d["w_in"][0], 0), column_chunk(d["w_in"][0], 512)]
        m_zero = [g.do(lambda e: e.memset(wpool, 0.0))]
        s.do(lambda e: e.dma_start(rows, d["rows"].broadcast_to([P, ROWS.n])), params_in, 16)
        mask_f32 = zone[:, zone.shape[1] - 15 * P:]
        m_mask = s.do(lambda e: e.dma_start(mask_f32, d["masks"]), mask_in, 16)
        s.do(lambda e: e.dma_start(pick_row[0:36, :], d["pick"]), params_in, 16)
        s.do(lambda e: e.dma_start(wp1, d["conv_pw_w"][0].rearrange("(k p) n -> p k n", p=P)), params_in, 16)
        for w_r, names, ne in ((w_route[0], ("router_g_w", "router_e_w"), E1), (w_route[1], ("w_group_2", "w_router_2"), E2)):
            wv = w_r.rearrange("p (k n) -> p k n", k=KD)
            for nm, lo, hi in ((names[0], 0, NG), (names[1], NG, NG + NG * ne)):
                s.do(lambda e, nm=nm, wv=wv, lo=lo, hi=hi: e.dma_start(wv[:, :, lo:hi], d[nm][0].rearrange("(k p) n -> p k n", p=P)), params_in, 16)
        s.wait(m_zero)
        for gi in range(4):
            o = 64 * (gi % 2)
            m_params = s.do(lambda e, gi=gi, o=o: e.dma_start(wpool[o:o + 64, gi // 2, o:o + 64], d["pool_w"][0, gi]), params_in, 16)
        chunk0 += [column_chunk(d["w_in"][0], 1024), column_chunk(d["w_in"][0], 1536, 256)]

        for q in (v, a, pe, g):
            q.wait(m_x)
        g.wait(m_mask)
        m_mask8 = g.do(lambda e: e.tensor_copy(level_mask, mask_f32))

        def rstd_of(src, dst, scale, after=()):
            v.wait(after)
            m = v.do(lambda e: e.tensor_scalar(dst, src, scale, EPS, ALU.mult, ALU.add))
            a.wait(m)
            m = a.do(lambda e: e.activation(dst, dst, ACT.Sqrt))
            v.wait(m)
            return v.step(lambda e: e.reciprocal(dst, dst))

        def norm_tokens(src, dst, stat, after=()):
            a.wait(after)
            for t in range(NT):
                m = a.do(lambda e, t=t: e.activation(dst[:, t * D:(t + 1) * D], src[:, t * D:(t + 1) * D], ACT.Square, accum_out=stat[:, t:t + 1]))
            rstd_of(stat[:, 0:NT], stat[:, 0:NT], 1.0 / D, m)
            out = []
            for t in range(NT):
                out.append(v.do(lambda e, t=t: e.tensor_scalar(dst[:, t * D:(t + 1) * D], src[:, t * D:(t + 1) * D], stat[:, t:t + 1], None, ALU.mult)))
            return out

        def to_channels(src, dst, scale, shift, after, free):
            pe.wait(after)
            out = []
            free = list(free)
            for k in range(KD):
                b = banks[6 + k % 2]
                pe.wait(free[k % 2])
                for t in range(NT):
                    fn = lambda e, k=k, t=t, b=b: e.transpose(b[:, t * P:(t + 1) * P], src[:, t * D + k * P:t * D + (k + 1) * P], ident)
                    m = pe.do(fn)
                q = v if k % 2 == 0 else a
                q.wait(m)
                if q is v:
                    sh = None if shift is None else shift(k)
                    m = v.do(lambda e, k=k, b=b, sh=sh: e.tensor_scalar(dst(k), b[:, 0:T], scale(k), sh, ALU.mult, *([] if sh is None else [ALU.add])))
                else:
                    sh = 0.0 if shift is None else shift(k)
                    m = a.do(lambda e, k=k, b=b, sh=sh: e.activation(dst(k), b[:, 0:T], ACT.Identity, bias=sh, scale=scale(k)))
                free[k % 2] = m
                out.append(m)
            return out

        bank_free = [None] * 8

        turn = [0]

        def next_bank():
            turn[0] += 1
            return turn[0] % 2

        def project(chunk, j, rhs, n, b):
            pe.wait(bank_free[b])
            w = chunk[2]

            def fn(e):
                for k in range(KD):
                    m = e.matmul(banks[b][:, 0:n], w[:, k, j * P:(j + 1) * P], rhs(k), start=(k == 0), stop=(k == KD - 1))
                return m
            return pe.do(fn)

        def project_tokens(chunk, lhsT, n, b, bias=None, c0=0):
            pe.wait(bank_free[b])
            w = chunk[2]

            def fn(e):
                for k in range(KD):
                    m = e.matmul(banks[b][:, 0:n], lhsT(k), w[:, k, c0:c0 + n], start=(k == 0), stop=(k == KD - 1 and bias is None))
                if bias is not None:
                    m = e.matmul(banks[b][:, 0:n], ones[0:1, :], bias, start=False, stop=True)
                return m
            return pe.do(fn)

        def first_block():
            stat = small[:, 0:8]
            m_xn = norm_tokens(x, xn, stat)
            hTk = hT.rearrange("p (k t) -> p k t", k=KD)
            m_h = to_channels(xn, lambda k: hTk[:, k, :], lambda k: C("attn_norm_g", k), None, m_xn, [None, None])
            bank_free[6], bank_free[7] = m_h[-2], m_h[-1]
            h_rhs = lambda k: hTk[:, k, :]

            gate = z.take(2 * T).rearrange("p (j t) -> p j t", j=2)
            U = T + CONV_W - 1
            u = z.take(2 * U).rearrange("p (j t) -> p j t", j=2)
            pin = z.take(2 * (T + PADP)).rearrange("p (j t) -> p j t", j=2)
            qk = z.take(8 * T).rearrange("p (j t) -> p j t", j=8)
            vv = z.take(NT * 512).rearrange("p (t n) -> p t n", t=NT)
            m_pad = g.do(lambda e: e.memset(u[:, :, 0:CONV_W - 1], 0.0))
            m_pad = g.do(lambda e: e.memset(pin[:, :, 0:PADP], 0.0))
            pe.wait(m_h)

            c = chunk0[0]
            pe.wait(c[1])
            m_gate = []
            for j in (2, 3):
                b = next_bank()
                m = project(c, j, h_rhs, T, b)
                a.wait(m)
                bank_free[b] = a.do(lambda e, j=j, b=b: e.activation(gate[:, j - 2, :], banks[b][:, 0:T], ACT.Sigmoid))
                m_gate.append(bank_free[b])
            for j in (0, 1):
                b = next_bank()
                m = project(c, j, h_rhs, T, b)
                v.wait(m, m_gate[j])
                bank_free[b] = v.do(lambda e, j=j, b=b: e.tensor_tensor(u[:, j, CONV_W - 1:U], banks[b][:, 0:T], gate[:, j, :], ALU.mult))
            m_u = bank_free[b]
            stream.release(c[0], m)
            c = chunk0[1]
            pe.wait(c[1])
            m_qk = []
            for j in range(4):
                b = next_bank()
                m = project(c, j, h_rhs, T, b)
                dst = pin[:, j, PADP:] if j < 2 else qk[:, j - 2, :]
                a.wait(m)
                bank_free[b] = a.do(lambda e, dst=dst, b=b: e.activation(dst, banks[b][:, 0:T], ACT.Copy))
                if j == 1:
                    m_pin = bank_free[b]
            stream.release(c[0], m)
            jq = 2
            c_v = column_chunk(d["w_in"][0], 1792)
            for c, nj in ((chunk0[2], 4), (chunk0[3], 2)):
                pe.wait(c[1])
                for j in range(nj):
                    b = next_bank()
                    m = project(c, j, h_rhs, T, b)
                    a.wait(m)
                    bank_free[b] = a.do(lambda e, jq=jq, b=b: e.activation(qk[:, jq, :], banks[b][:, 0:T], ACT.Copy))
                    jq += 1
                stream.release(c[0], m)
            m_qk = bank_free[b]
            pe.wait(c_v[1])
            for t in range(NT):
                b = next_bank()
                m = project_tokens(c_v, lambda k, t=t: hTk[:, k, t * P:(t + 1) * P], 512, b)
                a.wait(m)
                bank_free[b] = a.do(lambda e, t=t, b=b: e.activation(vv[:, t, :], banks[b], ACT.Copy))
            m_vv = bank_free[b]
            stream.release(c_v[0], m)

            ada = z.take(3 * D)
            cc = small[:, 8:24].rearrange("p (k c) -> p k c", k=KD)
            m = a.do(lambda e: e.activation(cc[:, :, 0], Call("c"), ACT.Silu))
            m_cc = a.do(lambda e: e.activation(cc[:, :, 1], Call("c_ctx"), ACT.Silu))
            n_ada = 6 * D // 1024
            ada_chunks = {n: column_chunk(d["w_ada_2"][0], n * 512) for n in range(4)}

            def ada_step(n):
                if n >= n_ada:
                    return None
                two = [ada_chunks[2 * n + c] for c in range(2)]
                pe.wait(m_cc, [c[1] for c in two], bank_free[5])

                def mm(e):
                    for kk in range(KD):
                        for c in range(2):
                            r = e.matmul(banks[5][32 * c:32 * c + 2, :], cc[:, kk, :], two[c][2][:, kk, :], start=(kk == 0), stop=(kk == KD - 1), tile_position=(0, 32 * c))
                    return r
                m = pe.do(mm)
                for c in two:
                    stream.release(c[0], m)
                if n + 2 < n_ada:
                    for c in range(2):
                        ada_chunks[2 * n + 4 + c] = column_chunk(d["w_ada_2"][0], (2 * n + 4 + c) * 512)
                a.wait(m)
                for c in range(2):
                    bank_free[5] = a.do(lambda e, c=c: e.activation(ada[32 * c:32 * c + 2, n * 512:(n + 1) * 512], banks[5][32 * c:32 * c + 2, :], ACT.Copy))
                return bank_free[5]

            yc = z.take(2 * T).rearrange("p (j t) -> p j t", j=2)
            v.wait(m_pad, m_u)
            m_y = [v.do(lambda e, j=j: e.tensor_scalar(yc[:, j, :], u[:, j, 0:T], C("conv_w", j * CONV_W), C("conv_b", j), ALU.mult, ALU.add)) for j in range(2)]
            for w in range(1, CONV_W):
                for j in range(2):
                    v.wait(m_y[j])
                    m_y[j] = v.do(lambda e, j=j, w=w: e.scalar_tensor_tensor(yc[:, j, :], u[:, j, w:w + T], C("conv_w", j * CONV_W + w), yc[:, j, :], ALU.mult, ALU.add))

            sums = [z.take(2 * (T + PADP)).rearrange("p (j t) -> p j t", j=2) for _ in range(2)]
            dd = z.take(2 * T).rearrange("p (j t) -> p j t", j=2)
            inv = Call("inv_count").rearrange("p (j t) -> p j t", j=2)
            v.wait(m_pin)
            end = T + PADP
            src = pin
            for n, win in enumerate(WINDOWS):
                dst = sums[n % 2]
                h_ = win // 2
                v.step(lambda e, src=src, dst=dst, win=win, h_=h_: e.tensor_tensor(dst[:, :, win:end], src[:, :, win:end], src[:, :, win - h_:end - h_], ALU.add))
                o, j = 64 * (n % 2), n // 2
                v.do(lambda e, dst=dst, o=o, j=j: e.tensor_tensor(dd[o:o + 64, j, :], dst[o:o + 64, j, PADP:end], inv[o:o + 64, j, :], ALU.mult))
                src = dst
            v.wait(Mark(v.counter, None, v.counter.total))
            m_dd = v.do(lambda e: e.tensor_tensor(dd, dd, pin[:, :, PADP:end], ALU.subtract))

            sq = z.take(8 * T).rearrange("p (j t) -> p j t", j=8)
            sqf = sq.rearrange("p j t -> p (j t)")
            qkf = qk.rearrange("p j t -> p (j t)")
            qg = small[:, 24:25]
            v.do(lambda e: e.tensor_scalar(qg, C("q_norm_g"), DH ** -0.5, None, ALU.mult))
            a.wait(m_qk)
            m_sq = a.do(lambda e: e.activation(sq, qk, ACT.Square))
            pe.wait(m_sq)
            m_ms, ms_bank = [], [2, 3, 4, 1]
            for n in range(4):
                pe.wait(bank_free[ms_bank[n]])
                m_ms.append(pe.do(lambda e, n=n: e.matmul(banks[ms_bank[n]], Call("ones64"), sqf[:, n * 512:(n + 1) * 512], start=True, stop=True)))
            ada_step(0)
            for n in range(4):
                v.wait(m_ms[n])
                m = v.do(lambda e, n=n: e.tensor_scalar(sqf[:, n * 512:(n + 1) * 512], banks[ms_bank[n]], 1.0 / DH, EPS, ALU.mult, ALU.add))
                bank_free[ms_bank[n]] = m
            a.wait(m)
            m = a.do(lambda e: e.activation(sq, sq, ACT.Sqrt))
            v.wait(m)
            v.step(lambda e: e.reciprocal(sqf, sqf))
            v.do(lambda e: e.scalar_tensor_tensor(qkf[:, 0:4 * T], qkf[:, 0:4 * T], qg, sqf[:, 0:4 * T], ALU.mult, ALU.mult))
            m_qkn = v.do(lambda e: e.scalar_tensor_tensor(qkf[:, 4 * T:], qkf[:, 4 * T:], C("k_norm_g"), sqf[:, 4 * T:], ALU.mult, ALU.mult))

            v.wait(m_params)
            lmb = R("lambdas").rearrange("p (n d) -> p n d", n=4)
            lm = small[:, 32:160].rearrange("p (n d) -> p n d", n=2)
            ls, nlam, sg = small[:, 26:28], small[:, 28:29], small[:, 29:30]
            v.step(lambda e: e.tensor_tensor(lm, lmb[:, 0:4:2, :], lmb[:, 1:4:2, :], ALU.mult))
            m = v.step(lambda e: e.tensor_reduce(ls, lm, AX, ALU.add))
            a.wait(m)
            m = a.do(lambda e: e.activation(ls, ls, ACT.Exp))
            v.wait(m)
            v.step(lambda e: e.tensor_tensor(nlam, ls[:, 1:2], ls[:, 0:1], ALU.subtract))
            v.step(lambda e: e.tensor_scalar(nlam, nlam, -LAM_INIT, None, ALU.add))
            v.do(lambda e: e.tensor_scalar(sg, C("attn_sub_norm_g"), 1.0 - LAM_INIT, None, ALU.mult))

            mixT = z.take(KD * T).rearrange("p (k t) -> p k t", k=KD)
            sc = [z.take(2 * T).rearrange("p (m k) -> p m k", m=2) for _ in range(2)]
            aT = [z.take(T) for _ in range(2)]
            st = small[:, 160:256].rearrange("p (u n) -> p u n", u=8)
            ali = Call("alibi").rearrange("p (h k) -> p h k", h=HA)
            pe.wait(m_qkn, m_vv)
            sc_free = [None, None]
            o_marks = {}
            exp_done = {}
            units = [(h, blk) for h in range(HA) for blk in range(NT)]

            def scores(n):
                h, blk = units[n]
                nk = (blk + 1) * P
                b = 2 * (n % 2)
                pe.wait(bank_free[b], bank_free[b + 1])

                def mm(e):
                    for mp in range(2):
                        o = 64 * mp
                        r = e.matmul(banks[b + mp][:, 0:nk], qk[o:o + 64, h, blk * P:(blk + 1) * P], qk[o:o + 64, 4 + h, 0:nk], start=True, stop=True)
                    return r
                m = pe.do(mm)
                s2 = sc[n % 2]
                v.wait(m, sc_free[n % 2])
                for mp in range(2):
                    m = v.do(lambda e, mp=mp: e.tensor_tensor(s2[:, mp, 0:nk], banks[b + mp][:, 0:nk], ali[:, h, T - nk:T], ALU.add))
                    bank_free[b + mp] = m
                v.wait(m)
                m = v.do(lambda e: e.tensor_reduce(st[:, n, 0:2], s2[:, :, 0:nk], AX, ALU.max, negate=True))
                a.wait(m)
                for mp in range(2):
                    m = a.do(lambda e, mp=mp: e.activation(s2[:, mp, 0:nk], s2[:, mp, 0:nk], ACT.Exp, bias=st[:, n, mp:mp + 1], accum_out=st[:, n, 2 + mp:3 + mp]))
                exp_done[n] = m

            def combine(n):
                h, blk = units[n]
                nk = (blk + 1) * P
                s2, at = sc[n % 2], aT[n % 2]
                v.wait(exp_done[n])
                v.step(lambda e: e.reciprocal(st[:, n, 4:6], st[:, n, 2:4]))
                v.step(lambda e: e.tensor_tensor(st[:, n, 5:6], st[:, n, 5:6], nlam, ALU.mult))
                v.step(lambda e: e.tensor_scalar(s2[:, 0, 0:nk], s2[:, 0, 0:nk], st[:, n, 4:5], None, ALU.mult))
                m = v.do(lambda e: e.scalar_tensor_tensor(s2[:, 0, 0:nk], s2[:, 1, 0:nk], st[:, n, 5:6], s2[:, 0, 0:nk], ALU.mult, ALU.add))
                pe.wait(m, bank_free[4])
                for kt in range(blk + 1):
                    m = pe.do(lambda e, kt=kt: e.transpose(banks[4][:, kt * P:(kt + 1) * P], s2[:, 0, kt * P:(kt + 1) * P], ident))
                sc_free[n % 2] = m
                a.wait(m, o_marks.get(n - 2))
                m = bank_free[4] = a.do(lambda e: e.activation(at[:, 0:nk], banks[4][:, 0:nk], ACT.Copy))
                ob = 6 + h // 2
                pe.wait(m, bank_free[ob])

                def mm(e):
                    o = (h % 2) * T + blk * P
                    for kt in range(blk + 1):
                        r = e.matmul(banks[ob][:, o:o + P], vv[:, kt, h * P:(h + 1) * P], at[:, kt * P:(kt + 1) * P], start=(kt == 0), stop=(kt == blk))
                    return r
                o_marks[n] = pe.do(mm)

            done = {}

            def other_branches():
                pe.wait(m_dd, m_params)
                for j in range(2):
                    pe.wait(bank_free[4 + j])
                    m = pe.do(lambda e, j=j: e.matmul(banks[4 + j][:, 0:T], wpool[:, j, :], dd[:, j, :], start=True, stop=True))
                    a.wait(m)
                    bank_free[4 + j] = a.do(lambda e, j=j: e.activation(mixT[:, 2 + j, :], banks[4 + j][:, 0:T], ACT.Copy, scale=C("pool_scale", j)))
                done["pool"] = bank_free[5]

                yield
                ycf = yc.rearrange("p j t -> p (j t)")
                a.wait(m_qkn), v.wait(m_qkn)
                pe.wait(m_y, bank_free[2])
                lnb = sqf[:, 1024:1024 + 2 * T]
                r_ = sqf[:, 1536:1536 + T]

                def sum_channels(src, b):
                    def mm(e):
                        for j in range(2):
                            r = e.matmul(banks[b][:, 0:T], ones, src[:, j, :], start=(j == 0), stop=(j == 1))
                        return r
                    return pe.do(mm)
                m = sum_channels(yc, 2)
                v.wait(m)
                for j in range(2):
                    m = v.do(lambda e, j=j: e.scalar_tensor_tensor(yc[:, j, :], banks[2][:, 0:T], -1.0 / C_CONV, yc[:, j, :], ALU.mult, ALU.add))
                bank_free[2] = m
                yield
                a.wait(m)
                m = a.do(lambda e: e.activation(lnb, ycf, ACT.Square))
                yield
                pe.wait(m, bank_free[3])
                m = sum_channels(lnb.rearrange("p (j t) -> p j t", j=2), 3)
                m = rstd_of(banks[3][:, 0:T], r_, 1.0 / C_CONV, m)
                bank_free[3] = m
                for j in range(2):
                    m = v.do(lambda e, j=j: e.tensor_tensor(yc[:, j, :], yc[:, j, :], r_, ALU.mult))
                yield
                a.wait(m)
                for j in range(2):
                    m = a.do(lambda e, j=j: e.activation(yc[:, j, :], yc[:, j, :], ACT.Silu, bias=C("conv_ln_b", j), scale=C("conv_ln_g", j)))
                yield
                pe.wait(m)
                for j in range(2):
                    b = 4 + j
                    pe.wait(bank_free[b])

                    def mm(e, j=j, b=b):
                        for k in range(2):
                            r = e.matmul(banks[b][:, 0:T], wp1[:, k, j * P:(j + 1) * P], yc[:, k, :], start=(k == 0), stop=(k == 1))
                        return r
                    m = pe.do(mm)
                    a.wait(m)
                    bank_free[b] = a.do(lambda e, j=j, b=b: e.activation(mixT[:, j, :], banks[b][:, 0:T], ACT.Identity, bias=C("conv_pw_b", j)))
                done["conv"] = bank_free[b]

            rest = other_branches()

            scores(0)
            m_ada = None
            for n in range(len(units)):
                if n + 1 < len(units):
                    scores(n + 1)
                m_ada = ada_step(1 + n) or m_ada
                combine(n)
                next(rest, None)
            m_o = o_marks[len(units) - 1]
            osq = sqf[:, 0:2 * T]
            for hp in range(2):
                ob = 6 + hp
                dst = sqf[:, hp * 512:(hp + 1) * 512]
                a.wait(m_o)
                m = a.do(lambda e, ob=ob, dst=dst: e.activation(dst, banks[ob], ACT.Square))
                pe.wait(m, bank_free[2 + hp])
                m = pe.do(lambda e, dst=dst, hp=hp: e.matmul(banks[2 + hp], ones, dst, start=True, stop=True))
                m = rstd_of(banks[2 + hp], dst, 1.0 / P, m)
                bank_free[2 + hp] = m
                md = mixT[:, 4 + 2 * hp:6 + 2 * hp, :].rearrange("p k t -> p (k t)")
                m_att = v.do(lambda e, ob=ob, dst=dst, md=md: e.scalar_tensor_tensor(md, banks[ob], sg, dst, ALU.mult, ALU.mult))
                bank_free[ob] = m_att

            mcol = small[:, 256:352].rearrange("p (n c) -> p n c", c=2)
            pe.wait(m_ada, bank_free[0], bank_free[2])

            def mm(e):
                for n in range(48):
                    c, o = n // 4 % 2, n // 8 * 512 + n % 4 * P
                    r = e.matmul(banks[2 * c][:, 2 * n:2 * n + 2], ada[32 * c:32 * c + 2, o:o + P], ident[32 * c:32 * c + 2, 32 * c:32 * c + 2], start=True, stop=True)
                return r
            m = pe.do(mm)
            v.wait(m)
            for c in range(2):
                bada = Call("b_ada").rearrange("p (m h n o) -> p m h n o", m=6, h=2, o=1)[:, :, c].to_broadcast([P, 6, 4, 2])
                v.step(lambda e, c=c, bada=bada: e.tensor_tensor(mcol.rearrange("p (m h n) c -> p m h n c", m=6, h=2)[:, :, c], banks[2 * c][:, 0:96].rearrange("p (m h n c) -> p m h n c", m=6, h=2, c=2)[:, :, c], bada, ALU.add))
            bank_free[0] = bank_free[2] = Mark(v.counter, None, v.counter.total)
            scl1, scl2 = small[:, 352:368].rearrange("p (k c) -> p k c", c=2), small[:, 368:376]
            n1 = Call("norm1_g").rearrange("p (k o) -> p k o", o=1).to_broadcast([P, 8, 2])
            v.do(lambda e: e.scalar_tensor_tensor(scl1, mcol[:, 8:16, :], 1.0, n1, ALU.add, ALU.mult))
            m_mod = v.do(lambda e: e.scalar_tensor_tensor(scl2, mcol[:, 32:40, 0], 1.0, Call("norm2_g"), ALU.add, ALU.mult))

            pe.wait(m_att, done["pool"], done["conv"])
            m_x1 = []
            for nb in range(2):
                c = column_chunk(d["w_out"][0], nb * 512)
                pe.wait(c[1])
                for t in range(NT):
                    b = 2 * (nb % 2) + t
                    m = project_tokens(c, lambda k, t=t: mixT[:, k, t * P:(t + 1) * P], 512, b)
                    v.wait(m)
                    xs = x[:, t * D + nb * 512:t * D + (nb + 1) * 512]
                    bank_free[b] = v.do(lambda e, xs=xs, b=b: e.tensor_tensor(xs, xs, banks[b], ALU.add))
                    m_x1.append(bank_free[b])
                stream.release(c[0], m)
            join()
            assert z.n <= zone.shape[1] - 15 * P
            return mcol, scl1, scl2

        mcol, scl1, scl2 = first_block()
        def moe(name, ne, nf, wr, bias, wg, wu, wd, scale, shift, acc, after):
            ft = nf // P
            nr = NG + NG * ne
            n_ex = NG * ne
            by_expert = nf == F2
            ranked = n_ex if by_expert else NG
            z = Zone()
            hx = z.take(NT * D)
            slotid = z.take(NT * ranked).rearrange("p (t n) -> p t n", t=NT)
            gates = z.take(NT * n_ex).rearrange("p (t n) -> p t n", t=NT)
            over = group_most[:, 2 * (ne == E2):2 * (ne == E2) + 2]
            if by_expert:
                spare = [z.take(SLOT) for _ in range(RING_MOE - RING)]
            else:
                hg = z.take(NG * KD * P)
                gates_bc = z.take(NG * ne * P)
                selT = z.take(NG * T)
                hcur, gcur, scur = z.take(KD * P), z.take(ne * P), z.take(T)
                act = [z.take(ft * P) for _ in range(2)]
                sil = [z.take(ft * P) for _ in range(2)]
                ysb = z.take(D)
            keep = z.n
            hr = z.take(KD * T).rearrange("p (k t) -> p k t", k=KD)
            lg = z.take(NT * nr).rearrange("p (t n) -> p t n", t=NT)
            oh = z.take(NT * NG).rearrange("p (t g) -> p t g", t=NT)
            assigned = z.take(NT * n_ex).rearrange("p (t g e) -> p t g e", t=NT, g=NG)
            tmp = z.take(NT * NG * ne)
            le = z.take(NT * ne).rearrange("p (t e) -> p t e", t=NT)
            l2 = z.take(NT * ne).rearrange("p (t e) -> p t e", t=NT)
            oh1 = z.take(NT * ne).rearrange("p (t e) -> p t e", t=NT)
            oh2 = z.take(NT * ne).rearrange("p (t e) -> p t e", t=NT)
            ohs = z.take(NT * ne).rearrange("p (t e) -> p t e", t=NT)
            one = z.take(16 * NT).rearrange("p (n t) -> p n t", t=NT)
            def by_groups():
                gates_ge = gates.rearrange("p t (g e) -> p t g e", g=NG)
                z.n = keep
                sel = z.take(NT * NG * P).rearrange("p (t g s) -> p t g s", t=NT, g=NG)
                wsel = z.take(NT * ne * P).rearrange("p (t n) -> p t n", t=NT)
                m_oh = Mark(v.counter, None, v.counter.total)
                pe.wait(m_oh)

                def mm(e):
                    e.matmul(banks[1][:, 0:NG], Call("before"), oh[:, 0, :], start=True, stop=True)
                    e.matmul(banks[1][:, NG:2 * NG], Call("before"), oh[:, 1, :], start=True, stop=False)
                    e.matmul(banks[1][:, NG:2 * NG], ones, oh[:, 0, :], start=False, stop=True)
                    e.matmul(banks[1][:, 2 * NG:3 * NG], ones, oh[:, 0, :], start=True, stop=False)
                    return e.matmul(banks[1][:, 2 * NG:3 * NG], ones, oh[:, 1, :], start=False, stop=True)
                m = pe.do(mm)
                v.wait(m)
                v.step(lambda e: e.tensor_scalar(tmp[:, 0:NT * NG].rearrange("p (t g) -> p t g", t=NT), oh, -1.0, BIG, ALU.add, ALU.mult))
                v.step(lambda e: e.tensor_tensor(slotid, banks[1][:, 0:NT * NG].rearrange("p (t g) -> p t g", t=NT), oh, ALU.mult))
                v.step(lambda e: e.tensor_tensor(slotid, slotid, tmp[:, 0:NT * NG].rearrange("p (t g) -> p t g", t=NT), ALU.add))
                v.step(lambda e: e.tensor_reduce(over[:, 1:2], banks[1][:, 2 * NG:3 * NG], AX, ALU.max))
                m_over = v.step(lambda e: e.tensor_copy(over[:, 0:1].bitcast(I32), over[:, 1:2]))

                def prepare(start):
                    if start:
                        v.step(lambda e: e.tensor_scalar(slotid, slotid, -float(start), None, ALU.add))
                    for t in range(NT):
                        for gi in range(NG):
                            m = v.do(lambda e, t=t, gi=gi: e.tensor_scalar(sel[:, t, gi, :], Call("iota"), slotid[:, t, gi:gi + 1], None, ALU.is_equal))
                    v.wait(m)
                    pe.wait(m)
                    f = [None] * 4
                    m_out = []
                    for gi in range(NG):
                        for half in range(2):
                            b = half

                            def mm(e, gi=gi, half=half, b=b):
                                for kk in range(4):
                                    k = half * 4 + kk
                                    for t in range(NT):
                                        r = e.matmul(banks[b][:, kk * P:(kk + 1) * P], hx[:, t * D + k * P:t * D + (k + 1) * P], sel[:, t, gi, :], start=(t == 0), stop=(t == NT - 1))
                                return r
                            pe.wait(f[b])
                            m = pe.do(mm)
                            q = a if half else v
                            q.wait(m)
                            for kk in range(4):
                                k = half * 4 + kk
                                dst = hg[:, gi * D + k * P:gi * D + (k + 1) * P]
                                src = banks[b][:, kk * P:(kk + 1) * P]
                                sc_, sh_ = scale(k), None if shift is None else shift(k)
                                if q is v:
                                    m = v.do(lambda e, dst=dst, src=src, sc_=sc_, sh_=sh_: e.tensor_scalar(dst, src, sc_, sh_, ALU.mult, *([] if sh_ is None else [ALU.add])))
                                else:
                                    m = a.do(lambda e, dst=dst, src=src, sc_=sc_, sh_=sh_: e.activation(dst, src, ACT.Identity, bias=0.0 if sh_ is None else sh_, scale=sc_))
                            f[b] = m
                            m_out.append(m)
                        for t in range(NT):
                            if gi or t:
                                v.wait(m_w)
                            m = v.do(lambda e, t=t, gi=gi: e.tensor_tensor(wsel[:, t, :].rearrange("p (e s) -> p e s", e=ne), sel[:, t, gi, :].unsqueeze(1).to_broadcast([P, ne, P]), gates_ge[:, t, gi, :].unsqueeze(2).to_broadcast([P, ne, P]), ALU.mult))
                            m_w = m if t == 0 and gi == 0 else m_w
                        pe.wait(m)
                        for nb in range(ne * P // 512):
                            b = 2 + nb

                            def mm(e, nb=nb, b=b):
                                for t in range(NT):
                                    r = e.matmul(banks[b], ones, wsel[:, t, nb * 512:(nb + 1) * 512], start=(t == 0), stop=(t == NT - 1))
                                return r
                            pe.wait(f[b])
                            m_w = pe.do(mm)
                            a.wait(m_w)
                            o = gi * ne * P + nb * 512
                            f[b] = a.do(lambda e, o=o, b=b: e.activation(gates_bc[:, o:o + 512], banks[b], ACT.Copy))
                        m_out.append(f[b])
                    for gp in range(NG // 2):
                        b = 4 + gp
                        for gi in range(2):
                            for t in range(NT):
                                m = pe.do(lambda e, gi=gi, t=t, gp=gp, b=b: e.transpose(banks[b][:, gi * T + t * P:gi * T + (t + 1) * P], sel[:, t, 2 * gp + gi, :], ident))
                        a.wait(m)
                        m_out.append(a.do(lambda e, gp=gp, b=b: e.activation(selT[:, gp * 2 * T:(gp + 1) * 2 * T], banks[b], ACT.Copy)))
                    return m_out

                pack = 2 if nf == F1 else 1

                def sources(ex):
                    return (wg[bass.ds(ex, 1)].rearrange("o (k p) f -> p (o k) f", p=P), wu[bass.ds(ex, 1)].rearrange("o (k p) f -> p (o k) f", p=P),
                            wd[bass.ds(ex, 1)].rearrange("o (k p) n -> p (o k) n", p=P))

                half_a = lambda slot: slot[:, 0:KD * nf].rearrange("p (k n) -> p k n", k=KD)
                half_b = lambda slot: slot[:, KD * nf:2 * KD * nf].rearrange("p (k n) -> p k n", k=KD)
                down_a = lambda slot: slot[:, 0:ft * D].rearrange("p (k n) -> p k n", k=ft)
                down_b = lambda slot: slot[:, ft * D:2 * ft * D].rearrange("p (k n) -> p k n", k=ft)

                groups_per_turn = 2 if pack == 2 else 1
                turns = NG // groups_per_turn
                nx = ne * groups_per_turn
                plan = []
                if pack == 2:
                    for e2 in range(0, nx, 2):
                        plan.append([("gu", e2, [(half_a, 0, e2), (half_b, 1, e2)])])
                        plan.append([("gu", e2 + 1, [(half_a, 0, e2 + 1), (half_b, 1, e2 + 1)])])
                        plan.append([("d", e2, [(down_a, 2, e2), (down_b, 2, e2 + 1)])])
                    plan = [p_[0] for p_ in plan]
                else:
                    for ex in range(nx + 1):
                        if ex < nx:
                            plan.append(("g", ex, [(half_a, 0, ex)]))
                            plan.append(("u", ex, [(half_a, 1, ex)]))
                        if ex > 0:
                            plan.append(("d", ex - 1, [(down_a, 2, ex - 1)]))
                assert len(plan) % RING == 0

                base = stream.n

                def load_chunk(j, turn_of):
                    k = (base + j) % RING
                    for view, which, ex in plan[j][2]:
                        def go(e, i=None, view=view, which=which, ex=ex, k=k):
                            t0 = turn_of(i)
                            return e.dma_start(view(ring[k]), sources(t0 * nx + ex)[which])
                        m = s.do(go, stream.slot_in[k], 16)
                    return m

                def groups(m_ready):
                    for k in range(RING):
                        s.wait(stream.released[(base + k) % RING])
                        load_chunk(k, lambda i: 0)
                    for q in (pe, v, a):
                        q.wait(m_ready)

                    def turn():
                        ahead = [Later() for _ in range(RING)]
                        loaded = ahead + [None] * (len(plan) - RING)
                        released = [None] * len(plan)
                        rel = [Later2() for _ in plan]
                        for j in range(RING, len(plan)):
                            s.wait(rel[j - RING])
                            loaded[j] = load_chunk(j, lambda i: i)
                        s.ahead_part = True
                        for j in range(RING):
                            s.wait(rel[len(plan) - RING + j])
                            ahead[j].set(load_chunk(j, lambda i: i + 1))
                        at = {}
                        for j, (what, ex, _) in enumerate(plan):
                            at[what, ex] = j

                        prev_gu, prev_sel, prev_add = Later(), Later(), [Later(), Later()]
                        prev_bank = [Later(), Later()]
                        prev_y = [Later(), Later()]
                        prev_down = [Later(), Later()]
                        act_m, gu_free, down_m = {}, {}, {}
                        state = {}

                        def gate_up(ex):
                            p2 = ex % 2
                            gl, el = ex // ne, ex % ne
                            if el == 0:
                                if gl:
                                    v.wait(state["gu"]), a.wait(state["gu"])
                                    v.wait(state["scatter"])
                                else:
                                    v.wait(prev_gu, prev_sel), a.wait(prev_gu)
                                m1 = v.do(lambda e, i: e.tensor_copy(hcur, hg[:, bass.ds((i * groups_per_turn + gl) * D, D)]))
                                m2 = a.do(lambda e, i: e.activation(gcur, gates_bc[:, bass.ds((i * groups_per_turn + gl) * (ne * P), ne * P)], ACT.Copy))
                                m3 = v.do(lambda e, i: e.tensor_copy(scur, selT[:, bass.ds((i * groups_per_turn + gl) * T, T)]))
                                v.wait(m2)
                                pe.wait(m1)
                                state["scur"] = m3
                            pe.wait(gu_free[ex - 2] if ex >= 2 else prev_bank[ex])
                            gb, ub = banks[2 * p2], banks[2 * p2 + 1]
                            ms = []
                            for n, (bk, key) in enumerate(((gb, "g"), (ub, "u"))):
                                if pack == 2:
                                    j = at["gu", ex]
                                    view = half_b if n else half_a
                                else:
                                    j = at[key, ex]
                                    view = half_a
                                if n == 0 or pack == 1:
                                    pe.wait(loaded[j])
                                w = view(ring[(base + j) % RING])

                                def mm(e, i, bk=bk, w=w):
                                    for f_ in range(ft):
                                        for k in range(KD):
                                            r = e.matmul(bk[:, f_ * P:(f_ + 1) * P], w[:, k, f_ * P:(f_ + 1) * P], hcur[:, k * P:(k + 1) * P], start=(k == 0), stop=(k == KD - 1))
                                    return r
                                ms.append(pe.do(mm))
                                rel[j].set(ms[-1])
                            state["gu"] = ms[1]
                            if ex == nx - 1:
                                prev_gu.set(ms[1])
                            a.wait(ms[0])
                            if ex >= 2:
                                a.wait(act_m[ex - 2])
                            else:
                                a.wait(prev_bank[ex])
                            m = a.do(lambda e, i: e.activation(sil[p2], gb[:, 0:ft * P], ACT.Silu))
                            v.wait(m, ms[1])
                            m = v.do(lambda e, i: e.tensor_tensor(sil[p2], sil[p2], ub[:, 0:ft * P], ALU.mult))
                            gu_free[ex] = m
                            v.wait(m)
                            v.wait(down_m[ex - 2] if ex >= 2 else prev_down[ex])
                            gc = gcur[:, el * P:(el + 1) * P].unsqueeze(1).to_broadcast([P, ft, P])
                            act_m[ex] = v.do(lambda e, i: e.tensor_tensor(act[p2].rearrange("p (f s) -> p f s", f=ft), sil[p2].rearrange("p (f s) -> p f s", f=ft), gc, ALU.mult))
                            if ex >= nx - 2:
                                prev_bank[ex - nx + 2].set(act_m[ex])

                        def down(ex):
                            p2 = ex % 2
                            gl, el = ex // ne, ex % ne
                            j = at["d", ex - ex % 2] if pack == 2 else at["d", ex]
                            w = (down_b if pack == 2 and ex % 2 else down_a)(ring[(base + j) % RING])
                            pe.wait(loaded[j], act_m[ex])
                            if el == 0:
                                pe.wait(state["y"] if gl else prev_y)

                            def mm(e, i):
                                for f_ in range(ft):
                                    for nb in range(2):
                                        r = e.matmul(banks[4 + nb], act[p2][:, f_ * P:(f_ + 1) * P], w[:, f_, nb * 512:(nb + 1) * 512],
                                                     start=(el == 0 and f_ == 0), stop=(el == ne - 1 and f_ == ft - 1))
                                return r
                            down_m[ex] = pe.do(mm)
                            if pack == 1 or ex % 2:
                                rel[j].set(down_m[ex])
                            if ex >= nx - 2:
                                prev_down[ex - nx + 2].set(down_m[ex])
                            if el == ne - 1:
                                scatter(gl)

                        def scatter(gl):
                            v.wait(down_m[gl * ne + ne - 1], state["scatter"] if gl else prev_sel)
                            a.wait(down_m[gl * ne + ne - 1], state["scatter"] if gl else prev_sel)
                            y0 = v.do(lambda e, i: e.tensor_copy(ysb[:, 0:512], banks[4]))
                            y1 = a.do(lambda e, i: e.activation(ysb[:, 512:1024], banks[5], ACT.Copy))
                            state["y"] = [y0, y1]
                            if gl == groups_per_turn - 1:
                                prev_y[0].set(y0), prev_y[1].set(y1)
                            pe.wait(y0, y1, state["scur"])
                            for n, (t, nb) in enumerate([(t, nb) for t in range(NT) for nb in range(2)]):
                                b = 6 + n % 2
                                pe.wait(state["add", n - 2] if n >= 2 else (state["add", n + 2] if gl else prev_add[n]))
                                m = pe.do(lambda e, i, t=t, nb=nb, b=b: e.matmul(banks[b], scur[:, t * P:(t + 1) * P], ysb[:, nb * 512:(nb + 1) * 512], start=True, stop=True))
                                state["scatter"] = m
                                v.wait(m)
                                av = acc[:, t * D + nb * 512:t * D + (nb + 1) * 512]
                                v.wait(state.get(("acc", t, nb)) or prev_acc[t * 2 + nb])
                                m = v.do(lambda e, i, av=av, b=b: e.tensor_tensor(av, av, banks[b], ALU.add))
                                state["add", n] = m
                                state["acc", t, nb] = m
                                if gl == groups_per_turn - 1:
                                    prev_acc[t * 2 + nb].set(m)
                                    if n >= 2:
                                        prev_add[n - 2].set(m)
                            if gl == groups_per_turn - 1:
                                prev_sel.set(state["scatter"])

                        prev_acc = [Later() for _ in range(4)]
                        for what, ex, _ in plan:
                            if what in ("u", "gu"):
                                gate_up(ex)
                            if what == "d":
                                down(ex)
                                if pack == 2:
                                    down(ex + 1)
                        for k in range(RING):
                            stream.released[(base + k) % RING] = rel[len(plan) - RING + k].mark
                    prog.loop(turns, turn)

                m_ready = prepare(0)
                groups(m_ready)

                def second_pass():
                    released, stream.released = stream.released, [None] * RING
                    stream.slot_in = [prog.new_counter(f"{name}_slot_in{k}") for k in range(RING)]
                    groups(prepare(P))
                    stream.released, stream.slot_in = released, slot_in
                for q in prog.queues:
                    q.wait(m_over)
                s.wait(stream.released)
                prog.branch(over[0:1, 0:1].bitcast(I32), T, P, name, second_pass)


            def by_experts():
                m_oh = Mark(v.counter, None, v.counter.total)
                pe.wait(m_oh)
                asg = assigned.rearrange("p t g e -> p t (g e)")

                def mm(e):
                    rank = banks[1]
                    e.matmul(rank[:, 0:n_ex], Call("before"), asg[:, 0, :], start=True, stop=True)
                    e.matmul(rank[:, n_ex:2 * n_ex], Call("before"), asg[:, 1, :], start=True, stop=False)
                    e.matmul(rank[:, n_ex:2 * n_ex], ones, asg[:, 0, :], start=False, stop=True)
                    e.matmul(rank[:, 2 * n_ex:3 * n_ex], ones, asg[:, 0, :], start=True, stop=False)
                    return e.matmul(rank[:, 2 * n_ex:3 * n_ex], ones, asg[:, 1, :], start=False, stop=True)
                m = pe.do(mm)
                v.wait(m)
                tv = tmp.rearrange("p (t n) -> p t n", t=NT)
                v.step(lambda e: e.tensor_scalar(tv, asg, -1.0, BIG, ALU.add, ALU.mult))
                v.step(lambda e: e.tensor_tensor(slotid, banks[1][:, 0:NT * n_ex].rearrange("p (t n) -> p t n", t=NT), asg, ALU.mult))
                v.step(lambda e: e.tensor_tensor(slotid, slotid, tv, ALU.add))
                v.step(lambda e: e.tensor_reduce(over[:, 1:2], banks[1][:, 2 * n_ex:3 * n_ex], AX, ALU.max))
                m_over = v.step(lambda e: e.tensor_copy(over[:, 0:1].bitcast(I32), over[:, 1:2]))

                small_ffn = 2 * nf == 512
                nx = 2 * PAIRS
                turns = n_ex // nx
                z.n = keep
                hgp = [z.take(KD * P).rearrange("p (k s) -> p k s", k=KD) for _ in range(2)]
                sel = [z.take(NT * P).rearrange("p (t s) -> p t s", t=NT) for _ in range(2)]
                wsel = [z.take(NT * P).rearrange("p (t s) -> p t s", t=NT) for _ in range(2)]
                back = [z.take(T) for _ in range(PAIRS)]
                sil = [z.take(nf) for _ in range(2)]
                actT = z.take(ft * P)
                ysb = z.take(D)
                slot_now = z.take(NT * nx).rearrange("p (t n) -> p t n", t=NT)
                gate_now = z.take(NT * nx).rearrange("p (t n) -> p t n", t=NT)

                assert z.n <= zone.shape[1] - NT * D

                plan = []
                for q in range(PAIRS + 1):
                    if q < PAIRS:
                        plan += [("gu", q, 0), ("gu", q, 1)] if small_ffn else [("g", q, 0), ("g", q, 1), ("u", q, 0), ("u", q, 1)]
                    if q > 0:
                        plan += [("d", q - 1, None)] if small_ffn else [("d", q - 1, 0), ("d", q - 1, 1)]
                assert len(plan) % RING_MOE == 0
                at = {what: j for j, what in enumerate(plan)}
                slots = ring + spare

                def load_chunk(j, turn_of):
                    what, q, c = plan[j]
                    slot = slots[j % RING_MOE]
                    counter = stream.slot_in[j % RING_MOE]

                    def dma(dst, w, ex, counter=counter):
                        def go(e, i=None):
                            src = w[bass.ds(turn_of(i) * nx + ex, 1)].rearrange("o (k p) n -> p (o k) n", p=P)
                            return e.dma_start(dst, src)
                        return s.do(go, counter, 16)
                    ex = 2 * q + (c or 0)
                    if what == "gu":
                        both = slot.rearrange("p (k n) -> p k n", k=KD)
                        dma(both[:, :, 0:nf], wg, ex)
                        return dma(both[:, :, nf:], wu, ex)
                    if what == "d" and small_ffn:
                        dma(slot[:, 0:ft * D].rearrange("p (k n) -> p k n", k=ft), wd, ex)
                        return dma(slot[:, ft * D:].rearrange("p (k n) -> p k n", k=ft), wd, ex + 1)
                    if what == "d":
                        return dma(slot.rearrange("p (k n) -> p k n", k=ft), wd, ex)
                    return dma(slot.rearrange("p (k n) -> p k n", k=KD), wg if what == "g" else wu, ex)

                def passes():
                    for j in range(RING_MOE):
                        s.wait(stream.released[j])
                        if j == RING:
                            s.wait(m_n)
                        load_chunk(j, lambda i: 0)

                    def turn():
                        ahead = [Later() for _ in range(RING_MOE)]
                        loaded = ahead + [None] * (len(plan) - RING_MOE)
                        rel = [Later2() for _ in plan]
                        for j in range(RING_MOE, len(plan)):
                            s.wait(rel[j - RING_MOE])
                            loaded[j] = load_chunk(j, lambda i: i)
                        s.ahead_part = True
                        for j in range(RING_MOE):
                            s.wait(rel[len(plan) - RING_MOE + j])
                            ahead[j].set(load_chunk(j, lambda i: i + 1))

                        ends = [Later(), Later(), Later()]
                        for q in (pe, v, a):
                            q.wait(ends)
                        M = {}

                        v.do(lambda e, i: e.tensor_copy(slot_now, slotid[:, :, bass.ds(i * nx, nx)]))
                        v.step(lambda e, i: e.tensor_copy(gate_now, gates[:, :, bass.ds(i * nx, nx)]))

                        def select(q):
                            v.wait(M.get(("gathered", q - 2)), M.get(("back", q - 2)))
                            for t in range(NT):
                                for c in range(2):
                                    cs, ex = slice(c * SLOTS, (c + 1) * SLOTS), 2 * q + c
                                    M["sel", q] = v.do(lambda e, i, t=t, cs=cs, ex=ex: e.tensor_scalar(sel[q % 2][:, t, cs], Call("iota")[:, 0:SLOTS], slot_now[:, t, ex:ex + 1], None, ALU.is_equal))
                            for t in range(NT):
                                for c in range(2):
                                    cs, ex = slice(c * SLOTS, (c + 1) * SLOTS), 2 * q + c
                                    M["wsel", q] = v.do(lambda e, i, t=t, cs=cs, ex=ex: e.tensor_scalar(wsel[q % 2][:, t, cs], Call("iota")[:, 0:SLOTS], slot_now[:, t, ex:ex + 1], gate_now[:, t, ex:ex + 1], ALU.is_equal, ALU.mult))

                        def gather(q, half):
                            pe.wait(M["sel", q], M.get("b5"))

                            def mm(e, i):
                                for kk in range(4):
                                    k = half * 4 + kk
                                    for t in range(NT):
                                        r = e.matmul(banks[5][:, kk * P:(kk + 1) * P], hx[:, t * D + k * P:t * D + (k + 1) * P], sel[q % 2][:, t, :], start=(t == 0), stop=(t == NT - 1))
                                return r
                            m = pe.do(mm)
                            M["gathered", q] = m
                            (a if half else v).wait(m, M.get(("up", q - 2)))
                            for kk in range(4):
                                k = half * 4 + kk
                                dst, src = hgp[q % 2][:, k, :], banks[5][:, kk * P:(kk + 1) * P]
                                sc_, sh_ = scale(k), None if shift is None else shift(k)
                                if half == 0:
                                    m = v.do(lambda e, i, dst=dst, src=src, sc_=sc_, sh_=sh_: e.tensor_scalar(dst, src, sc_, sh_, ALU.mult, *([] if sh_ is None else [ALU.add])))
                                else:
                                    m = a.do(lambda e, i, dst=dst, src=src, sc_=sc_, sh_=sh_: e.activation(dst, src, ACT.Identity, bias=0.0 if sh_ is None else sh_, scale=sc_))
                            M["b5"] = m
                            M.setdefault(("hg", q), []).append(m)

                        def turn_back(q):
                            pe.wait(M["wsel", q], M["b5"])
                            for t in range(NT):
                                m = pe.do(lambda e, i, t=t: e.transpose(banks[5][:, t * P:(t + 1) * P], wsel[q % 2][:, t, :], ident))
                            M["back", q] = m
                            a.wait(m)
                            M["b5"] = M["backT", q] = a.do(lambda e, i: e.activation(back[q], banks[5][:, 0:T], ACT.Copy))

                        def gate_up(q):
                            pe.wait(M["hg", q])
                            outs = [("gu", banks[q % 2])] if small_ffn else [("g", banks[0]), ("u", banks[1])]
                            for what, bank in outs:
                                js = [at[what, q, c] for c in range(2)]
                                pe.wait([loaded[j] for j in js])
                                pe.wait(M.get(("act", q - 2)) if small_ffn else M.get(("silu" if what == "g" else "act", q - 1)))
                                w = [slots[j % RING_MOE].rearrange("p (k n) -> p k n", k=KD) for j in js]

                                def mm(e, i, w=w, bank=bank):
                                    for k in range(KD):
                                        for c in range(2):
                                            cs = slice(c * SLOTS, (c + 1) * SLOTS)
                                            r = e.matmul(bank[cs, :], hgp[q % 2][:, k, cs], w[c][:, k, :], start=(k == 0), stop=(k == KD - 1), tile_position=(0, c * SLOTS))
                                    return r
                                m = pe.do(mm)
                                M["up", q] = m
                                for j in js:
                                    rel[j].set(m)
                                if what != "u":
                                    a.wait(m, M.get(("turned", q - 2)))
                                    M["silu", q] = a.do(lambda e, i, bank=bank: e.activation(sil[q % 2], bank[:, 0:nf], ACT.Silu))
                            up = outs[-1][1][:, 512 - nf:]
                            v.wait(M["silu", q], m)
                            M["act", q] = v.do(lambda e, i, up=up: e.tensor_tensor(sil[q % 2], sil[q % 2], up, ALU.mult))

                        def turn_act(q):
                            pe.wait(M["act", q], M.get(("actT", q - 1)))
                            for f_ in range(ft):
                                m = pe.do(lambda e, i, f_=f_: e.transpose(banks[4][:, f_ * P:(f_ + 1) * P], sil[q % 2][:, f_ * P:(f_ + 1) * P], ident))
                            M["turned", q] = m
                            a.wait(m, M.get(("down", q - 1)))
                            M["actT", q] = a.do(lambda e, i: e.activation(actT, banks[4][:, 0:ft * P], ACT.Copy))

                        def down(q):
                            js = [at["d", q, None]] if small_ffn else [at["d", q, c] for c in range(2)]
                            pe.wait([loaded[j] for j in js], M["actT", q], M.get(("y", q - 1)))
                            if small_ffn:
                                both = slots[js[0] % RING_MOE]
                                w = [both[:, c * ft * D:(c + 1) * ft * D].rearrange("p (k n) -> p k n", k=ft) for c in range(2)]
                            else:
                                w = [slots[j % RING_MOE].rearrange("p (k n) -> p k n", k=ft) for j in js]

                            def mm(e, i):
                                for nb in range(2):
                                    for f_ in range(ft):
                                        for c in range(2):
                                            r = e.matmul(banks[2 + nb][c * SLOTS:(c + 1) * SLOTS, :], actT[:, f_ * P + c * SLOTS:f_ * P + (c + 1) * SLOTS], w[c][:, f_, nb * 512:(nb + 1) * 512],
                                                         start=(f_ == 0), stop=(f_ == ft - 1), tile_position=(0, c * SLOTS))
                                return r
                            m = M["down", q] = pe.do(mm)
                            for j in js:
                                rel[j].set(m)
                            v.wait(m, M.get(("scattered", q - 1)))
                            a.wait(m, M.get(("scattered", q - 1)))
                            M["y", q] = [v.do(lambda e, i: e.tensor_copy(ysb[:, 0:512], banks[2])),
                                         a.do(lambda e, i: e.activation(ysb[:, 512:1024], banks[3], ACT.Copy))]

                        def scatter(q):
                            pe.wait(M["y", q], M["backT", q])
                            for n, (t, nb) in enumerate([(t, nb) for t in range(NT) for nb in range(2)]):
                                b = 6 + n % 2
                                pe.wait(M.get(("bank", b)))
                                m = M["scattered", q] = pe.do(lambda e, i, t=t, nb=nb, b=b: e.matmul(banks[b], back[q][:, t * P:(t + 1) * P], ysb[:, nb * 512:(nb + 1) * 512], start=True, stop=True))
                                av = acc[:, t * D + nb * 512:t * D + (nb + 1) * 512]
                                v.wait(m, M.get(("acc", n)))
                                M["bank", b] = M["acc", n] = v.do(lambda e, i, av=av, b=b: e.tensor_tensor(av, av, banks[b], ALU.add))

                        select(0)
                        gather(0, 0), gather(0, 1), turn_back(0)
                        for q in range(PAIRS):
                            if q + 1 < PAIRS:
                                select(q + 1)
                            gate_up(q)
                            if q > 0:
                                turn_act(q - 1)
                            if q + 1 < PAIRS:
                                gather(q + 1, 0)
                            if q > 1:
                                scatter(q - 2)
                            if q + 1 < PAIRS:
                                gather(q + 1, 1)
                            if q > 0:
                                down(q - 1)
                            if q + 1 < PAIRS:
                                turn_back(q + 1)
                        turn_act(PAIRS - 1)
                        scatter(PAIRS - 2)
                        down(PAIRS - 1)
                        scatter(PAIRS - 1)
                        ends[0].set(M["scattered", PAIRS - 1])
                        ends[1].set(M["acc", 3])
                        ends[2].set(M["y", PAIRS - 1][1])
                        for j in range(RING_MOE):
                            stream.released[j] = rel[len(plan) - RING_MOE + j].mark
                    prog.loop(turns, turn)

                def set_stream(released, slot_in_):
                    was = stream.released, stream.slot_in
                    stream.released, stream.slot_in = released, slot_in_
                    return was

                set_stream(stream.released[0:RING] + [None] * (RING_MOE - RING), slot_in)
                passes()
                for q in prog.queues:
                    q.wait(m_over)
                s.wait(stream.released)

                for n in range(1, T // SLOTS):
                    def next_pass():
                        was = set_stream([None] * RING_MOE, [prog.new_counter(f"{name}_pass{n}_slot_in{k}") for k in range(RING_MOE)])
                        m = v.step(lambda e: e.tensor_scalar(slotid, slotid, -float(SLOTS), None, ALU.add))
                        pe.wait(m)
                        passes()
                        set_stream(*was)
                    prog.branch(over[0:1, 0:1].bitcast(I32), T, n * SLOTS, f"{name}_pass{n}", next_pass)


            stat = small[:, 0:8]

            m_n = norm_tokens(x, hx, stat, after)
            m_h = to_channels(hx, lambda k: hr[:, k, :], scale, shift, m_n, [None, None])

            pe.wait(m_h)
            wv = wr.rearrange("p (k n) -> p k n", k=KD)
            for t in range(NT):
                def mm(e, t=t):
                    for k in range(KD):
                        r = e.matmul(banks[0][:, t * nr:(t + 1) * nr], hr[:, k, t * P:(t + 1) * P], wv[:, k, :], start=(k == 0), stop=(k == KD - 1))
                    return r
                m = pe.do(mm)
            v.wait(m)
            bb = bias.unsqueeze(1).to_broadcast([P, NT, nr])
            v.step(lambda e: e.tensor_tensor(lg, banks[0][:, 0:NT * nr].rearrange("p (t n) -> p t n", t=NT), bb, ALU.add))

            def bc(col, n):
                return one[:, col, :].unsqueeze(2).to_broadcast([P, NT, n])

            def first_of_max(src, n, out, cm, ci):
                io = Call("iota")[:, 0:n].unsqueeze(1).to_broadcast([P, NT, n])
                v.step(lambda e: e.tensor_reduce(one[:, cm, :], src, AX, ALU.max))
                v.step(lambda e: e.tensor_tensor(out, src, bc(cm, n), ALU.is_lt))
                v.step(lambda e: e.scalar_tensor_tensor(out, out, BIG, io, ALU.mult, ALU.add))
                v.step(lambda e: e.tensor_reduce(one[:, ci, :], out, AX, ALU.min))
                v.step(lambda e: e.tensor_tensor(out, io, bc(ci, n), ALU.is_equal))

            lgg = lg[:, :, 0:NG]
            first_of_max(lgg, NG, oh, 0, 1)
            v.step(lambda e: e.tensor_tensor(tmp[:, 0:NT * NG].rearrange("p (t g) -> p t g", t=NT), lgg, bc(0, NG), ALU.subtract))
            m_d = Mark(v.counter, None, v.counter.total)
            a.wait(m_d)
            m = a.do(lambda e: e.activation(tmp[:, 0:NT * NG], tmp[:, 0:NT * NG], ACT.Exp))
            v.wait(m)
            v.step(lambda e: e.tensor_reduce(one[:, 2, :], tmp[:, 0:NT * NG].rearrange("p (t g) -> p t g", t=NT), AX, ALU.add))
            for t in range(NT):
                src = lg[:, t, NG:].rearrange("p (g e) -> p g e", g=NG)
                tv = tmp[:, t * NG * ne:(t + 1) * NG * ne]
                v.step(lambda e, t=t, src=src, tv=tv: e.tensor_tensor(tv.rearrange("p (g e) -> p g e", g=NG), src, oh[:, t, :].unsqueeze(2).to_broadcast([P, NG, ne]), ALU.mult))
                v.step(lambda e, t=t, tv=tv: e.tensor_reduce(le[:, t, :], tv.rearrange("p (g e) -> p e g", g=NG), AX, ALU.add))
            first_of_max(le, ne, oh1, 3, 4)
            v.step(lambda e: e.scalar_tensor_tensor(l2, oh1, NEG, le, ALU.mult, ALU.add))
            first_of_max(l2, ne, oh2, 5, 6)
            v.step(lambda e: e.tensor_tensor(ohs, oh1, oh2, ALU.add))
            v.step(lambda e: e.tensor_tensor(one[:, 7, :], one[:, 5, :], one[:, 3, :], ALU.subtract))
            m_d = Mark(v.counter, None, v.counter.total)
            a.wait(m_d)
            m = a.do(lambda e: e.activation(one[:, 7, :], one[:, 7, :], ACT.Exp))
            v.wait(m)
            v.step(lambda e: e.tensor_scalar(one[:, 8, :], one[:, 7, :], 1.0, None, ALU.add))
            v.step(lambda e: e.tensor_tensor(one[:, 8, :], one[:, 8, :], one[:, 2, :], ALU.mult))
            v.step(lambda e: e.reciprocal(one[:, 8, :], one[:, 8, :]))
            v.step(lambda e: e.tensor_tensor(one[:, 7, :], one[:, 7, :], one[:, 8, :], ALU.mult))
            v.step(lambda e: e.tensor_tensor(oh1, oh1, bc(8, ne), ALU.mult))
            v.step(lambda e: e.tensor_tensor(oh2, oh2, bc(7, ne), ALU.mult))
            v.step(lambda e: e.tensor_tensor(oh1, oh1, oh2, ALU.add))
            for t in range(NT):
                for dst, of_two in ((gates[:, t].rearrange("p (g e) -> p g e", g=NG), oh1), (assigned[:, t], ohs))[:1 + by_expert]:
                    v.step(lambda e, t=t, dst=dst, of_two=of_two: e.tensor_tensor(dst, oh[:, t, :].unsqueeze(2).to_broadcast([P, NG, ne]), of_two[:, t, :].unsqueeze(1).to_broadcast([P, NG, ne]), ALU.mult))


            if by_expert:
                by_experts()
            else:
                by_groups()
        moe("moe1", E1, F1, w_route[0], R("r1_b"), d["w_gate"][0], d["w_up"][0], d["w_down"][0],
            lambda k: C("ffn_norm_g", k), None, x, [])
        m_moe1 = join()
        w2 = d["w_in_2"][0]
        for i_ in range(8):
            bank_free[i_] = None
        z = Zone()
        hT = z.take(KD * 2 * T).rearrange("p (k t) -> p k t", k=KD)
        yaT = z.take(KD * T).rearrange("p (k t) -> p k t", k=KD)
        brow = z.take(2048)
        w_if = z.take(KD * P).rearrange("p (k n) -> p k n", k=KD)
        keep_gla = z.n
        cx, xn, cn = z.take(NT * D), z.take(NT * D), z.take(NT * D)
        w16 = z.take(KD * 16).rearrange("p (k n) -> p k n", k=KD)

        for c0 in (O_FF, O_FB, O_Q):
            early[id(w2), c0] = column_chunk(w2, c0)
        s.wait(m_moe1)
        s.do(lambda e: e.dma_start(cx.rearrange("p (t n) -> p t n", t=NT), d["ctx_2"][0].rearrange("(t p) n -> p t n", p=P)), params_in, 16)
        s.do(lambda e: e.dma_start(brow[0:1, 0:1024], d["b_in_2"][0:1, O_HI:O_HI + 1024]), params_in, 16)
        s.do(lambda e: e.dma_start(brow[0:1, 1024:2048], d["b_in_2"][0:1, O_MV:O_MV + 1024]), params_in, 16)
        m_small = s.do(lambda e: e.dma_start(w16, w2[:, O_IF:O_IF + 16].rearrange("(k p) n -> p k n", p=P)), params_in, 16)
        m = g.do(lambda e: e.memset(w_if, 0.0))
        g.wait(m, m_small)
        for n in range(4):
            m_wif = g.do(lambda e, n=n: e.tensor_copy(w_if[:, :, 32 * n:32 * n + 4], w16[:, :, 4 * n:4 * n + 4]))

        lbv = Call("lb").rearrange("p (d l j) -> p d l j", d=2, l=2)
        lbs = small[:, 376:408].rearrange("p (o d j) -> p o d j", o=2, d=2)
        nbf = small[:, 408:424]
        v.do(lambda e: e.tensor_tensor(lbs[:, 0], lbv[:, :, 0, :], lbv[:, :, 1, :], ALU.subtract))
        v.do(lambda e: e.tensor_scalar(nbf, C("b_in", O_FF // P, 16), -1.0, None, ALU.mult))
        m = v.do(lambda e: e.tensor_tensor(lbs[:, 1], lbv[:, :, 1, :], lbv[:, :, 0, :], ALU.subtract))
        a.wait(m)
        m_lb = a.do(lambda e: e.activation(lbs, lbs, ACT.Sigmoid))

        m_n = norm_tokens(x, xn, small[:, 0:2])
        m_n2 = norm_tokens(cx, cn, small[:, 2:4], m_small)
        m_h = to_channels(xn, lambda k: hT[:, k, 0:T], lambda k: scl1[:, k, 0:1], lambda k: mcol[:, k, 0:1], m_n, [None, None])
        m_h2 = to_channels(cn, lambda k: hT[:, k, T:2 * T], lambda k: scl1[:, k, 1:2], lambda k: mcol[:, k, 1:2], m_n2, m_h[-2:])
        bank_free[6], bank_free[7] = m_h2[-2:]
        pe.wait(m_h, m_h2)
        h_all = lambda k: hT[:, k, :]
        h_lat = lambda k: hT[:, k, 0:T]

        def gated_linear_attention():
            z.n = keep_gla
            kk_ = z.take(2 * 2 * HB * T).rearrange("p (d n) -> p d n", d=2)
            ff_ = z.take(2 * 2 * HB * T).rearrange("p (d n) -> p d n", d=2)
            q_ = z.take(HB * T)
            qd = z.take(2 * HB * T).rearrange("p (d n) -> p d n", d=2)
            v_ = z.take(4 * 512).rearrange("p (s n) -> p s n", s=4)
            AT = z.take(HB * 4 * T).rearrange("p (h s t) -> p h s t", h=HB, s=4)
            SL = HB * T
            masks = level_mask.rearrange("p (n t) -> p n t", n=15)
            v.wait(m_params, m_mask8), a.wait(m_params)
            m_ya = None
            m_all = [m_h, m_h2]
            for q in (v, a, g):
                q.wait(m_all, m_wif, m_lb)

            prev_av = None
            for hb in range(HG // HB):
                heads = range(hb * HB, hb * HB + HB)
                for q in (v, a, g):
                    q.wait(prev_av)
                m_k = [[], []]
                m_f = [[], []]
                for dr, off in ((FWD, O_FF), (BWD, O_FB)):
                    c = column_chunk(w2, off + hb * 512)
                    pe.wait(c[1])
                    for j in range(HB):
                        b = next_bank()
                        m = project(c, j, h_all, 2 * T, b)
                        tile = 8 * dr + hb * HB + j
                        fv = ff_[:, dr, :].rearrange("p (s h t) -> p s h t", s=2, h=HB)[:, :, j, :]
                        kv = kk_[:, dr, :].rearrange("p (s h t) -> p s h t", s=2, h=HB)[:, :, j, :]
                        src = banks[b].rearrange("p (s t) -> p s t", s=2)
                        a.wait(m)
                        m1 = a.do(lambda e, fv=fv, src=src, tile=tile: e.activation(fv, src, ACT.Sigmoid, bias=C("b_in", O_FF // P + tile)))
                        m2 = a.do(lambda e, kv=kv, src=src, tile=tile: e.activation(kv, src, ACT.Sigmoid, bias=nbf[:, tile:tile + 1], scale=-1.0))
                        bank_free[b] = m2
                        lo, om = lbs[:, 0, dr, hb * HB + j:hb * HB + j + 1], lbs[:, 1, dr, hb * HB + j:hb * HB + j + 1]
                        v.wait(m1)
                        m_f[dr].append(v.do(lambda e, fv=fv, lo=lo, om=om: e.tensor_scalar(fv, fv, om, lo, ALU.mult, ALU.add)))
                        g.wait(m2)
                        m_k[dr].append(g.do(lambda e, kv=kv, om=om: e.tensor_scalar(kv, kv, om, None, ALU.mult)))
                    stream.release(c[0], m)
                c = column_chunk(w2, O_Q + hb * 512)
                pe.wait(c[1])
                for j in range(HB):
                    b = next_bank()
                    m = project(c, j, h_lat, T, b)
                    a.wait(m)
                    m_q = a.do(lambda e, j=j, b=b, hb=hb: e.activation(q_[:, j * T:(j + 1) * T], banks[b][:, 0:T], ACT.Silu, bias=C("b_in", O_Q // P + hb * HB + j)))
                    bank_free[b] = m_q
                stream.release(c[0], m)
                behind = []
                c_v, c_g = column_chunk(w2, O_HI + hb * 512), column_chunk(w2, O_HG + hb * 512)
                m_v, m_g = [], {}
                for n in range(4):
                    def values(n=n, c=c_v, hb=hb):
                        b = next_bank()
                        pe.wait(c[1])
                        m = project_tokens(c, lambda k: hT[:, k, n * P:(n + 1) * P], 512, b, brow[0:1, hb * 512:(hb + 1) * 512])
                        a.wait(m)
                        bank_free[b] = a.do(lambda e: e.activation(v_[:, n, :], banks[b], ACT.Copy))
                        m_v.append(bank_free[b])
                        if n == 3:
                            stream.release(c[0], m)

                    def output_gate(j=n, c=c_g, hb=hb):
                        b, k = next_bank(), hb * HB + j
                        pe.wait(c[1])
                        m = project(c, j, h_lat, T, b)
                        a.wait(m)
                        bank_free[b] = m_g[k] = a.do(lambda e: e.activation(yaT[:, k, :], banks[b][:, 0:T], ACT.Silu, bias=C("b_in", O_HG // P + k)))
                        if j == 3:
                            stream.release(c[0], m)
                    behind += [values, output_gate]

                pe.wait(m_q, m_k)
                pair = [[2, 3], [4, 5]]
                for t in range(NT):
                    b = pair[0][t]
                    pe.wait(bank_free[b])

                    def mm(e, t=t, b=b):
                        for h in range(HB):
                            for dr in range(2):
                                r = e.matmul(banks[b][:, h * P:(h + 1) * P], kk_[:, dr, h * T + t * P:h * T + (t + 1) * P], q_[:, h * T + t * P:h * T + (t + 1) * P], start=(dr == 0), stop=(dr == 1))
                        return r
                    m = pe.do(mm)
                    v.wait(m)
                    av = AT[:, :, t, t * P:(t + 1) * P]
                    m_ev0 = v.do(lambda e, av=av, b=b: e.tensor_copy(av, banks[b].rearrange("p (h t) -> p h t", h=HB)))
                    bank_free[b] = m_ev0
                v.wait(m_q, m_f[0])
                g.wait(m_q, m_f[1])
                eng = [v, g]
                m_qd = [eng[dr].do(lambda e, dr=dr: e.tensor_tensor(qd[:, dr, :], q_, ff_[:, dr, 0:SL], ALU.mult)) for dr in range(2)]
                m_kd = [m_k[0][-1], m_k[1][-1]]
                m_at = [m_ev0, m_ev0]
                for li, m_ in enumerate(LEVELS + [P]):
                    for dr in range(2):
                        pe.wait(m_qd[dr], m_kd[dr])
                        m_mm = None
                        if m_ < P:
                            for t in range(NT):
                                b = pair[dr][t]
                                pe.wait(bank_free[b])

                                def mm(e, t=t, b=b, dr=dr):
                                    for h in range(HB):
                                        o = h * T + t * P
                                        r = e.matmul(banks[b][:, h * P:(h + 1) * P], kk_[:, dr, o:o + P], qd[:, dr, o:o + P], start=True, stop=True)
                                    return r
                                m_mm = pe.do(mm)
                                v.wait(m_mm, m_at[t])
                                av = AT[:, :, t, t * P:(t + 1) * P]
                                mk = masks[:, 1 + 7 * dr + li:2 + 7 * dr + li, :].to_broadcast([P, HB, P])
                                m_at[t] = v.do(lambda e, av=av, mk=mk, b=b: e.copy_predicated(av, mk, banks[b].rearrange("p (h t) -> p h t", h=HB)))
                                bank_free[b] = m_at[t]
                        else:
                            kt, qt = (0, 1) if dr == FWD else (1, 0)
                            b = pair[dr][0]
                            pe.wait(bank_free[b])

                            def mm(e, kt=kt, qt=qt, b=b, dr=dr):
                                for h in range(HB):
                                    r = e.matmul(banks[b][:, h * P:(h + 1) * P], kk_[:, dr, h * T + kt * P:h * T + (kt + 1) * P], qd[:, dr, h * T + qt * P:h * T + (qt + 1) * P], start=True, stop=True)
                                return r
                            m_mm = pe.do(mm)
                            a.wait(m_mm)
                            bank_free[b] = a.do(lambda e, kt=kt, qt=qt, b=b: e.activation(AT[:, :, kt, qt * P:(qt + 1) * P], banks[b].rearrange("p (h t) -> p h t", h=HB), ACT.Copy))
                        q = eng[dr]
                        q.wait(m_mm)
                        late, early = (1, 0) if dr == FWD else (0, 1)
                        nblk = 2 * SL // (2 * m_)
                        kb = kk_[:, dr, :].rearrange("p (n o m) -> p n o m", o=2, m=m_)
                        qb = qd[:, dr, :].rearrange("p (n o m) -> p n o m", o=2, m=m_)
                        fb = ff_[:, dr, :].rearrange("p (n o m) -> p n o m", o=2, m=m_)
                        nl = SL // (2 * m_)
                        m_qd[dr] = q.do(lambda e, qb=qb, fb=fb, nl=nl, late=late, early=early, m_=m_: e.tensor_tensor(qb[:, :, late, :], qb[:, :, late, :], fb[:, 0:nl, early, 0:1].to_broadcast([P, nl, m_]), ALU.mult))
                        m_kd[dr] = q.do(lambda e, kb=kb, fb=fb, nblk=nblk, late=late, early=early, m_=m_: e.tensor_tensor(kb[:, :, early, :], kb[:, :, early, :], fb[:, :, late, 0:1].to_broadcast([P, nblk, m_]), ALU.mult))
                        q.wait(m_kd[dr])
                        if m_ < P:
                            m_t = q.do(lambda e, fb=fb: e.tensor_tensor(fb[:, :, 0, 0], fb[:, :, 0, 0], fb[:, :, 1, 0], ALU.mult))
                            q.wait(m_t)
                    behind.pop(0)()
                assert not behind
                for n in range(HB * 2):
                    h, cti = n // 2, n % 2
                    b = 2 + (n // 2) % 4
                    if cti == 0:
                        pe.wait(bank_free[b], m_qd, m_kd)

                    def mm(e, h=h, cti=cti, b=b):
                        for dr in range(2):
                            o = SL + h * T + cti * P
                            r = e.matmul(banks[b][:, cti * T:(cti + 1) * T], kk_[:, dr, o:o + P], qd[:, dr, h * T:(h + 1) * T], start=(dr == 0), stop=(dr == 1))
                        return r
                    m = pe.do(mm)
                    if cti == 1:
                        a.wait(m)
                        m_at2 = a.do(lambda e, h=h, b=b: e.activation(AT[:, h, 2:4, :].rearrange("p s t -> p (s t)"), banks[b], ACT.Copy))
                        bank_free[b] = m_at2
                pe.wait(m_at, m_at2, m_v)
                for hp in range(HB // 2):
                    b = 6 + hp
                    pe.wait(bank_free[b])

                    def mm(e, hp=hp, b=b):
                        for o in range(2):
                            h = 2 * hp + o
                            for st in range(4):
                                r = e.matmul(banks[b][:, o * T:(o + 1) * T], v_[:, st, h * P:(h + 1) * P], AT[:, h, st, :], start=(st == 0), stop=(st == 3))
                        return r
                    m = pe.do(mm)
                    prev_av = m
                    sqd = qd[:, hp, 0:512]
                    a.wait(m)
                    m = a.do(lambda e, b=b, sqd=sqd: e.activation(sqd, banks[b], ACT.Square))
                    pe.wait(m, bank_free[2 + hp])
                    m = pe.do(lambda e, hp=hp, sqd=sqd: e.matmul(banks[2 + hp], ones, sqd, start=True, stop=True))
                    m = rstd_of(banks[2 + hp], sqd, 1.0 / P, m)
                    bank_free[2 + hp] = m
                    for o in range(2):
                        h = hb * HB + 2 * hp + o
                        v.wait(m_g[h])
                        normed = sqd[:, o * T:(o + 1) * T]
                        bank_free[b] = v.step(lambda e, h=h, o=o, b=b, normed=normed: e.scalar_tensor_tensor(normed, banks[b][:, o * T:(o + 1) * T], C("hg_norm_g", h), normed, ALU.mult, ALU.mult))
                        m_ya = v.do(lambda e, h=h, normed=normed: e.tensor_tensor(yaT[:, h, :], yaT[:, h, :], normed, ALU.mult))
                prev_av = [prev_av, m_ya]
        gated_linear_attention()
        def mlstm():
            join()
            z.n = keep_gla
            qT = z.take(MLH * T).rearrange("p (h t) -> p h t", h=MLH)
            kT = z.take(MLH * 2 * T).rearrange("p (h s t) -> p h s t", h=MLH, s=2)
            shared = z.take(9 * 2 * T)
            va = shared[:, 0:4 * MLH * (MLV + 1)].rearrange("p (s h n) -> p s h n", s=4, h=MLH)
            Rb = z.take(8 * T).rearrange("p (d h t) -> p d h t", d=2, h=MLH)
            Rd = z.take(8 * T).rearrange("p (d h t) -> p d h t", d=2, h=MLH)
            cc_ = z.take(8 * 36).rearrange("p (q s n) -> p q s n", q=2, s=4)
            nm = z.take(2 * 36).rearrange("p (q n) -> p q n", q=2)
            share = z.n
            PADM = MLC // 2
            W = T + 2 * PADM
            raw = z.take(12 * W).rearrange("p (n t) -> p n t", n=12)
            names = "fr LI LF B M CS0 CS1 CO0 CO1".split()
            rw = {n: shared[:, i_ * 2 * T:(i_ + 1) * 2 * T] for i_, n in enumerate(names)}
            Rr, NMr = z.take(T), z.take(T)
            hp = z.take(KD * T).rearrange("p (k t) -> p k t", k=KD)

            def permuted(ap):
                return ap.rearrange("p (r c) -> p c r", r=GRID_R)

            for k in range(KD):
                m_hp = g.do(lambda e, k=k: e.tensor_copy(hp[:, k, :].rearrange("p (c r) -> p c r", r=GRID_R), permuted(hT[:, k, 0:T])))
            m_pad = g.do(lambda e: e.memset(raw[:, :, 0:PADM], 0.0))
            m_pad = g.do(lambda e: e.memset(raw[:, :, W - PADM:W], 0.0))
            m_z1 = g.do(lambda e: e.memset(rw["LI"], 0.0))
            m_z2 = g.do(lambda e: e.memset(rw["LF"], 0.0))
            m_z3 = g.do(lambda e: e.memset(rw["CO0"], 0.0))
            m_z3 = g.do(lambda e: e.memset(rw["CO1"], 0.0))
            m_z3 = g.do(lambda e: e.memset(Rr, 0.0))
            m_z3 = g.do(lambda e: e.memset(NMr, 0.0))

            pe.wait(bank_free[2])

            def mm(e):
                for k in range(KD):
                    r = e.matmul(banks[2], w_if[:, k, :], hT[:, k, :], start=(k == 0), stop=(k == KD - 1))
                return r
            m = pe.do(mm)
            a.wait(m)
            a.do(lambda e: e.activation(rw["fr"][:, 0:T], banks[2][:, T:2 * T], ACT.Identity, bias=C("b_if")))
            m = a.do(lambda e: e.activation(rw["fr"][:, T:2 * T].rearrange("p (c r) -> p c r", r=GRID_R), permuted(banks[2][:, 0:T]), ACT.Identity, bias=C("b_if")))
            bank_free[2] = m
            v.wait(m, m_z3)

            def turned(dst, src, o, o2):
                v.do(lambda e: e.tensor_copy(dst[0:4, :], src[o:o + 4, :]))
                v.do(lambda e: e.tensor_copy(dst[32:36, 0:T], src[o2:o2 + 4, T - 1::-1]))
                return v.do(lambda e: e.tensor_copy(dst[32:36, T:2 * T], src[o2:o2 + 4, 2 * T - 1:T - 1:-1]))
            turned(rw["LI"], rw["fr"], 0, 32)
            v.wait(turned(rw["LF"], rw["fr"], 64, 96))
            H = slice(0, 36)
            LI, LF, B_, M_ = (rw[n][H, :] for n in ("LI", "LF", "B", "M"))
            m_lf = Mark(v.counter, None, v.counter.total)
            a.wait(m_lf)
            a.step(lambda e: e.activation(B_, LF, ACT.Abs))
            m = a.step(lambda e: e.activation(B_, B_, ACT.Exp, scale=-1.0))
            m = a.do(lambda e: e.activation(B_, B_, ACT.Ln, bias=1.0))
            v.wait(m)
            v.step(lambda e: e.scalar_tensor_tensor(LF, LF, 0.0, B_, ALU.min, ALU.subtract))
            v.do(lambda e: e.tensor_tensor_scan(M_, LF, LI, 0.0, ALU.add, ALU.max))
            for j in range(4):
                v.do(lambda e, j=j: e.tensor_tensor_scan(B_[:, j * P:(j + 1) * P], ones[0:36, :], LF[:, j * P:(j + 1) * P], 0.0, ALU.mult, ALU.add))
            v.wait(Mark(v.counter, None, v.counter.total))
            CS = [rw["CS0"][H, :], rw["CS1"][H, :]]
            for qs in (0, 1):
                v.step(lambda e, qs=qs: e.tensor_tensor(CS[qs], LI, B_, ALU.subtract))
            v.step(lambda e: e.tensor_tensor(LI[:, 0:T], B_[:, T:2 * T], M_[:, T:2 * T], ALU.subtract))
            v.step(lambda e: e.tensor_copy(LI[:, T:2 * T], M_[:, T:2 * T]))
            for qs in (0, 1):
                for j in range(2 + qs):
                    for kt in range(j + 1):
                        v.step(lambda e, qs=qs, j=j, kt=kt: e.tensor_scalar(CS[qs][:, kt * P:(kt + 1) * P], CS[qs][:, kt * P:(kt + 1) * P], B_[:, j * P + P - 1:(j + 1) * P], None, ALU.add))
            CO = [rw["CO0"], rw["CO1"]]
            for qo in (0, 1):
                v.do(lambda e, qo=qo: e.tensor_copy(CO[qo][0:4, :], CS[qo][0:4, :]))
                v.do(lambda e, qo=qo: e.tensor_copy(CO[qo][32:36, 0:T], CS[1 - qo][32:36, T - 1::-1]))
                v.do(lambda e, qo=qo: e.tensor_copy(CO[qo][32:36, T:2 * T], CS[1 - qo][32:36, 2 * T - 1:T - 1:-1]))
            v.do(lambda e: e.tensor_copy(Rr[0:4, :], LI[0:4, 0:T]))
            v.do(lambda e: e.tensor_copy(Rr[32:36, :], LI[32:36, T - 1::-1]))
            v.do(lambda e: e.tensor_copy(NMr[0:4, :], LI[0:4, T:2 * T]))
            m_rows = v.do(lambda e: e.tensor_copy(NMr[32:36, :], LI[32:36, 2 * T - 1:T - 1:-1]))
            pe.wait(m_rows, bank_free[2], bank_free[3], bank_free[4], bank_free[5], bank_free[6])

            def mm(e):
                for qo in range(2):
                    for st in range(4):
                        o = (qo * 4 + st) * 36
                        r = e.transpose(banks[2][:, o:o + 36], CO[qo][0:36, st * P:(st + 1) * P], ident[0:36, 0:36])
                for t in range(2):
                    o = (8 + t) * 36
                    r = e.transpose(banks[2][:, o:o + 36], NMr[0:36, t * P:(t + 1) * P], ident[0:36, 0:36])
                return r
            m = pe.do(mm)
            v.wait(m)
            m_cc = v.do(lambda e: e.tensor_copy(cc_.rearrange("p q s n -> p (q s n)"), banks[2][:, 0:288]))
            a.wait(m, m_cc)
            m_nm = a.do(lambda e: e.activation(nm.rearrange("p q n -> p (q n)"), banks[2][:, 288:360], ACT.Exp, scale=-1.0))
            bank_free[2] = m_nm
            for n in range(4):
                b = 3 + n

                def mm(e, n=n, b=b):
                    for o in range(2):
                        r = e.matmul(banks[b][:, o * T:(o + 1) * T], pick_row[0:36, (2 * n + o) * P:(2 * n + o + 1) * P], Rr[0:36, :], start=True, stop=True)
                    return r
                m = pe.do(mm)
                a.wait(m)
                m = a.do(lambda e, n=n, b=b: e.activation(Rb.rearrange("p d h t -> p (d h t)")[:, n * 512:(n + 1) * 512], banks[b], ACT.Copy))
                bank_free[b] = m
            m_Rb = m
            v.wait(m)
            for dr in range(2):
                for t in range(NT):
                    mk = (Call("mask_f") if dr == FWD else Call("mask_b")).unsqueeze(1).to_broadcast([P, MLH, P])
                    m_Rd = v.do(lambda e, dr=dr, t=t, mk=mk: e.tensor_tensor(Rd[:, dr, :, t * P:(t + 1) * P], Rb[:, dr, :, t * P:(t + 1) * P], mk, ALU.add))

            a.wait(m_pad), v.wait(m_pad)
            m_c = []
            for what, off in ((0, O_MQ), (1, O_MK)):
                c = column_chunk(w2, off)
                pe.wait(c[1])
                for h in range(MLH):
                    b = next_bank()
                    m = project(c, h, h_all if what else h_lat, 2 * T if what else T, b)
                    row = 4 + 2 * h + 1 if what else h
                    bias = C("b_in", off // P + h)
                    a.wait(m)
                    m = a.do(lambda e, row=row, b=b, bias=bias: e.activation(raw[:, row, PADM:PADM + T].rearrange("p (c r) -> p c r", r=GRID_R), permuted(banks[b][:, 0:T]), ACT.Identity, bias=bias))
                    if what:
                        m = a.do(lambda e, row=row, b=b, bias=bias: e.activation(raw[:, row - 1, PADM:PADM + T], banks[b][:, T:2 * T], ACT.Identity, bias=bias))
                    bank_free[b] = m
                    v.wait(m)
                    src = raw[:, 4 + 2 * h:6 + 2 * h, :] if what else raw[:, h:h + 1, :]
                    dst = kT[:, h] if what else qT[:, h:h + 1, :]
                    cw = lambda w_, h=h, what=what: C("ml_conv_w", (4 * what + h) * MLC + w_)
                    v.step(lambda e, dst=dst, src=src, cw=cw: e.tensor_scalar(dst, src[:, :, 0:T], cw(0), None, ALU.mult))
                    for w_ in range(1, MLC):
                        m = v.step(lambda e, dst=dst, src=src, cw=cw, w_=w_: e.scalar_tensor_tensor(dst, src[:, :, w_:w_ + T], cw(w_), dst, ALU.mult, ALU.add))
                    a.wait(m)
                    m_c.append(a.do(lambda e, dst=dst, h=h, what=what: e.activation(dst, dst, ACT.Silu, bias=C("ml_conv_b", 4 * what + h))))
                stream.release(c[0], Mark(pe.counter, None, pe.counter.total))
                if not what:
                    g.wait(m_c)
                    m_q = g.do(lambda e: e.tensor_scalar(qT, qT, float(P) ** -0.5, None, ALU.mult))
            g.wait(m_cc, m_nm, m_Rd)
            m_one = g.do(lambda e: e.memset(va[:, :, :, MLV:MLV + 1], 1.0))
            a.wait(m_one)
            pe.wait(m_hp)
            m_vv = []
            for nb in range(2):
                c = column_chunk(w2, O_MV + nb * 512)
                pe.wait(c[1])
                for st in range(4):
                    b = next_bank()
                    if st < 2:
                        lh = lambda k, st=st: hT[:, k, T + st * P:T + (st + 1) * P]
                    else:
                        lh = lambda k, st=st: hp[:, k, (st - 2) * P:(st - 1) * P]
                    m = project_tokens(c, lh, 512, b, brow[0:1, 1024 + nb * 512:1024 + (nb + 1) * 512])
                    a.wait(m)
                    bank_free[b] = a.do(lambda e, st=st, b=b, nb=nb: e.activation(va[:, st, 2 * nb:2 * nb + 2, 0:MLV], banks[b].rearrange("p (h n) -> p h n", h=2), ACT.Copy))
                stream.release(c[0], m)
            m_va = bank_free[b]

            join()
            z.n = share
            ex = [z.take(4 * P) for _ in range(4)]
            hs = z.take(NT * D).rearrange("p (q h n) -> p q h n", q=NT, h=MLH)
            den = z.take(2 * 2 * NT * MLH).rearrange("p (n o) -> p n o", o=2)
            ybT = z.take(KD * T).rearrange("p (k t) -> p k t", k=KD)
            pe.wait(m_q, m_c, m_va, m_one)
            a.wait(m_cc, m_Rd)
            ex_read = [None] * 4
            n_u = 0
            for h in range(MLH):
                for qo in range(NT):
                    sb_ = 2 + n_u % 2
                    pe.wait(bank_free[sb_])

                    def mm(e, h=h, qo=qo, sb_=sb_):
                        for st in range(4):
                            r = e.matmul(banks[sb_][:, st * P:(st + 1) * P], kT[:, h, st // 2, (st % 2) * P:(st % 2 + 1) * P], qT[:, h, qo * P:(qo + 1) * P], start=True, stop=True)
                        return r
                    m_s = pe.do(mm)
                    for dr in range(2):
                        i4 = (2 * n_u + dr) % 4
                        eb = ex[i4]
                        lat = range(2, 3 + qo) if dr == FWD else range(2 + qo, 4)
                        row = 32 * dr + h
                        a.wait(ex_read[i4])
                        for st in [0, 1, *lat]:
                            src = (Rd if st == 2 + qo else Rb)[:, dr, h, qo * P:(qo + 1) * P]
                            m = a.do(lambda e, eb=eb, st=st, src=src, qo=qo, row=row: e.activation(eb[:, st * P:(st + 1) * P], src, ACT.Exp, bias=cc_[:, qo, st, row:row + 1]))
                        v.wait(m, m_s)
                        for lo, hi in ([(0, lat[-1] + 1)] if lat[0] == 2 else [(0, 2), (3, 4)]):
                            m = v.do(lambda e, eb=eb, lo=lo, hi=hi, sb_=sb_: e.tensor_tensor(eb[:, lo * P:hi * P], eb[:, lo * P:hi * P], banks[sb_][:, lo * P:hi * P], ALU.mult))
                        bank_free[sb_] = m
                        ob = 4 + i4
                        pe.wait(m, bank_free[ob])

                        def mm(e, eb=eb, lat=lat, h=h, ob=ob):
                            for st in [0, 1, *lat]:
                                r = e.matmul(banks[ob][:, 0:MLV + 1], eb[:, st * P:(st + 1) * P], va[:, st, h, :], start=(st == 0), stop=(st == lat[-1]))
                            return r
                        m = pe.do(mm)
                        ex_read[i4] = m
                        dn = den[:, 2 * n_u + dr, :]
                        a.wait(m)
                        m_abs = a.do(lambda e, dn=dn, ob=ob: e.activation(dn[:, 0:1], banks[ob][:, MLV:MLV + 1], ACT.Abs))
                        v.wait(m_abs, m_nm)
                        v.step(lambda e, dn=dn, qo=qo, row=row: e.tensor_scalar(dn[:, 0:1], dn[:, 0:1], nm[:, qo, row:row + 1], None, ALU.max))
                        v.step(lambda e, dn=dn: e.reciprocal(dn[:, 1:2], dn[:, 0:1]))
                        if dr == FWD:
                            m_hs = v.do(lambda e, dn=dn, ob=ob, qo=qo, h=h: e.tensor_scalar(hs[:, qo, h, :], banks[ob][:, 0:MLV], dn[:, 1:2], None, ALU.mult))
                        else:
                            v.wait(m_hs)
                            m_hs = v.do(lambda e, dn=dn, ob=ob, qo=qo, h=h: e.scalar_tensor_tensor(hs[:, qo, h, :], banks[ob][:, 0:MLV], dn[:, 1:2], hs[:, qo, h, :], ALU.mult, ALU.add))
                        bank_free[ob] = m_hs
                    n_u += 1
            hst = small[:, 424:432]
            a.wait(m_hs)
            for n in range(NT * MLH):
                junk = ex[n % 4][:, (n // 4) * T:(n // 4 + 1) * T]
                m = a.do(lambda e, n=n, junk=junk: e.activation(junk, hs[:, n // MLH, n % MLH, :], ACT.Square, accum_out=hst[:, n:n + 1]))
            rstd_of(hst, hst, 1.0 / MLV, m)
            for n in range(NT * MLH):
                m = v.do(lambda e, n=n: e.tensor_scalar(hs[:, n // MLH, n % MLH, :], hs[:, n // MLH, n % MLH, :], hst[:, n:n + 1], None, ALU.mult))
            pe.wait(m)
            hsf = hs.rearrange("p q h n -> p q (h n)")
            m_yb = [None, None]
            gts = [ex[2][:, 0:T], ex[3][:, 0:T]]
            for nb in range(2):
                c = column_chunk(w2, O_MG + nb * 512)
                pe.wait(c[1])
                for j in range(4):
                    k = nb * 4 + j
                    b = next_bank()
                    m = project(c, j, h_lat, T, b)
                    a.wait(m, m_yb[k % 2])
                    bank_free[b] = a.do(lambda e, k=k, b=b: e.activation(gts[k % 2], banks[b][:, 0:T], ACT.Sigmoid, bias=C("b_in", 56 + k)))
                    m_g = bank_free[b]
                    tb = 2 + k % 2
                    pe.wait(bank_free[tb])
                    for t in range(NT):
                        m2 = pe.do(lambda e, t=t, k=k, tb=tb: e.transpose(banks[tb][:, t * P:(t + 1) * P], hsf[:, t, k * P:(k + 1) * P], ident))
                    v.wait(m_g, m2)
                    v.step(lambda e, k=k, tb=tb: e.tensor_scalar(permuted(ybT[:, k, :]), banks[tb][:, 0:T].rearrange("p (c r) -> p c r", r=GRID_R), C("ml_norm_g", k), None, ALU.mult))
                    bank_free[tb] = Mark(v.counter, None, v.counter.total)
                    m_yb[k % 2] = v.do(lambda e, k=k: e.tensor_tensor(ybT[:, k, :], ybT[:, k, :], gts[k % 2], ALU.mult))
                stream.release(c[0], m)

            return ybT, share

        ybT, share = mlstm()

        join()
        z.n = keep_gla
        yT = z.take(KD * T).rearrange("p (k t) -> p k t", k=KD)
        sg_ = [z.take(T) for _ in range(2)]
        tg_ = [z.take(T) for _ in range(2)]
        assert z.n <= share
        m_y = {}
        n_s = [None, None]
        t_s = [None, None]
        for part, (og, wname, src_) in enumerate(((O_GA, "w_branch_a_2", yaT), (O_GB, "w_branch_b_2", ybT))):
            for nb in range(2):
                c1 = column_chunk(w2, og + nb * 512)
                c2 = column_chunk(d[wname][0], nb * 512)
                pe.wait(c1[1], c2[1])
                for j in range(4):
                    k = nb * 4 + j
                    b = next_bank()
                    m1 = project(c1, j, h_lat, T, b)
                    a.wait(m1, n_s[k % 2])
                    m = a.do(lambda e, k=k, b=b, og=og: e.activation(sg_[k % 2], banks[b][:, 0:T], ACT.Sigmoid, bias=C("b_in", 56 + (og - O_MG) // P + k)))
                    bank_free[b] = m
                    b2 = 2 + b
                    m2 = project(c2, j, lambda kk, src_=src_: src_[:, kk, :], T, b2)
                    v.wait(m, m2)
                    if part == 0:
                        m_y[k] = v.do(lambda e, k=k, b2=b2: e.tensor_tensor(yT[:, k, :], banks[b2][:, 0:T], sg_[k % 2], ALU.mult))
                        n_s[k % 2] = bank_free[b2] = m_y[k]
                    else:
                        v.wait(t_s[k % 2])
                        m3 = v.step(lambda e, k=k, b2=b2: e.tensor_tensor(tg_[k % 2], banks[b2][:, 0:T], sg_[k % 2], ALU.mult))
                        n_s[k % 2] = bank_free[b2] = m3
                        v.wait(m_y[k])
                        m_y[k] = v.do(lambda e, k=k: e.tensor_tensor(yT[:, k, :], yT[:, k, :], tg_[k % 2], ALU.add))
                        t_s[k % 2] = m_y[k]
                stream.release(c1[0], m1)
                stream.release(c2[0], m2)

        def row_of(col0, dst, pair_):
            pe.wait([bank_free[b] for b in pair_])

            def mm(e):
                for k in range(KD):
                    r = e.matmul(banks[pair_[k // 4]][:, (k % 4) * P:(k % 4 + 1) * P], mcol[:, col0 + k, 0:1].to_broadcast([P, P]), ident, start=True, stop=True)
                return r
            m = pe.do(mm)
            a.wait(m)
            for n, b in enumerate(pair_):
                bank_free[b] = a.do(lambda e, n=n, b=b: e.activation(dst[:, n * 512:(n + 1) * 512], banks[b], ACT.Copy))
            return bank_free[pair_[1]]
        g1 = z.take(D)
        mt = [z.take(512) for _ in range(2)]
        m_g1 = row_of(16, g1, (4, 5))

        pe.wait([m_y[k] for k in range(KD)])
        v.wait(m_g1)
        m_t = [None, None]
        n_ = 0
        for nb in range(2):
            c = column_chunk(d["w_out_2"][0], nb * 512)
            pe.wait(c[1])
            for t in range(NT):
                b = 2 * nb + t
                m = project_tokens(c, lambda k, t=t: yT[:, k, t * P:(t + 1) * P], 512, b)
                v.wait(m, m_t[n_ % 2])
                v.step(lambda e, n_=n_, b=b, nb=nb: e.tensor_tensor(mt[n_ % 2], banks[b], g1[:, nb * 512:(nb + 1) * 512], ALU.mult))
                xs = x[:, t * D + nb * 512:t * D + (nb + 1) * 512]
                m_t[n_ % 2] = v.do(lambda e, n_=n_, xs=xs: e.tensor_tensor(xs, xs, mt[n_ % 2], ALU.add))
                bank_free[b] = m_t[n_ % 2]
                n_ += 1
            stream.release(c[0], m)
        join()
        acc = zone[:, zone.shape[1] - NT * D:]
        m = g.do(lambda e: e.memset(acc, 0.0))
        v.wait(m)
        moe("moe2", E2, F2, w_route[1], R("r2_b"), d["w_gate_2"][0], d["w_up_2"][0], d["w_down_2"][0],
            lambda k: scl2[:, k:k + 1], lambda k: mcol[:, 24 + k, 0:1], acc, [])
        join()
        for i_ in range(8):
            bank_free[i_] = None
        z = Zone()
        g2 = z.take(D)
        on = z.take(NT * D)
        m = row_of(40, g2, (0, 1))
        v.wait(m)
        for t in range(NT):
            ts_ = slice(t * D, (t + 1) * D)
            v.step(lambda e, ts_=ts_: e.tensor_tensor(acc[:, ts_], acc[:, ts_], g2, ALU.mult))
            m = v.step(lambda e, ts_=ts_: e.tensor_tensor(x[:, ts_], x[:, ts_], acc[:, ts_], ALU.add))
        m_n = norm_tokens(x, on, small[:, 0:8], m)
        for t in range(NT):
            v.wait(m_n[t])
            m = v.do(lambda e, t=t: e.tensor_tensor(on[:, t * D:(t + 1) * D], on[:, t * D:(t + 1) * D], R("final_g"), ALU.mult))
            s.wait(m)
            m = s.do(lambda e, t=t: e.dma_start(y_out[0, t * P:(t + 1) * P, :], on[:, t * D:(t + 1) * D]), out_done, 16)
        s.wait(m)
        emit(prog, nc, ctx)


def emit(prog, nc, ctx):
    block = ctx.enter_context(nc.Block())
    block.sync(lambda e: prog.s.run(e))
    block.tensor(lambda e: prog.pe.run(e))
    block.vector(lambda e: prog.v.run(e))
    block.scalar(lambda e: prog.a.run(e))
    block.gpsimd(lambda e: prog.g.run(e))


def pack_cols(i):
    def tiles(vec):
        return np.reshape(vec, (-1, P)).T

    f = np.float32
    p = np.arange(P)
    t = np.arange(T)
    dist = (p[:, None] + P) - t[None, :]
    slopes = [(2.0 ** (-8.0 / HA)) ** (h + 1) for h in range(HA)]
    count = np.stack([np.minimum(t + 1, w) for w in WINDOWS])
    inv = np.concatenate([np.repeat(1.0 / count[2 * j:2 * j + 2], 64, axis=0) for j in range(2)], axis=1)
    b_in = i["b_in_2"][0]
    b_if = np.zeros((P, 1), f)
    for n in range(4):
        b_if[32 * n:32 * n + 4, 0] = b_in[O_IF + 4 * n:O_IF + 4 * n + 4]
    parts = {
        "ident": np.eye(P), "ones": np.ones((P, P)), "ones64": np.kron(np.eye(2), np.ones((64, 64))),
        "before": np.triu(np.ones((P, P)), 1), "iota": np.tile(p, (P, 1)), "iota8": np.tile(np.arange(8), (P, 1)),
        "alibi": np.concatenate([np.where(dist >= 0, -sl * dist, NEG) for sl in slopes], axis=1),
        "inv_count": inv, "mask_f": np.where(p[:, None] <= p[None, :], 0.0, NEG),
        "mask_b": np.where(p[:, None] >= p[None, :], 0.0, NEG),
        "attn_norm_g": tiles(i["attn_norm_g"]), "ffn_norm_g": tiles(i["ffn_norm_g"]),
        "norm1_g": tiles(i["norm1_g_2"]), "norm2_g": tiles(i["norm2_g_2"]),
        "conv_w": np.concatenate([i["conv_w"][0][:, j * P:(j + 1) * P].T for j in range(2)], axis=1),
        "conv_b": tiles(i["conv_b"]), "conv_ln_g": tiles(i["conv_ln_g"]), "conv_ln_b": tiles(i["conv_ln_b"]),
        "conv_pw_b": tiles(i["conv_pw_b"]), "pool_scale": tiles(i["pool_scale"]),
        "q_norm_g": np.tile(i["q_norm_g"][0], 2)[:, None], "k_norm_g": np.tile(i["k_norm_g"][0], 2)[:, None],
        "attn_sub_norm_g": tiles(i["attn_sub_norm_g"]),
        "lb": np.reshape(i["hg_lb_logits_2"], (32, P)).T,
        "hg_norm_g": tiles(i["hg_norm_g_2"]), "ml_norm_g": tiles(i["ml_norm_g_2"]),
        "ml_conv_w": np.concatenate([i["ml_conv_w_2"][0][:, j * P:(j + 1) * P].T for j in range(8)], axis=1),
        "ml_conv_b": tiles(i["ml_conv_b_2"]),
        "b_in": np.concatenate([tiles(b_in[0:O_IF]), tiles(b_in[O_MG:])], axis=1), "b_if": b_if,
        "b_ada": tiles(i["b_ada_2"]), "c": tiles(i["c_2"]), "c_ctx": tiles(i["c_ctx_2"]),
    }
    for name, (_, w) in COLS.at.items():
        assert parts[name].shape == (P, w), (name, parts[name].shape)
    return np.concatenate([np.asarray(parts[name], f) for name in COLS.at], axis=1)


def pack_rows(i):
    parts = [i["router_g_b"][0], i["router_e_b"][0], i["b_group_2"][0], i["b_router_2"][0],
             i["lambda_q1"][0], i["lambda_k1"][0], i["lambda_q2"][0], i["lambda_k2"][0], i["final_norm_g_2"]]
    return np.concatenate(parts)[None, :]


def level_masks():
    p = np.arange(P)
    out = [np.eye(P)]
    for m in LEVELS:
        same = (p[:, None] // (2 * m)) == (p[None, :] // (2 * m))
        out.append(same & ((p[:, None] // m) % 2 == 0) & ((p[None, :] // m) % 2 == 1))
    out += [m.T for m in out[1:]]
    return np.concatenate([m.astype(np.float32) for m in out], axis=1)


def row_picks():
    out = np.zeros((36, 8, P), np.float32)
    for n in range(8):
        out[32 * (n // 4) + n % 4, n] = 1.0
    return out.reshape(36, 8 * P)


WEIGHTS = ["x", "w_in", "conv_pw_w", "pool_w", "w_out", "router_g_w", "router_e_w", "w_gate", "w_up", "w_down",
           "ctx_2", "w_ada_2", "w_in_2", "b_in_2", "w_branch_a_2", "w_branch_b_2", "w_out_2", "w_group_2", "w_router_2",
           "w_gate_2", "w_up_2", "w_down_2"]


def program(nc, arrays):
    d = {n: nc.dram_tensor(n + "_dram", a.shape, mybir.dt.from_np(a.dtype), kind="ExternalInput").ap() for n, a in arrays.items()}
    out = nc.dram_tensor("out_dram", (1, T, D), F32, kind="ExternalOutput").ap()
    with nc.allow_non_contiguous_dma(reason="short rows of small parameters"):
        build(nc, d, out)


def arrays_of(inputs):
    i = {n: np.asarray(a) for n, a in inputs.items()}
    arrays = {n: np.ascontiguousarray(i[n]) for n in WEIGHTS}
    arrays |= {"cols": pack_cols(i), "rows": pack_rows(i), "masks": level_masks(), "pick": row_picks()}
    return arrays


def kernel(**inputs):
    import concourse.bacc as bacc
    from concourse.bass_utils import run_bass_kernel_spmd

    nc = bacc.Bacc("TRN2", target_bir_lowering=False, num_devices=1)
    arrays = arrays_of(inputs)
    program(nc, arrays)
    r = run_bass_kernel_spmd(nc, [{n + "_dram": a for n, a in arrays.items()}], core_ids=[0])
    return r.results[0]["out_dram"]
```
